# Optimizing a Trainium2 kernel written in Bass

```python
import jax, jax.numpy as jnp
from jax import lax
import numpy as np

D_MODEL = 1024
BATCH = 1
SEQ = 2048
DEPTH = 1
DEC_BATCH = 1
DEC_SEQ = 1024
PAST_LEN = 128

MIX_WIDTH = D_MODEL
A_HEADS = 4
A_HEAD_DIM = MIX_WIDTH // 8
A_WIDTH = A_HEADS * A_HEAD_DIM
B_GROUPS = 4
B_GROUP_DIM = MIX_WIDTH // 8
B_WIDTH = B_GROUPS * B_GROUP_DIM
POOL_WINDOWS = (2, 4, 8, 16)
D_FF = ((8 * D_MODEL // 3 + 255) // 256) * 256
EPS = 1e-6

kernel_name = 'hybrid_fourier_pool_encoder'

def rmsnorm(x, g):
    xf = x.astype(jnp.float32)
    r = lax.rsqrt(jnp.mean(xf * xf, axis=-1, keepdims=True) + EPS)
    return (xf * r * g.astype(jnp.float32)).astype(x.dtype)

def fourier_mix(za, w_a):
    f = jnp.fft.fftn(za.astype(jnp.float32), axes=(1, 3), norm='ortho').real
    f = f.astype(za.dtype)
    return jnp.einsum('bshc,hcd->bshd', f, w_a)

def centred_mean(u, k):
    s = u.shape[1]
    cs = jnp.concatenate([jnp.zeros_like(u[:, :1]), jnp.cumsum(u, axis=1)], axis=1)
    t = jnp.arange(s)
    lo = jnp.clip(t - k // 2, 0, s)
    hi = jnp.clip(t + k // 2, 0, s)
    sums = jnp.take(cs, hi, axis=1) - jnp.take(cs, lo, axis=1)
    cnt = (hi - lo).astype(jnp.float32)
    return sums / cnt[None, :, None]

def pool_mix(zb, w_b, scale_b):
    zf = zb.astype(jnp.float32)
    pooled = jnp.stack([centred_mean(zf[:, :, g], POOL_WINDOWS[g]) for g in range(B_GROUPS)], axis=2)
    d = (pooled - zf).astype(zb.dtype)
    y = jnp.einsum('bsgc,gcd->bsgd', d, w_b)
    return y * scale_b.reshape(B_GROUPS, B_GROUP_DIM)

def encoder_layer(x, norm1_g, w_in, w_fourier, w_pool, pool_scale, w_out, norm2_g, w_gate, w_up, w_down):
    b, s, _ = x.shape
    h = rmsnorm(x, norm1_g)
    z = h @ w_in
    za = z[..., :A_WIDTH].reshape(b, s, A_HEADS, A_HEAD_DIM)
    zb = z[..., A_WIDTH:].reshape(b, s, B_GROUPS, B_GROUP_DIM)
    ya = fourier_mix(za, w_fourier).reshape(b, s, A_WIDTH)
    yb = pool_mix(zb, w_pool, pool_scale).reshape(b, s, B_WIDTH)
    x = x + jnp.concatenate([ya, yb], axis=-1) @ w_out
    h = rmsnorm(x, norm2_g)
    x = x + (jax.nn.silu(h @ w_gate) * (h @ w_up)) @ w_down
    return x

def trunk(x, norm1_g, w_in, w_fourier, w_pool, pool_scale, w_out, norm2_g, w_gate, w_up, w_down, normf_g):
    for l in range(DEPTH):
        x = encoder_layer(x, norm1_g[l], w_in[l], w_fourier[l], w_pool[l], pool_scale[l], w_out[l],
                          norm2_g[l], w_gate[l], w_up[l], w_down[l])
    return rmsnorm(x, normf_g)

def setup_inputs(seed: int = 0) -> dict:
    key = jax.random.key(seed)
    ks = jax.random.split(key, 16)
    f32 = jnp.float32
    def nrm(k, shape, fan_in):
        return jax.random.normal(k, shape, f32) * (fan_in ** -0.5)
    return {
        'x_prompt': jax.random.normal(ks[0], (BATCH, SEQ, D_MODEL), f32),
        'x_sample': jax.random.normal(ks[1], (DEC_BATCH, DEC_SEQ, D_MODEL), f32),
        'norm1_g': 1.0 + 0.02 * jax.random.normal(ks[2], (DEPTH, D_MODEL), f32),
        'w_in': nrm(ks[3], (DEPTH, D_MODEL, MIX_WIDTH), D_MODEL),
        'w_fourier': nrm(ks[4], (DEPTH, A_HEADS, A_HEAD_DIM, A_HEAD_DIM), A_HEAD_DIM),
        'w_pool': nrm(ks[5], (DEPTH, B_GROUPS, B_GROUP_DIM, B_GROUP_DIM), B_GROUP_DIM),
        'pool_scale': 1.0 + 0.02 * jax.random.normal(ks[6], (DEPTH, B_WIDTH), f32),
        'w_out': nrm(ks[7], (DEPTH, MIX_WIDTH, D_MODEL), MIX_WIDTH),
        'norm2_g': 1.0 + 0.02 * jax.random.normal(ks[8], (DEPTH, D_MODEL), f32),
        'w_gate': nrm(ks[9], (DEPTH, D_MODEL, D_FF), D_MODEL),
        'w_up': nrm(ks[10], (DEPTH, D_MODEL, D_FF), D_MODEL),
        'w_down': nrm(ks[11], (DEPTH, D_FF, D_MODEL), D_FF),
        'normf_g': 1.0 + 0.02 * jax.random.normal(ks[12], (D_MODEL,), f32),
    }

def reference(x_prompt, x_sample, norm1_g, w_in, w_fourier, w_pool, pool_scale, w_out, norm2_g, w_gate, w_up, w_down, normf_g):
    y_prompt = trunk(x_prompt, norm1_g, w_in, w_fourier, w_pool, pool_scale, w_out, norm2_g, w_gate, w_up, w_down, normf_g)
    y_sample = trunk(x_sample, norm1_g, w_in, w_fourier, w_pool, pool_scale, w_out, norm2_g, w_gate, w_up, w_down, normf_g)
    return (y_prompt, y_sample)


_drawn_inputs = setup_inputs


def setup_inputs(seed=0):
    import zlib

    import numpy as np

    out = dict(_drawn_inputs(seed))
    spreads = {}
    factors = {'norm1_g': 4.09, 'pool_scale': 5.19, 'norm2_g': 13.121, 'normf_g': 8.335}
    for name, (base, spread) in spreads.items():
        noise = np.random.default_rng([zlib.crc32(name.encode()), seed]).standard_normal(out[name].shape)
        drawn = base * np.exp(spread * noise) if base else spread * noise
        out[name] = __import__('jax').numpy.asarray(drawn.astype(out[name].dtype))
    for name, factor in factors.items():
        out[name] = (out[name] * factor).astype(out[name].dtype)
    return out
```

```python
from contextlib import ExitStack

import numpy as np

import concourse.bass as bass
from concourse import mybir

F32 = mybir.dt.float32
F32R = mybir.dt.float32r
ALU = mybir.AluOpType
ACT = mybir.ActivationFunctionType

P = 128
D = 1024
KT = D // P
SEQS = (2048, 1024)
TOKENS = sum(SEQS)
HALF = 512
EPS = 1e-6
HEADS = 4
WINDOWS = (2, 4, 8, 16)
PAD = max(WINDOWS) // 2
BASE = 256
D_FF = 2816
FT = D_FF // P
DMA = 16


def levels(S):
    out = []
    while S > BASE:
        out.append(S)
        S //= 2
    return out


def table_places():
    at, places = 0, {}
    for M in levels(max(SEQS)):
        for part in ("cos", "sin"):
            places[M, part] = at
            at += (M // 4 // P) * (M // 4)
    for part in ("cos", "sin"):
        places[BASE, part] = at
        at += (BASE // P) * BASE
    return places, at


def fourier_tables():
    places, width = table_places()
    table = np.zeros((P, width))

    def put(key, rows_by_cols):
        rows, cols = rows_by_cols.shape
        for t in range(rows // P):
            table[:, places[key] + t * cols:places[key] + (t + 1) * cols] = rows_by_cols[t * P:(t + 1) * P]

    for M in levels(max(SEQS)):
        odd = 2 * np.arange(M // 4) + 1
        put((M, "cos"), np.cos(2 * np.pi / M * (np.outer(np.arange(M // 4), odd) % M)))
        sin = np.sin(2 * np.pi / M * (np.outer(np.arange(M // 4) + 1, odd) % M))
        sin[-1] *= 0.5
        put((M, "sin"), sin)
    angle = 2 * np.pi / BASE * (np.outer(np.arange(BASE), np.arange(BASE)) % BASE)
    put((BASE, "cos"), np.cos(angle))
    put((BASE, "sin"), -np.sin(angle))
    angle = 2 * np.pi / P * (np.outer(np.arange(P), np.arange(P)) % P)
    channel = np.concatenate([np.cos(angle), np.sin(angle)], axis=1) / np.sqrt(P)
    return table.astype(np.float32), channel.astype(np.float32)


def edge_counts():
    out = []
    for k in WINDOWS:
        out += [1.0 / (t + k // 2) for t in range(k // 2)]
        out += [1.0 / (k - t) for t in range(k // 2)]
    return np.tile(np.array(out, np.float32), (P, 1))


def three_products(pe, out, w_hi, w_lo, m_hi, m_lo, first, last):
    pe.matmul(out, w_hi, m_hi, start=first, stop=False)
    pe.matmul(out, w_hi, m_lo, start=False, stop=False)
    return pe.matmul(out, w_lo, m_hi, start=False, stop=last)


def refined_rstd(dve, chain, done, std, var, tmp, rstd):
    dve.reciprocal(tmp, std).then_inc(chain, 1)
    dve.wait_ge(chain, done + 1)
    dve.scalar_tensor_tensor(out=rstd, in0=tmp, scalar=-0.5, in1=tmp, op0=ALU.mult, op1=ALU.mult).then_inc(chain, 1)
    dve.wait_ge(chain, done + 2)
    dve.tensor_tensor(rstd, rstd, var, ALU.mult).then_inc(chain, 1)
    dve.wait_ge(chain, done + 3)
    dve.scalar_tensor_tensor(out=rstd, in0=rstd, scalar=1.5, in1=tmp, op0=ALU.add, op1=ALU.mult).then_inc(chain, 1)
    dve.wait_ge(chain, done + 4)


def project_in(nc, x, w_in, g1, ident, z_scr):
    NJ = TOKENS // HALF
    with ExitStack() as ctx:
        def sb(name, shape, dt=F32):
            return ctx.enter_context(nc.sbuf_tensor(name, shape, dt))

        def sem(name):
            return ctx.enter_context(nc.semaphore(name))

        w_hi = sb("win_hi", [P, KT, D], F32R)
        w_lo = sb("win_lo", [P, KT, D], F32R)
        w_raw = sb("win_raw", [P, 2, D])
        xin = sb("xin", [P, 2, 4, D])
        h_hi = sb("h_hi", [P, 2, KT, HALF], F32R)
        h_lo = sb("h_lo", [P, 2, KT, HALF], F32R)
        z_out = sb("z_out", [P, 4, HALF])
        junk = sb("junk1", [P, D])
        eye = sb("eye1", [P, P])
        gain = sb("gain1", [P, KT])
        sumsq = sb("sumsq1", [P, 2, 4])
        var = sb("var1", [P, 2, 4])
        std = sb("std1", [P, 2, 4])
        tmp = sb("tmp1", [P, 2, 4])
        rstd = sb("rstd1", [P, 2, 4])
        z_ps = [ctx.enter_context(nc.psum_tensor(f"z_ps{i}", [P, HALF], F32)) for i in range(4)]
        t_ps = [ctx.enter_context(nc.psum_tensor(f"t_ps{i}", [P, HALF], F32)) for i in range(4)]

        const_loaded = sem("const_loaded1")
        w_loaded = [sem(f"win_loaded{i}") for i in range(2)]
        x_loaded = [sem(f"x_loaded{i}") for i in range(2)]
        w_hi_done = sem("win_hi_done")
        w_ready = sem("win_ready")
        squares_done = sem("squares_done1")
        var_ready = sem("var_ready1")
        std_ready = sem("std_ready1")
        rstd_chain = sem("rstd_chain1")
        xn_ready = sem("xn_ready1")
        transposed = sem("transposed1")
        h_hi_done = sem("h_hi_done1")
        h_ready = sem("h_ready1")
        z_ready = sem("z_ready")
        z_staged = sem("z_staged")
        z_stored = [sem(f"z_stored{i}") for i in range(4)]

        block = ctx.enter_context(nc.Block())

        @block.sync
        def _(sp):
            def load_x(j, slot):
                sp.dma_start(xin[:, slot, :, :],
                             x[bass.ds(j * HALF, HALF), :].rearrange("(t p) d -> p t d", p=P)).then_inc(x_loaded[slot], DMA)

            load_x(0, 0)
            sp.dma_start(eye[:, :], ident).then_inc(const_loaded, DMA)
            sp.dma_start(gain[:, :], g1).then_inc(const_loaded, DMA)
            for d in range(KT):
                if d >= 2:
                    sp.wait_ge(w_ready, d - 1)
                sp.dma_start(w_raw[:, d % 2, :], w_in[d * P:(d + 1) * P, :]).then_inc(w_loaded[d % 2], DMA)
            load_x(1, 1)
            with sp.Fori(0, (NJ - 2) // 2) as it:
                for slot in range(2):
                    j = it * 2 + 2 + slot
                    sp.wait_ge(transposed, (j - 1) * KT)
                    load_x(j, slot)

        @block.scalar
        def _(act):
            def squares(j, n, slot):
                act.wait_ge(x_loaded[slot], (n + 1) * DMA)
                for t in range(4):
                    if t:
                        act.wait_ge(squares_done, j * 4 + t)
                    act.activation(junk[:, :], xin[:, slot, t, :], ACT.Square,
                                   accum_out=sumsq[:, slot, t:t + 1]).then_inc(squares_done, 1)
                act.wait_ge(var_ready, j + 1)
                act.activation(std[:, slot, :], var[:, slot, :], ACT.Sqrt).then_inc(std_ready, 1)

            def round_h(j, slot, d):
                act.wait_ge(transposed, j * KT + d + 1)
                act.activation(h_hi[:, slot, d, :], t_ps[d % 4][:, :], ACT.Identity,
                               scale=gain[:, d:d + 1]).then_inc(h_hi_done, 1)

            def stage_z(j, c, first=False):
                act.wait_ge(z_ready, j * KT + c + 1)
                if not (first and c < 4):
                    act.wait_ge(z_stored[c % 4], (j * 2 + c // 4) * DMA)
                act.activation(z_out[:, c % 4, :], z_ps[c % 4][:, :], ACT.Copy).then_inc(z_staged, 1)

            def step(j, n_next, slot, first=False):
                squares(j + 1, n_next, 1 - slot)
                for c in range(3):
                    stage_z(j, c, first)
                for c in range(3, KT):
                    for d in range(2 * (c - 3), min(2 * (c - 2), KT)):
                        round_h(j + 1, 1 - slot, d)
                    stage_z(j, c, first)

            squares(0, 0, 0)
            for d in range(KT):
                act.wait_ge(w_loaded[d % 2], (d // 2 + 1) * DMA)
                act.activation(w_hi[:, d, :], w_raw[:, d % 2, :], ACT.Copy).then_inc(w_hi_done, 1)
                if d == 0:
                    act.wait_ge(const_loaded, 2 * DMA)
                round_h(0, 0, d)
            step(0, 0, 0, first=True)
            with act.Fori(0, (NJ - 2) // 2) as it:
                step(it * 2 + 1, it + 1, 1)
                step(it * 2 + 2, it + 1, 0)
            for c in range(KT):
                stage_z(NJ - 1, c)

        @block.vector
        def _(dve):
            def norm(j, slot):
                dve.wait_ge(squares_done, j * 4 + 4)
                dve.tensor_scalar(var[:, slot, :], sumsq[:, slot, :], 1.0 / D, EPS, ALU.mult, ALU.add).then_inc(var_ready, 1)
                dve.wait_ge(std_ready, j + 1)
                refined_rstd(dve, rstd_chain, j * 4, std[:, slot, :], var[:, slot, :], tmp[:, slot, :], rstd[:, slot, :])
                for t in range(4):
                    dve.tensor_scalar(xin[:, slot, t, :], xin[:, slot, t, :], rstd[:, slot, t:t + 1], None,
                                      ALU.mult).then_inc(xn_ready, 1)

            def rest_of_h(j, slot, d):
                dve.wait_ge(h_hi_done, j * KT + d + 1)
                dve.scalar_tensor_tensor(out=h_lo[:, slot, d, :], in0=t_ps[d % 4][:, :], scalar=gain[:, d:d + 1],
                                         in1=h_hi[:, slot, d, :].bitcast(F32), op0=ALU.mult,
                                         op1=ALU.subtract).then_inc(h_ready, 1)

            def step(j, slot):
                norm(j + 1, 1 - slot)
                for d in range(KT):
                    rest_of_h(j + 1, 1 - slot, d)

            norm(0, 0)
            dve.wait_ge(const_loaded, 2 * DMA)
            for d in range(KT):
                dve.wait_ge(w_hi_done, d + 1)
                dve.tensor_tensor(w_lo[:, d, :], w_raw[:, d % 2, :], w_hi[:, d, :].bitcast(F32),
                                  ALU.subtract).then_inc(w_ready, 1)
                rest_of_h(0, 0, d)
            step(0, 0)
            with dve.Fori(0, (NJ - 2) // 2) as it:
                step(it * 2 + 1, 1)
                step(it * 2 + 2, 0)

        @block.tensor
        def _(pe):
            def transposes(j, slot, d, first=False):
                if d == 0:
                    pe.wait_ge(xn_ready, j * 4 + 4)
                if not (first and d < 4):
                    pe.wait_ge(h_ready, j * KT + d - 3)
                for t in range(4):
                    mm = pe.transpose(t_ps[d % 4][:, t * P:(t + 1) * P], xin[:, slot, t, d * P:(d + 1) * P], eye[:, :])
                mm.then_inc(transposed, 1)

            def products(j, slot, c, first=False):
                if not (first and c < 4):
                    pe.wait_ge(z_staged, j * KT + c - 3)
                for d in range(KT):
                    if c == 0:
                        pe.wait_ge(h_ready, j * KT + d + 1)
                        if first:
                            pe.wait_ge(w_ready, d + 1)
                    mm = three_products(pe, z_ps[c % 4][:, :], w_hi[:, d, c * P:(c + 1) * P], w_lo[:, d, c * P:(c + 1) * P],
                                        h_hi[:, slot, d, :], h_lo[:, slot, d, :], d == 0, d == KT - 1)
                mm.then_inc(z_ready, 1)

            def step(j, slot, first=False):
                for c in range(KT):
                    products(j, slot, c, first)
                    if 2 <= c < 6:
                        transposes(j + 1, 1 - slot, 2 * (c - 2))
                        transposes(j + 1, 1 - slot, 2 * (c - 2) + 1)

            pe.wait_ge(const_loaded, 2 * DMA)
            for d in range(KT):
                transposes(0, 0, d, first=True)
            step(0, 0, first=True)
            with pe.Fori(0, (NJ - 2) // 2) as it:
                step(it * 2 + 1, 1)
                step(it * 2 + 2, 0)
            for c in range(KT):
                products(NJ - 1, (NJ - 1) % 2, c)

        @block.gpsimd
        def _(pool):
            with pool.Fori(0, NJ) as j:
                for c in range(KT):
                    pool.wait_ge(z_staged, j * KT + c + 1)
                    pool.dma_start(z_scr[c, :, bass.ds(j * HALF, HALF)], z_out[:, c % 4, :]).then_inc(z_stored[c % 4], DMA)
            for s in range(4):
                pool.wait_ge(z_stored[s], 2 * NJ * DMA)


def mix(nc, z_scr, y_scr, table, channel, w_fourier, w_pool, pool_gain, edge):
    places, TW = table_places()
    top = levels(max(SEQS))
    SMAX = max(SEQS)
    NCOL = 4

    def plan(S):
        lv = levels(S)
        fold_at, at = {}, 0
        for M in lv:
            for part in ("cos", "sin"):
                fold_at[M, part] = at
                at += M // 4 // P
        fold_at[BASE] = at
        n_fold = at + BASE // P
        tiles, need = [], []
        for i, M in enumerate(lv):
            for k, part in enumerate(("cos", "sin")):
                for t in range(M // 4 // P):
                    tiles.append((fold_at[M, part] + t, part))
                    need.append(2 * i + k + 1)
        for part in ("cos", "sin"):
            for t in range(BASE // P):
                tiles.append((fold_at[BASE] + t, part))
                need.append(2 * len(lv) + 1)
        groups = [list(range(a, min(a + NCOL, len(tiles)))) for a in range(0, len(tiles), NCOL)]
        return {
            "levels": lv, "fold_at": fold_at, "n_fold": n_fold, "tiles": tiles, "groups": groups,
            "need": [max(need[t] for t in g) for g in groups],
            "early": 2 * (S // 4 // P) // NCOL,
            "stages": len(lv) + 1,
            "folds": 2 * len(lv) + 1,
            "chain": 2 * len(lv) - 1,
        }

    plans = [plan(S) for S in SEQS]
    UV = max(len(p["tiles"]) for p in plans)
    NF = max(p["n_fold"] for p in plans)
    CREDIT = 4
    ch0 = [0, HEADS * len(plans[0]["groups"])]
    fold0 = [0, HEADS * plans[0]["folds"]]
    chain0 = [0, HEADS * plans[0]["chain"]]
    stage0 = [CREDIT, CREDIT + HEADS * plans[0]["stages"]]
    tok0 = [0, SEQS[0]]
    chunk0 = [0, HEADS * SEQS[0] // HALF]
    edge_at = [sum(WINDOWS[:g]) for g in range(4)]
    RAW = TW // 4

    with ExitStack() as ctx:
        def sb(name, shape, dt=F32):
            return ctx.enter_context(nc.sbuf_tensor(name, shape, dt))

        def sem(name):
            return ctx.enter_context(nc.semaphore(name))

        tab_hi = sb("tab_hi", [P, TW], F32R)
        tab_lo = sb("tab_lo", [P, TW], F32R)
        tab_raw = sb("tab_raw", [P, 2, RAW])
        zy = sb("zy", [P, HEADS * SMAX])
        folds = sb("folds", [P, NF, P])
        diff = sb("diff", [P, SMAX // 2 + 1])
        sums = sb("sums", [P, SMAX - BASE])
        uv_hi = sb("uv_hi", [P, UV, P], F32R)
        uv_lo = sb("uv_lo", [P, UV, P], F32R)
        sine_part = sb("sine_part", [P, 2, SMAX // 4])
        chan = sb("chan", [P, 2, P])
        wf = sb("wf", [P, HEADS, P])
        chan_w = sb("chan_w", [P, 2, HEADS, P])
        wp = sb("wp", [P, 4, P])
        pg = sb("pg", [P, 4])
        edges = sb("edges", [P, sum(WINDOWS)])
        zb = sb("zb", [P, 4, PAD + SMAX + PAD])
        win = [sb(f"win{i}", [P, PAD + SMAX + PAD]) for i in range(2)]
        yb = sb("yb", [P, 4, HALF])
        ch_ps = [ctx.enter_context(nc.psum_tensor(f"ch_ps{i}", [P, NCOL, P], F32)) for i in range(2)]
        cos_ps = [ctx.enter_context(nc.psum_tensor(f"cos_ps{i}", [P, SMAX // 4], F32)) for i in range(2)]
        sin_ps = [ctx.enter_context(nc.psum_tensor(f"sin_ps{i}", [P, SMAX // 4], F32)) for i in range(2)]
        base_ps = ctx.enter_context(nc.psum_tensor("base_ps", [P, BASE], F32))

        chan_loaded = sem("chan_loaded")
        pool_w_loaded = sem("pool_w_loaded")
        tab_loaded = [sem(f"tab_loaded{i}") for i in range(2)]
        tab_hi_done = sem("tab_hi_done")
        tab_ready = sem("tab_ready")
        chan_w_ps_ready = sem("chan_w_ps_ready")
        chan_w_ready = sem("chan_w_ready")
        z_loaded = [sem(f"zh_loaded{i}") for i in range(2 * HEADS)]
        zb_loaded = [sem(f"zb_loaded{i}") for i in range(4)]
        zeroed = sem("zeroed")
        fold_chain = sem("fold_chain")
        fold_done = sem("fold_done")
        ch_ready = sem("ch_ready")
        uv_hi_done = sem("uv_hi_done")
        uv_ready = sem("uv_ready")
        cos_sin_ready = sem("cos_sin_ready")
        sine_copied = sem("sine_copied")
        stage_done = sem("stage_done")
        y_stored = [sem(f"y_stored{i}") for i in range(2)]
        pool_chain = sem("pool_chain")
        dve_pool_chain = sem("dve_pool_chain")
        d_by_pool = sem("d_by_pool")
        d_by_dve = sem("d_by_dve")
        yb_ready = sem("yb_ready")
        yb_staged = sem("yb_staged")
        yb_stored = [sem(f"yb_stored{i}") for i in range(4)]

        block = ctx.enter_context(nc.Block())

        @block.sync
        def _(sp):
            sp.dma_start(chan[:, :, :], channel.rearrange("p (a c) -> p a c", a=2)).then_inc(chan_loaded, DMA)
            sp.dma_start(wf[:, :, :], w_fourier.rearrange("h c d -> c h d")).then_inc(chan_loaded, DMA)

            def load_head(q, h):
                S = SEQS[q]
                sp.dma_start(zy[:, h * S:(h + 1) * S], z_scr[h, :, tok0[q]:tok0[q] + S]).then_inc(z_loaded[q * HEADS + h], DMA)

            def load_groups(q):
                S = SEQS[q]
                for g in (3, 2, 0, 1):
                    sp.dma_start(zb[:, g, PAD:PAD + S], z_scr[HEADS + g, :, tok0[q]:tok0[q] + S]).then_inc(zb_loaded[g], DMA)

            load_head(0, 0)
            for n in range(2):
                sp.dma_start(tab_raw[:, n, :], table[:, n * RAW:(n + 1) * RAW]).then_inc(tab_loaded[n], DMA)
            load_groups(0)
            load_head(0, 1)
            for n in range(2, 4):
                sp.wait_ge(tab_ready, n - 1)
                sp.dma_start(tab_raw[:, n % 2, :], table[:, n * RAW:(n + 1) * RAW]).then_inc(tab_loaded[n % 2], DMA)
            sp.dma_start(wp[:, :, :], w_pool.rearrange("g c d -> c g d")).then_inc(pool_w_loaded, DMA)
            sp.dma_start(pg[:, :], pool_gain).then_inc(pool_w_loaded, DMA)
            sp.dma_start(edges[:, :], edge).then_inc(pool_w_loaded, DMA)
            load_head(0, 2)
            load_head(0, 3)
            for q, S in enumerate(SEQS):
                with sp.Fori(0, HEADS) as h:
                    sp.wait_ge(stage_done, h * plans[q]["stages"] + (stage0[q] + plans[q]["stages"]))
                    sp.dma_start(y_scr[bass.ds(h, 1), :, tok0[q]:tok0[q] + S].rearrange("a p s -> p (a s)"),
                                 zy[:, bass.ds(h * S, S)]).then_inc(y_stored[q], DMA)
                if q == 0:
                    sp.wait_ge(y_stored[0], HEADS * DMA)
                    for h in range(HEADS):
                        load_head(1, h)
                with sp.Fori(0, HEADS * S // HALF // 4) as i:
                    for s in range(4):
                        n = i * 4 + s
                        sp.wait_ge(yb_staged, n + (chunk0[q] + 1))
                        if S == SEQS[0]:
                            dst = y_scr[bass.ds(i + HEADS, 1), :, s * HALF:(s + 1) * HALF]
                        else:
                            dst = y_scr[bass.ds(i * 2 + (HEADS + s // 2), 1), :,
                                        tok0[q] + (s % 2) * HALF:tok0[q] + (s % 2 + 1) * HALF]
                        sp.dma_start(dst.rearrange("a p s -> p (a s)"), yb[:, s, :]).then_inc(yb_stored[s], DMA)
                if q == 0:
                    load_groups(1)
            sp.wait_ge(y_stored[1], HEADS * DMA)
            for s in range(4):
                sp.wait_ge(yb_stored[s], HEADS * TOKENS // HALF // 4 * DMA)

        @block.gpsimd
        def _(pool):
            chained = 0

            def chain(ins):
                nonlocal chained
                chained += 1
                ins.then_inc(pool_chain, 1)
                pool.wait_ge(pool_chain, chained)

            pool.memset(diff[:, SMAX // 2:], 0.0).then_inc(zeroed, 1)
            for q, S in enumerate(SEQS):
                if q:
                    pool.wait_ge(yb_ready, chunk0[1])
                for g in range(4):
                    if q == 0:
                        pool.memset(zb[:, g, 0:PAD], 0.0).then_inc(zeroed, 1)
                    pool.memset(zb[:, g, PAD + S:PAD + S + PAD], 0.0).then_inc(zeroed, 1)
                pool.wait_ge(zeroed, 1 + 8 + 4 * q)
                for g in (3, 2):
                    k = WINDOWS[g]
                    pool.wait_ge(zb_loaded[g], (q + 1) * DMA)
                    if g == 2:
                        pool.wait_ge(d_by_pool, 2 * q + 1)
                    if q == 0 and g == 3:
                        pool.wait_ge(pool_w_loaded, 3 * DMA)
                    src, lo, hi = zb[:, g, :], PAD - k // 2 + 1, PAD + S + k // 2 - 1
                    chain(pool.tensor_tensor(win[0][:, lo:hi], src[:, lo - 1:hi - 1], src[:, lo:hi], ALU.add))
                    n, a = 2, 0
                    while n < k:
                        lo, hi = lo + n // 2, hi - n // 2
                        chain(pool.tensor_tensor(win[1 - a][:, lo:hi], win[a][:, lo - n // 2:hi - n // 2],
                                                 win[a][:, lo + n // 2:hi + n // 2], ALU.add))
                        n, a = 2 * n, 1 - a
                    s = win[a][:, PAD:PAD + S]
                    z = src[:, PAD:PAD + S]
                    e = edge_at[g]
                    chain(pool.tensor_scalar(s[:, k // 2:S - k // 2], s[:, k // 2:S - k // 2], 1.0 / k, None, ALU.mult))
                    chain(pool.tensor_tensor(s[:, :k // 2], s[:, :k // 2], edges[:, e:e + k // 2], ALU.mult))
                    chain(pool.tensor_tensor(s[:, S - k // 2:], s[:, S - k // 2:], edges[:, e + k // 2:e + k], ALU.mult))
                    pool.tensor_tensor(z, s, z, ALU.subtract).then_inc(d_by_pool, 1)

        @block.scalar
        def _(act):
            for n in range(4):
                act.wait_ge(tab_loaded[n % 2], (n // 2 + 1) * DMA)
                act.activation(tab_hi[:, n * RAW:(n + 1) * RAW], tab_raw[:, n % 2, :], ACT.Copy).then_inc(tab_hi_done, 1)
                if n == 0:
                    act.wait_ge(chan_w_ps_ready, 1)
                    for part in range(2):
                        act.activation(chan_w[:, part, :, :], ch_ps[part][:, :, :], ACT.Copy).then_inc(chan_w_ready, 1)
            act.wait_ge(pool_w_loaded, 3 * DMA)
            for q, S in enumerate(SEQS):
                p = plans[q]
                G, L = len(p["groups"]), len(p["levels"])

                def round_uv(h, g):
                    act.wait_ge(ch_ready, h * G + (ch0[q] + g + 1))
                    ts = p["groups"][g]
                    act.activation(uv_hi[:, ts[0]:ts[-1] + 1, :], ch_ps[g % 2][:, 0:len(ts), :], ACT.Copy).then_inc(uv_hi_done, 1)

                def copy_sine(h, level):
                    n = p["levels"][level] // 4
                    act.wait_ge(cos_sin_ready, h * p["stages"] + (stage0[q] - CREDIT + level + 1))
                    act.wait_ge(stage_done, h * p["stages"] + (stage0[q] + level - 1))
                    act.activation(sine_part[:, level % 2, 0:n], sin_ps[level % 2][:, 0:n], ACT.Copy,
                                   scale=float(S) ** -0.5).then_inc(sine_copied, 1)

                def body(h, more):
                    copy_sine(h, 0)
                    if more:
                        for g in range(p["early"]):
                            round_uv(h + 1, g)
                    for level in range(1, L):
                        copy_sine(h, level)
                    if more:
                        for g in range(p["early"], G):
                            round_uv(h + 1, g)

                for g in range(G):
                    round_uv(0, g)
                with act.Fori(0, HEADS - 1) as h:
                    body(h, True)
                body(HEADS - 1, False)

                def stage_yb(n, s, g, first=False):
                    act.wait_ge(yb_ready, n + 1)
                    if not first:
                        act.wait_ge(yb_stored[s], n // 4 * DMA)
                    act.activation(yb[:, s, :], ch_ps[s % 2][:, :, :].rearrange("p a b -> p (a b)"), ACT.Identity,
                                   scale=pg[:, g:g + 1]).then_inc(yb_staged, 1)

                for i in range(HEADS * S // HALF):
                    stage_yb(chunk0[q] + i, i % 4, i // (S // HALF), first=chunk0[q] + i < 4)

        @block.vector
        def _(dve):
            dve.sem_inc(stage_done, CREDIT)
            dve_chained = 0
            for q, S in enumerate(SEQS):
                p = plans[q]
                G, L = len(p["groups"]), len(p["levels"])
                fold_at = p["fold_at"]
                gidx = {}
                for g, ts in enumerate(p["groups"]):
                    for t in ts:
                        gidx[p["tiles"][t][0]] = g

                def fold(h, static=None):
                    if static is not None:
                        dve.wait_ge(z_loaded[q * HEADS + static], DMA)
                    src = zy[:, bass.ds(h * S, S)]
                    chain = h * p["chain"] + chain0[q]
                    steps = 0
                    out = 0
                    for level, M in enumerate(p["levels"]):
                        n, m = M // 2, M // 4
                        last = level == L - 1
                        d = diff[:, SMAX // 2 - n:SMAX // 2 + 1]
                        if level or q or static is None:
                            dve.wait_ge(fold_done, h * p["folds"] + (fold0[q] + 2 * level))
                        dve.tensor_tensor(d[:, 0:n], src[:, 0:n], src[:, n:M], ALU.subtract).then_inc(fold_chain, 1)
                        if last:
                            dst = folds[:, fold_at[BASE]:fold_at[BASE] + BASE // P, :].rearrange("p a b -> p (a b)")
                        else:
                            dst = sums[:, out:out + n]
                            dve.tensor_tensor(dst, src[:, 0:n], src[:, n:M], ALU.add).then_inc(fold_chain, 1)
                        dve.wait_ge(fold_chain, chain + steps + 1)
                        for k, part in enumerate(("cos", "sin")):
                            f = fold_at[M, part]
                            if static is None or q:
                                dve.wait_ge(ch_ready, (h - 1) * G + (ch0[q] + gidx[f + m // P - 1] + 1) if static is None
                                            else ch0[q])
                            o = folds[:, f:f + m // P, :].rearrange("p a b -> p (a b)")
                            if k == 0:
                                dve.tensor_tensor(o, d[:, 0:m], d[:, n:n - m:-1], ALU.subtract).then_inc(fold_done, 1)
                            else:
                                dve.tensor_tensor(o, d[:, 1:m + 1], d[:, n - 1:n - m - 1:-1], ALU.add).then_inc(fold_done, 1)
                        if last:
                            if static is None:
                                dve.wait_ge(ch_ready, (h - 1) * G + (ch0[q] + G))
                            dve.tensor_tensor(dst, src[:, 0:n], src[:, n:M], ALU.add).then_inc(fold_done, 1)
                        else:
                            dve.wait_ge(fold_chain, chain + steps + 2)
                            src, out, steps = dst, out + n, steps + 2

                def rest_of_uv(h, g):
                    dve.wait_ge(uv_hi_done, h * G + (ch0[q] + g + 1))
                    ts = p["groups"][g]
                    dve.tensor_tensor(uv_lo[:, ts[0]:ts[-1] + 1, :], ch_ps[g % 2][:, 0:len(ts), :],
                                      uv_hi[:, ts[0]:ts[-1] + 1, :].bitcast(F32), ALU.subtract).then_inc(uv_ready, 1)

                def outputs(h, level):
                    M = p["levels"][level]
                    m, step = M // 4, S // M
                    y = zy[:, bass.ds(h * S, S)]
                    dve.wait_ge(sine_copied, h * L + (q * HEADS * len(plans[0]["levels"]) + level + 1))
                    dve.scalar_tensor_tensor(out=y[:, step:step + 2 * step * m:2 * step], in0=cos_ps[level % 2][:, 0:m],
                                             scalar=float(S) ** -0.5, in1=sine_part[:, level % 2, 0:m],
                                             op0=ALU.mult, op1=ALU.subtract)
                    dve.scalar_tensor_tensor(out=y[:, S // 2 + step:S:2 * step], in0=cos_ps[level % 2][:, m - 1::-1],
                                             scalar=float(S) ** -0.5, in1=sine_part[:, level % 2, m - 1::-1],
                                             op0=ALU.mult, op1=ALU.add).then_inc(stage_done, 1)

                def base_outputs(h):
                    dve.wait_ge(cos_sin_ready, h * p["stages"] + (stage0[q] - CREDIT + p["stages"]))
                    y = zy[:, bass.ds(h * S, S)]
                    dve.tensor_scalar(y[:, 0:S:S // BASE], base_ps[:, :], float(S) ** -0.5, None,
                                      ALU.mult).then_inc(stage_done, 1)

                def body(h, more, fold_next):
                    outputs(h, 0)
                    if more:
                        for g in range(p["early"]):
                            rest_of_uv(h + 1, g)
                    for level in range(1, L):
                        outputs(h, level)
                    if more:
                        for g in range(p["early"], G):
                            rest_of_uv(h + 1, g)
                    base_outputs(h)
                    if fold_next:
                        fold(h + 2)

                if q == 0:
                    dve.wait_ge(zeroed, 1)
                fold(0, static=0)
                if q == 0:
                    for n in range(4):
                        dve.wait_ge(tab_hi_done, n + 1)
                        dve.tensor_tensor(tab_lo[:, n * RAW:(n + 1) * RAW], tab_raw[:, n % 2, :],
                                          tab_hi[:, n * RAW:(n + 1) * RAW].bitcast(F32), ALU.subtract).then_inc(tab_ready, 1)
                for g in range(G):
                    rest_of_uv(0, g)
                for h in range(1, HEADS):
                    dve.wait_ge(z_loaded[q * HEADS + h], DMA)
                fold(1)
                with dve.Fori(0, HEADS - 2) as h:
                    body(h, True, True)
                body(HEADS - 2, True, False)
                body(HEADS - 1, False, False)

                for g in range(2):
                    k = WINDOWS[g]
                    dve.wait_ge(zb_loaded[g], (q + 1) * DMA)
                    if g == 1:
                        dve.wait_ge(d_by_dve, 2 * q + 1)
                    if g == 0:
                        dve.wait_ge(zeroed, 1 + 8 + 4 * q)
                        dve.wait_ge(pool_w_loaded, 3 * DMA)
                        dve.wait_ge(d_by_pool, 2 * q + 2)
                    src, lo, hi = zb[:, g, :], PAD - k // 2 + 1, PAD + S + k // 2 - 1
                    dve.tensor_tensor(win[0][:, lo:hi], src[:, lo - 1:hi - 1], src[:, lo:hi], ALU.add).then_inc(dve_pool_chain, 1)
                    dve_chained += 1
                    dve.wait_ge(dve_pool_chain, dve_chained)
                    a = 0
                    if k == 4:
                        dve.tensor_tensor(win[1][:, lo + 1:hi - 1], win[0][:, lo:hi - 2], win[0][:, lo + 2:hi],
                                          ALU.add).then_inc(dve_pool_chain, 1)
                        dve_chained += 1
                        dve.wait_ge(dve_pool_chain, dve_chained)
                        a = 1
                    s = win[a][:, PAD:PAD + S]
                    z = src[:, PAD:PAD + S]
                    e = edge_at[g]
                    dve.tensor_tensor(s[:, :k // 2], s[:, :k // 2], edges[:, e:e + k // 2], ALU.mult)
                    dve.tensor_tensor(s[:, S - k // 2:], s[:, S - k // 2:], edges[:, e + k // 2:e + k], ALU.mult).then_inc(dve_pool_chain, 1)
                    dve.scalar_tensor_tensor(out=z[:, k // 2:S - k // 2], in0=s[:, k // 2:S - k // 2], scalar=1.0 / k,
                                             in1=z[:, k // 2:S - k // 2], op0=ALU.mult, op1=ALU.subtract)
                    dve_chained += 1
                    dve.wait_ge(dve_pool_chain, dve_chained)
                    dve.tensor_tensor(z[:, :k // 2], s[:, :k // 2], z[:, :k // 2], ALU.subtract)
                    dve.tensor_tensor(z[:, S - k // 2:], s[:, S - k // 2:], z[:, S - k // 2:], ALU.subtract).then_inc(d_by_dve, 1)

        @block.tensor
        def _(pe):
            pe.wait_ge(chan_loaded, 2 * DMA)
            for part in range(2):
                for h in range(HEADS):
                    mm = pe.matmul(ch_ps[part][:, h, :], chan[:, part, :], wf[:, h, :], start=True, stop=True)
            mm.then_inc(chan_w_ps_ready, 1)
            pe.wait_ge(chan_w_ready, 2)
            for q, S in enumerate(SEQS):
                p = plans[q]
                G, L = len(p["groups"]), len(p["levels"])

                def channel_products(h, g, first=False):
                    pe.wait_ge(fold_done, h * p["folds"] + (fold0[q] + p["need"][g]))
                    if g >= 2:
                        pe.wait_ge(uv_ready, h * G + (ch0[q] + g - 1))
                    elif not first:
                        pe.wait_ge(uv_ready, h * G + ch0[q])
                    for i, t in enumerate(p["groups"][g]):
                        f, part = p["tiles"][t]
                        mm = pe.matmul(ch_ps[g % 2][:, i, :], folds[:, f, :], chan_w_of(h, part), start=True, stop=True)
                    mm.then_inc(ch_ready, 1)

                def chan_w_of(h, part):
                    return chan_w[:, ("cos", "sin").index(part), bass.ds(h, 1), :].rearrange("p a b -> p (a b)")

                tile_at = {}
                t = 0
                for M in p["levels"]:
                    for part in ("cos", "sin"):
                        tile_at[M, part] = t
                        t += M // 4 // P
                for part in ("cos", "sin"):
                    tile_at[BASE, part] = t
                    t += BASE // P

                def transform(out, M, part, width, rows, first, last):
                    for r in range(rows):
                        t = tile_at[M, part] + r
                        a = places[M, part] + r * width
                        mm = three_products(pe, out, uv_hi[:, t, :], uv_lo[:, t, :], tab_hi[:, a:a + width], tab_lo[:, a:a + width],
                                            first and r == 0, last and r == rows - 1)
                    return mm

                def level_products(h, level):
                    M = p["levels"][level]
                    m = M // 4
                    pe.wait_ge(stage_done, h * p["stages"] + (stage0[q] + level - 1))
                    transform(cos_ps[level % 2][:, 0:m], M, "cos", m, m // P, True, True)
                    transform(sin_ps[level % 2][:, 0:m], M, "sin", m, m // P, True, True).then_inc(cos_sin_ready, 1)

                def base_products(h):
                    pe.wait_ge(stage_done, h * p["stages"] + stage0[q])
                    transform(base_ps[:, :], BASE, "cos", BASE, BASE // P, True, False)
                    transform(base_ps[:, :], BASE, "sin", BASE, BASE // P, False, True).then_inc(cos_sin_ready, 1)

                def body(h, more):
                    pe.wait_ge(uv_ready, h * G + (ch0[q] + p["early"]))
                    level_products(h, 0)
                    if more:
                        for g in range(p["early"]):
                            channel_products(h + 1, g)
                    pe.wait_ge(uv_ready, h * G + (ch0[q] + G))
                    for level in range(1, L):
                        level_products(h, level)
                    base_products(h)
                    if more:
                        for g in range(p["early"], G):
                            channel_products(h + 1, g)

                if q:
                    pe.wait_ge(yb_staged, chunk0[1])
                for g in range(G):
                    channel_products(0, g, first=q == 0)
                if q == 0:
                    pe.wait_ge(tab_ready, 4)
                with pe.Fori(0, HEADS - 1) as h:
                    body(h, True)
                body(HEADS - 1, False)

                pe.wait_ge(uv_ready, ch0[q] + HEADS * G)
                pe.wait_ge(pool_w_loaded, 3 * DMA)
                for i in range(HEADS * S // HALF):
                    n, g, c = chunk0[q] + i, i // (S // HALF), i % (S // HALF)
                    if c == 0:
                        if g < 2:
                            pe.wait_ge(d_by_dve, 2 * q + g + 1)
                        elif g == 2:
                            pe.wait_ge(d_by_pool, 2 * q + 2)
                    if n >= 2:
                        pe.wait_ge(yb_staged, n - 1)
                    pe.matmul(ch_ps[i % 2][:, :, :].rearrange("p a b -> p (a b)"), wp[:, g, :],
                              zb[:, g, PAD + c * HALF:PAD + (c + 1) * HALF], start=True, stop=True).then_inc(yb_ready, 1)


def project_out(nc, y_scr, x, w_out, ident, x1_scr, h2_scr):
    NT = TOKENS // P
    with ExitStack() as ctx:
        def sb(name, shape, dt=F32):
            return ctx.enter_context(nc.sbuf_tensor(name, shape, dt))

        def sem(name):
            return ctx.enter_context(nc.semaphore(name))

        w_hi = sb("wout_hi", [P, KT, D], F32R)
        w_lo = sb("wout_lo", [P, KT, D], F32R)
        w_raw = sb("wout_raw", [P, 2, D])
        y_raw = sb("y_raw", [P, KT, HALF])
        y_hi = sb("y_hi", [P, 4, KT, P], F32R)
        y_lo = sb("y_lo", [P, 4, KT, P], F32R)
        x1 = sb("x1", [P, 4, D])
        xn = sb("xn", [P, 2, D])
        junk = sb("junk3", [P, D])
        h_out = sb("h_out", [P, 4, KT, P])
        eye = sb("eye3", [P, P])
        sumsq = sb("sumsq3", [P, 4])
        var = sb("var3", [P, 4])
        std = sb("std3", [P, 4])
        tmp = sb("tmp3", [P, 4])
        rstd = sb("rstd3", [P, 4])
        o_ps = [ctx.enter_context(nc.psum_tensor(f"o_ps{i}", [P, HALF], F32)) for i in range(4)]
        t_ps = [ctx.enter_context(nc.psum_tensor(f"t3_ps{i}", [P, 4, P], F32)) for i in range(4)]

        const_loaded = sem("const_loaded3")
        w_loaded = [sem(f"wout_loaded{i}") for i in range(2)]
        w_hi_done = sem("wout_hi_done")
        w_ready = sem("wout_ready")
        y_loaded = sem("y_loaded")
        x_loaded = [sem(f"x3_loaded{i}") for i in range(4)]
        y_hi_done = sem("y_hi_done")
        y_ready = sem("y_ready")
        o_ready_half = sem("o_ready_half")
        x1_ready = sem("x1_ready")
        squares_done = sem("squares_done3")
        var_ready = sem("var_ready3")
        std_ready = sem("std_ready3")
        rstd_chain = sem("rstd_chain3")
        xn_ready = sem("xn_ready3")
        transposed = sem("transposed3")
        h_staged = sem("h_staged3")
        x1_stored = [sem(f"x1_stored{i}") for i in range(4)]
        h_stored = [sem(f"h_stored{i}") for i in range(4)]

        block = ctx.enter_context(nc.Block())

        @block.sync
        def _(sp):
            def load_y(j):
                sp.dma_start(y_raw[:, :, :], y_scr[:, :, bass.ds(j * HALF, HALF)].rearrange("c p s -> p c s")).then_inc(y_loaded, DMA)

            def load_x(j, t):
                sp.dma_start(x1[:, t, :], x[bass.ds(j * HALF + t * P, P), :]).then_inc(x_loaded[t], DMA)

            load_y(0)
            sp.dma_start(eye[:, :], ident).then_inc(const_loaded, DMA)
            for d in range(KT):
                if d >= 2:
                    sp.wait_ge(w_ready, d - 1)
                sp.dma_start(w_raw[:, d % 2, :], w_out[d * P:(d + 1) * P, :]).then_inc(w_loaded[d % 2], DMA)
            for t in range(4):
                load_x(0, t)
            with sp.Fori(1, NT // 4) as j:
                sp.wait_ge(y_ready, j * 4)
                load_y(j)
                for t in range(4):
                    sp.wait_ge(x1_stored[t], j * DMA)
                    load_x(j, t)

        @block.scalar
        def _(act):
            def round_y(j, t, first=False):
                act.wait_ge(y_loaded, (j + 1) * DMA)
                if not first:
                    act.wait_ge(o_ready_half, j * 8 + 2 * (t - 3))
                act.activation(y_hi[:, t, :, :], y_raw[:, :, t * P:(t + 1) * P], ACT.Copy).then_inc(y_hi_done, 1)

            def norm(n, t):
                act.wait_ge(x1_ready, n * 2 + 2)
                act.activation(junk[:, :], x1[:, t, :], ACT.Square, accum_out=sumsq[:, t:t + 1]).then_inc(squares_done, 1)
                act.wait_ge(var_ready, n + 1)
                act.activation(std[:, t:t + 1], var[:, t:t + 1], ACT.Sqrt).then_inc(std_ready, 1)

            def stage_h(m, slot, stored=None):
                for k in range(2):
                    act.wait_ge(transposed, m * 2 + (k + 1))
                    if k == 0 and stored is not None:
                        act.wait_ge(h_stored[slot], stored)
                    act.activation(h_out[:, slot, 4 * k:4 * k + 4, :], t_ps[(slot % 2) * 2 + k][:, :, :], ACT.Copy).then_inc(h_staged, 1)

            def step(j, t, lead=True, first=False):
                n = j * 4 + t
                if lead:
                    round_y(j + (t + 2) // 4, (t + 2) % 4, first=first and t < 2)
                if not (first and t == 0):
                    norm(n - 1, (t + 3) % 4)
                    uses = j if t else j - 1
                    stage_h(n - 1, (t + 3) % 4, None if isinstance(uses, int) and uses < 1 else uses * DMA)

            for d in range(KT):
                act.wait_ge(w_loaded[d % 2], (d // 2 + 1) * DMA)
                act.activation(w_hi[:, d, :], w_raw[:, d % 2, :], ACT.Copy).then_inc(w_hi_done, 1)
                if d in (1, 2):
                    round_y(0, d - 1, first=True)
            for t in range(4):
                step(0, t, first=True)
            for t in range(4):
                step(1, t)
            with act.Fori(2, NT // 4 - 1) as j:
                for t in range(4):
                    step(j, t)
            for t in range(4):
                step(NT // 4 - 1, t, lead=t < 2)
            norm(NT - 1, 3)
            stage_h(NT - 1, 3, (NT // 4 - 1) * DMA)

        @block.vector
        def _(dve):
            def rest_of_y(j, t):
                dve.wait_ge(y_hi_done, j * 4 + (t + 1))
                dve.tensor_tensor(y_lo[:, t, :, :], y_raw[:, :, t * P:(t + 1) * P], y_hi[:, t, :, :].bitcast(F32),
                                  ALU.subtract).then_inc(y_ready, 1)

            def residual(m, slot, loads):
                dve.wait_ge(x_loaded[slot], loads)
                for c in range(2):
                    dve.wait_ge(o_ready_half, m * 2 + (c + 1))
                    dve.tensor_tensor(x1[:, slot, c * HALF:(c + 1) * HALF], o_ps[(slot % 2) * 2 + c][:, :],
                                      x1[:, slot, c * HALF:(c + 1) * HALF], ALU.add).then_inc(x1_ready, 1)
                dve.wait_ge(squares_done, m + 1)
                one = slice(slot, slot + 1)
                dve.tensor_scalar(var[:, one], sumsq[:, one], 1.0 / D, EPS, ALU.mult, ALU.add).then_inc(var_ready, 1)
                dve.wait_ge(std_ready, m + 1)
                refined_rstd(dve, rstd_chain, m * 4, std[:, one], var[:, one], tmp[:, one], rstd[:, one])
                dve.tensor_scalar(xn[:, slot % 2, :], x1[:, slot, :], rstd[:, one], None, ALU.mult).then_inc(xn_ready, 1)

            def step(j, t, lead=True, first=False):
                if lead:
                    rest_of_y(j + (t + 2) // 4, (t + 2) % 4)
                if not (first and t == 0):
                    residual(j * 4 + (t - 1), (t + 3) % 4, (j + 1) * DMA if t else j * DMA)

            for d in range(KT):
                dve.wait_ge(w_hi_done, d + 1)
                dve.tensor_tensor(w_lo[:, d, :], w_raw[:, d % 2, :], w_hi[:, d, :].bitcast(F32),
                                  ALU.subtract).then_inc(w_ready, 1)
                if d in (1, 2):
                    rest_of_y(0, d - 1)
            for t in range(4):
                step(0, t, first=True)
            with dve.Fori(1, NT // 4 - 1) as j:
                for t in range(4):
                    step(j, t)
            for t in range(4):
                step(NT // 4 - 1, t, lead=t < 2)
            residual(NT - 1, 3, NT // 4 * DMA)

        @block.tensor
        def _(pe):
            def products(n, t, first=False):
                pe.wait_ge(y_ready, n + 1)
                for c in range(2):
                    if not (first and t < 2):
                        pe.wait_ge(x1_ready, n * 2 + (c - 3))
                    for d in range(KT):
                        if first and t == 0 and c == 0:
                            pe.wait_ge(w_ready, d + 1)
                        mm = three_products(pe, o_ps[(t % 2) * 2 + c][:, :], y_hi[:, t, d, :], y_lo[:, t, d, :],
                                            w_hi[:, d, c * HALF:(c + 1) * HALF], w_lo[:, d, c * HALF:(c + 1) * HALF],
                                            d == 0, d == KT - 1)
                    mm.then_inc(o_ready_half, 1)

            def transposes(m, slot, first=False):
                pe.wait_ge(xn_ready, m + 1)
                for k in range(2):
                    if not first:
                        pe.wait_ge(h_staged, m * 2 + (k - 3))
                    for i in range(4):
                        d = 4 * k + i
                        mm = pe.transpose(t_ps[(slot % 2) * 2 + k][:, i, :], xn[:, slot % 2, d * P:(d + 1) * P], eye[:, :])
                    mm.then_inc(transposed, 1)

            def step(j, t, first=False):
                products(j * 4 + t, t, first)
                if not (first and t == 0):
                    transposes(j * 4 + (t - 1), (t + 3) % 4, first=first and t < 3)

            pe.wait_ge(const_loaded, DMA)
            for t in range(4):
                step(0, t, first=True)
            with pe.Fori(1, NT // 4) as j:
                for t in range(4):
                    step(j, t)
            transposes(NT - 1, 3)

        @block.gpsimd
        def _(pool):
            def store_x1(j, t):
                pool.wait_ge(xn_ready, j * 4 + (t + 1))
                pool.dma_start(x1_scr[bass.ds(j * HALF + t * P, P), :], x1[:, t, :]).then_inc(x1_stored[t], DMA)

            def store_h(m, slot):
                pool.wait_ge(h_staged, m * 2 + 2)
                pool.dma_start(h2_scr[:, :, bass.ds(m * P, P)].rearrange("d p s -> p d s"), h_out[:, slot, :, :]).then_inc(h_stored[slot], DMA)

            for t in range(4):
                store_x1(0, t)
                if t:
                    store_h(t - 1, t - 1)
            with pool.Fori(1, NT // 4) as j:
                for t in range(4):
                    store_x1(j, t)
                    store_h(j * 4 + (t - 1), (t + 3) % 4)
            store_h(NT - 1, 3)
            for t in range(4):
                pool.wait_ge(x1_stored[t], NT // 4 * DMA)
                pool.wait_ge(h_stored[t], NT // 4 * DMA)


def ffn(nc, x1_scr, h2_scr, w_gate, w_up, w_down, g2, gf, out):
    TB = 2 * HALF
    NB = TOKENS // TB
    NP = FT // 2
    ST = HALF // P
    with ExitStack() as ctx:
        def sb(name, shape, dt=F32):
            return ctx.enter_context(nc.sbuf_tensor(name, shape, dt))

        def sem(name):
            return ctx.enter_context(nc.semaphore(name))

        h_hi = sb("h2_hi", [P, 2, KT, HALF], F32R)
        h_lo = sb("h2_lo", [P, 2, KT, HALF], F32R)
        h_raw = sb("h2_raw", [P, 2, HALF])
        acc = sb("acc", [P, 2 * ST, D])
        raw = sb("w_raw4", [P, 3, D])
        w_hi = sb("w_hi4", [P, 6, D], F32R)
        w_lo = sb("w_lo4", [P, 6, D], F32R)
        silu = sb("silu", [P, 2, HALF])
        prod = sb("prod", [P, 2, HALF])
        a_hi = sb("a_hi", [P, 4, HALF], F32R)
        a_lo = sb("a_lo", [P, 4, HALF], F32R)
        junk = sb("junk4", [P, D])
        gain2 = sb("gain2", [P, KT])
        gain_f = sb("gain_f", [P, D])
        sumsq = sb("sumsq4", [P, 2 * ST])
        var = sb("var4", [P, 2 * ST])
        std = sb("std4", [P, 2 * ST])
        tmp = sb("tmp4", [P, 2 * ST])
        rstd = sb("rstd4", [P, 2 * ST])
        gate_ps = [ctx.enter_context(nc.psum_tensor(f"gate_ps{i}", [P, HALF], F32)) for i in range(2)]
        up_ps = [ctx.enter_context(nc.psum_tensor(f"up_ps{i}", [P, HALF], F32)) for i in range(2)]
        down_ps = [ctx.enter_context(nc.psum_tensor(f"down_ps{i}", [P, HALF], F32)) for i in range(4)]

        gain_loaded = sem("gain_loaded4")
        gain_f_loaded = sem("gain_f_loaded")
        raw_loaded = [sem(f"raw_loaded{i}") for i in range(3)]
        w_hi_done = sem("w_hi_done4")
        w_ready = sem("w_ready4")
        h_loaded = [sem(f"h2_loaded{i}") for i in range(2)]
        h_hi_done = sem("h_hi_done4")
        h_ready = sem("h_ready4")
        x1_loaded = [sem(f"x1_loaded{i}") for i in range(2)]
        gate_ready = sem("gate_ready")
        up_ready = sem("up_ready")
        silu_done = sem("silu_done")
        prod_done = sem("prod_done")
        a_hi_done = sem("a_hi_done")
        a_ready = sem("a_ready")
        down_ready = sem("down_ready")
        down_added = sem("down_added")
        squares_done = sem("squares_done4")
        var_ready = sem("var_ready4")
        std_ready = sem("std_ready4")
        rstd_chain = sem("rstd_chain4")
        out_ready = sem("out_ready")
        out_stored = [sem(f"out_stored{i}") for i in range(2)]

        block = ctx.enter_context(nc.Block())

        def run(eng, body, tail):
            body(0, 0, 0, "first")
            with eng.Fori(0, NB - 1) as b:
                with eng.Fori(1, NP - 1) as i:
                    body(b * NP + i, b, i, "inner")
                body(b * NP + (NP - 1), b, NP - 1, "last")
                body(b * NP + NP, b + 1, 0, "first")
            with eng.Fori(1, NP - 1) as i:
                body(i + (NB - 1) * NP, NB - 1, i, "inner")
            body(NB * NP - 1, NB - 1, NP - 1, "last")
            tail()

        def fixed(q, value):
            return isinstance(q, int) and q == value

        @block.sync
        def _(sp):
            def load_weights(q, i, ks):
                for k in ks:
                    first = fixed(q, 0) and k < 3
                    if not first:
                        sp.wait_ge(w_ready, q * 6 + (k - 2))
                    if k >= 6:
                        f = 0 if fixed(i, NP - 1) else i * 2 + 2
                    else:
                        f = i * 2 + (0, 0, 1, 1, 0, 1)[k]
                    if k % 6 < 4:
                        src = (w_gate, w_up)[k % 2][bass.ds(f, 1), :, :].rearrange("a p n -> p (a n)")
                    else:
                        src = w_down[bass.ds(f * P, P), :]
                    sp.dma_start(raw[:, k % 3, :], src).then_inc(raw_loaded[k % 3], DMA)

            def load_h(b, half):
                for d in range(KT):
                    if not (fixed(b, 0) and half == 0 and d < 2):
                        sp.wait_ge(h_ready, b * (2 * KT) + (half * KT + d - 1))
                    sp.dma_start(h_raw[:, d % 2, :],
                                 h2_scr[d, :, bass.ds(b * TB + half * HALF, HALF)]).then_inc(h_loaded[d % 2], DMA)

            def load_x1(b, half):
                if not fixed(b, 0):
                    sp.wait_ge(out_stored[half], b * (ST * DMA))
                sp.dma_start(acc[:, half * ST:(half + 1) * ST, :],
                             x1_scr[bass.ds(b * TB + half * HALF, HALF), :].rearrange("(t p) n -> p t n", p=P)).then_inc(x1_loaded[half], DMA)

            def body(q, b, i, place):
                final = place == "last" and isinstance(b, int)
                if place == "inner":
                    load_weights(q, i, (2, 3, 4, 5, 6, 7))
                elif place == "first":
                    load_weights(q, i, (2, 3, 4))
                    load_h(b, 1)
                    load_x1(b, 0)
                    load_weights(q, i, (5, 6, 7))
                    load_x1(b, 1)
                else:
                    load_weights(q, i, (2, 3, 4, 5))
                    if not final:
                        load_h(b + 1, 0)
                        load_weights(q, i, (6, 7))

            sp.dma_start(gain2[:, :], g2).then_inc(gain_loaded, DMA)
            load_weights(0, 0, (0, 1))
            load_h(0, 0)
            sp.dma_start(gain_f[:, :], gf.partition_broadcast(P)).then_inc(gain_f_loaded, DMA)
            run(sp, body, lambda: None)

        @block.scalar
        def _(act):
            def round_w(q, ks):
                for k in ks:
                    if k in (2, 3) and not fixed(q, 0):
                        act.wait_ge(up_ready, q * 4)
                    if k in (4, 5) and not fixed(q, 0):
                        act.wait_ge(down_ready, q * 16)
                    if k in (6, 7):
                        act.wait_ge(up_ready, q * 4 + 3)
                    act.wait_ge(raw_loaded[k % 3], (q * 2 + (k // 3 + 1)) * DMA)
                    act.activation(w_hi[:, k % 6, :], raw[:, k % 3, :], ACT.Copy).then_inc(w_hi_done, 1)

            def round_h(b, half):
                if not fixed(b, 0):
                    act.wait_ge(up_ready, b * (4 * NP) + (2 * half - 2))
                for d in range(KT):
                    act.wait_ge(h_loaded[d % 2], (b * KT + (half * KT + d) // 2 + 1) * DMA)
                    act.activation(h_hi[:, half, d, :], h_raw[:, d % 2, :], ACT.Identity,
                                   scale=gain2[:, d:d + 1]).then_inc(h_hi_done, 1)

            def gate(q, m):
                act.wait_ge(gate_ready, q * 4 + (m + 1))
                if not (fixed(q, 0) and m < 2):
                    act.wait_ge(prod_done, q * 4 + (m - 1))
                act.activation(silu[:, m % 2, :], gate_ps[m % 2][:, :], ACT.Silu).then_inc(silu_done, 1)

            def round_a(q, m):
                act.wait_ge(prod_done, q * 4 + (m + 1))
                act.activation(a_hi[:, m, :], prod[:, m % 2, :], ACT.Copy).then_inc(a_hi_done, 1)

            def last_norm(b, half):
                nth = b * 2 + half
                act.wait_ge(down_added, down_done(b, half))
                for t in range(ST):
                    one = half * ST + t
                    if t:
                        act.wait_ge(squares_done, nth * ST + t)
                    act.activation(junk[:, :], acc[:, one, :], ACT.Square,
                                   accum_out=sumsq[:, one:one + 1]).then_inc(squares_done, 1)
                act.wait_ge(var_ready, nth + 1)
                act.activation(std[:, half * ST:(half + 1) * ST], var[:, half * ST:(half + 1) * ST], ACT.Sqrt).then_inc(std_ready, 1)

            def down_done(b, half):
                return b * (16 * NP) + (16 * NP - 8 + 8 * half)

            def body(q, b, i, place):
                first, last = place == "first", place == "last"
                final = last and isinstance(b, int)
                if fixed(q, 0):
                    round_w(q, (0, 1))
                    act.wait_ge(gain_loaded, DMA)
                    round_h(b, 0)
                round_w(q, (2, 3))
                gate(q, 0)
                round_a(q, 0)
                if first and not fixed(q, 0):
                    last_norm(b - 1, 1)
                if first:
                    round_h(b, 1)
                round_w(q, (4, 5))
                gate(q, 1)
                round_a(q, 1)
                if last and not final:
                    round_h(b + 1, 0)
                gate(q, 2)
                round_a(q, 2)
                if not final:
                    round_w(q, (6, 7))
                gate(q, 3)
                round_a(q, 3)
                if last:
                    last_norm(b, 0)

            run(act, body, lambda: last_norm(NB - 1, 1))

        @block.vector
        def _(dve):
            def rest_of_w(q, ks):
                for k in ks:
                    dve.wait_ge(w_hi_done, q * 6 + (k + 1))
                    dve.tensor_tensor(w_lo[:, k % 6, :], raw[:, k % 3, :], w_hi[:, k % 6, :].bitcast(F32),
                                      ALU.subtract).then_inc(w_ready, 1)

            def rest_of_h(b, half):
                for d in range(KT):
                    dve.wait_ge(h_hi_done, b * (2 * KT) + (half * KT + d + 1))
                    dve.scalar_tensor_tensor(out=h_lo[:, half, d, :], in0=h_raw[:, d % 2, :], scalar=gain2[:, d:d + 1],
                                             in1=h_hi[:, half, d, :].bitcast(F32), op0=ALU.mult,
                                             op1=ALU.subtract).then_inc(h_ready, 1)

            def product(q, m):
                dve.wait_ge(silu_done, q * 4 + (m + 1))
                dve.wait_ge(up_ready, q * 4 + (m + 1))
                dve.tensor_tensor(prod[:, m % 2, :], up_ps[m % 2][:, :], silu[:, m % 2, :], ALU.mult).then_inc(prod_done, 1)
                dve.wait_ge(a_hi_done, q * 4 + (m + 1))
                dve.tensor_tensor(a_lo[:, m, :], prod[:, m % 2, :], a_hi[:, m, :].bitcast(F32),
                                  ALU.subtract).then_inc(a_ready, 1)

            def add(q, half, loaded=None):
                if loaded is not None:
                    dve.wait_ge(x1_loaded[half], loaded)
                for t in range(ST):
                    for c in range(2):
                        g = 2 * t + c
                        dve.wait_ge(down_ready, q * 16 + (half * 8 + g + 1))
                        dst = acc[:, half * ST + t, c * HALF:(c + 1) * HALF]
                        dve.tensor_tensor(dst, down_ps[g % 4][:, :], dst, ALU.add).then_inc(down_added, 1)

            def last_norm_var(b, half):
                these = slice(half * ST, (half + 1) * ST)
                nth = b * 2 + half
                dve.wait_ge(squares_done, nth * ST + ST)
                dve.tensor_scalar(var[:, these], sumsq[:, these], 1.0 / D, EPS, ALU.mult, ALU.add).then_inc(var_ready, 1)
                dve.wait_ge(std_ready, nth + 1)
                refined_rstd(dve, rstd_chain, nth * 4, std[:, these], var[:, these], tmp[:, these], rstd[:, these])
                for t in range(ST):
                    one = half * ST + t
                    dve.scalar_tensor_tensor(out=acc[:, one, :], in0=acc[:, one, :], scalar=rstd[:, one:one + 1],
                                             in1=gain_f[:, :], op0=ALU.mult, op1=ALU.mult).then_inc(out_ready, 1)

            def body(q, b, i, place):
                first, last = place == "first", place == "last"
                final = last and isinstance(b, int)
                loaded = (b + 1) * DMA if first else None
                if fixed(q, 0):
                    rest_of_w(q, (0, 1))
                    dve.wait_ge(gain_loaded, DMA)
                    rest_of_h(b, 0)
                    dve.wait_ge(gain_f_loaded, DMA)
                rest_of_w(q, (2, 3))
                product(q, 0)
                if not fixed(q, 0):
                    add(q - 1, 1)
                if first and not fixed(q, 0):
                    last_norm_var(b - 1, 1)
                if first:
                    rest_of_h(b, 1)
                rest_of_w(q, (4, 5))
                product(q, 1)
                if last and not final:
                    rest_of_h(b + 1, 0)
                product(q, 2)
                if not final:
                    rest_of_w(q, (6, 7))
                add(q, 0, loaded)
                product(q, 3)
                if first:
                    dve.wait_ge(x1_loaded[1], loaded)
                if last:
                    last_norm_var(b, 0)

            def tail():
                add(NB * NP - 1, 1)
                last_norm_var(NB - 1, 1)

            run(dve, body, tail)

        @block.tensor
        def _(pe):
            def up(q, m, b, first):
                tile, half = m % 2, m // 2
                if not (fixed(q, 0) and m < 2):
                    pe.wait_ge(prod_done, q * 4 + (m - 1))
                for part, ps in ((0, gate_ps), (1, up_ps)):
                    k = 2 * tile + part
                    if half == 0:
                        pe.wait_ge(w_ready, q * 6 + (k + 1))
                    for d in range(KT):
                        if first and tile == 0 and part == 0:
                            pe.wait_ge(h_ready, b * (2 * KT) + (half * KT + d + 1))
                        mm = three_products(pe, ps[m % 2][:, :], w_hi[:, k, d * P:(d + 1) * P], w_lo[:, k, d * P:(d + 1) * P],
                                            h_hi[:, half, d, :], h_lo[:, half, d, :], d == 0, d == KT - 1)
                    mm.then_inc((gate_ready, up_ready)[part], 1)

            def down(q, half):
                pe.wait_ge(a_ready, q * 4 + (2 * half + 2))
                if half == 0:
                    pe.wait_ge(w_ready, q * 6 + 6)
                for t in range(ST):
                    for c in range(2):
                        g = 2 * t + c
                        if not (fixed(q, 0) and half == 0 and g < 4):
                            pe.wait_ge(down_added, q * 16 + (half * 8 + g - 3))
                        for f in range(2):
                            m = 2 * half + f
                            mm = three_products(pe, down_ps[g % 4][:, :], a_hi[:, m, t * P:(t + 1) * P], a_lo[:, m, t * P:(t + 1) * P],
                                                w_hi[:, 4 + f, c * HALF:(c + 1) * HALF], w_lo[:, 4 + f, c * HALF:(c + 1) * HALF],
                                                f == 0, f == 1)
                        mm.then_inc(down_ready, 1)

            def body(q, b, i, place):
                first = place == "first"
                up(q, 0, b, first)
                if not fixed(q, 0):
                    down(q - 1, 1)
                up(q, 1, b, first)
                up(q, 2, b, first)
                down(q, 0)
                up(q, 3, b, first)

            run(pe, body, lambda: down(NB * NP - 1, 1))

        @block.gpsimd
        def _(pool):
            def store(b, half):
                for t in range(ST):
                    pool.wait_ge(out_ready, b * (2 * ST) + (half * ST + t + 1))
                    pool.dma_start(out[bass.ds(b * TB + (half * ST + t) * P, P), :],
                                   acc[:, half * ST + t, :]).then_inc(out_stored[half], DMA)

            with pool.Fori(0, NB) as b:
                for half in range(2):
                    store(b, half)
            for half in range(2):
                pool.wait_ge(out_stored[half], NB * ST * DMA)


def encoder(nc, x, w_in, w_fourier, w_pool, w_out, w_gate, w_up, w_down, g1, g2, gf, pool_gain,
            table, channel, edge, ident, out):
    def scratch(name, shape):
        return nc.dram_tensor(name, shape, F32, kind="Internal").ap()

    z_scr = scratch("z_scr", (KT, P, TOKENS))
    y_scr = scratch("y_scr", (KT, P, TOKENS))
    x1_scr = scratch("x1_scr", (TOKENS, D))
    h2_scr = scratch("h2_scr", (KT, P, TOKENS))
    project_in(nc, x, w_in, g1, ident, z_scr)
    mix(nc, z_scr, y_scr, table, channel, w_fourier, w_pool, pool_gain, edge)
    project_out(nc, y_scr, x, w_out, ident, x1_scr, h2_scr)
    ffn(nc, x1_scr, h2_scr, w_gate, w_up, w_down, g2, gf, out)


def kernel(x_prompt, x_sample, norm1_g, w_in, w_fourier, w_pool, pool_scale, w_out, norm2_g, w_gate, w_up, w_down, normf_g):
    import concourse.bacc as bacc
    from concourse.bass_utils import run_bass_kernel_spmd

    def a(v):
        return np.ascontiguousarray(np.asarray(v))

    def by_partition(g):
        return a(a(g).reshape(-1, P).T)

    def hidden_tiles(w):
        return a(a(w).reshape(KT, P, FT, P).transpose(2, 1, 0, 3).reshape(FT, P, KT * P))

    table, channel = fourier_tables()
    arrays = {
        "x": a(np.concatenate([a(x_prompt)[0], a(x_sample)[0]], axis=0)),
        "w_in": a(w_in)[0],
        "w_fourier": a(w_fourier)[0],
        "w_pool": a(w_pool)[0],
        "w_out": a(w_out)[0],
        "w_gate": hidden_tiles(a(w_gate)[0]),
        "w_up": hidden_tiles(a(w_up)[0]),
        "w_down": a(w_down)[0],
        "g1": by_partition(a(norm1_g)[0]),
        "g2": by_partition(a(norm2_g)[0]),
        "gf": a(normf_g),
        "pool_gain": by_partition(a(pool_scale)[0]),
        "table": table,
        "channel": channel,
        "edge": edge_counts(),
        "ident": np.eye(P, dtype=np.float32),
    }
    arrays = {f"in_{k}": a(v) for k, v in arrays.items()}
    nc = bacc.Bacc("TRN2", target_bir_lowering=False, num_devices=1)
    args = [nc.dram_tensor(k, v.shape, mybir.dt.from_np(v.dtype), kind="ExternalInput").ap() for k, v in arrays.items()]
    out = nc.dram_tensor("out", (TOKENS, D), F32, kind="ExternalOutput").ap()
    encoder(nc, *args, out)
    r = run_bass_kernel_spmd(nc, [arrays], core_ids=[0])
    y = r.results[0]["out"]
    return y[:SEQS[0]][None], y[SEQS[0]:][None]
```

```python
from contextlib import ExitStack

import numpy as np

import concourse.bass as bass
from concourse import mybir

F32 = mybir.dt.float32
F32R = mybir.dt.float32r
ALU = mybir.AluOpType
ACT = mybir.ActivationFunctionType

P = 128
D = 1024
KT = D // P
SEQS = (2048, 1024)
TOKENS = sum(SEQS)
HALF = 512
EPS = 1e-6
HEADS = 4
WINDOWS = (2, 4, 8, 16)
PAD = max(WINDOWS) // 2
BASE = 256
D_FF = 2816
FT = D_FF // P
DMA = 16


def levels(S):
    out = []
    while S > BASE:
        out.append(S)
        S //= 2
    return out


def table_places():
    at, places = 0, {}
    for M in levels(max(SEQS)):
        for part in ("cos", "sin"):
            places[M, part] = at
            at += (M // 4 // P) * (M // 4)
    for part in ("cos", "sin"):
        places[BASE, part] = at
        at += (BASE // P) * BASE
    return places, at


def fourier_tables():
    places, width = table_places()
    table = np.zeros((P, width))

    def put(key, rows_by_cols):
        rows, cols = rows_by_cols.shape
        for t in range(rows // P):
            table[:, places[key] + t * cols:places[key] + (t + 1) * cols] = rows_by_cols[t * P:(t + 1) * P]

    for M in levels(max(SEQS)):
        odd = 2 * np.arange(M // 4) + 1
        put((M, "cos"), np.cos(2 * np.pi / M * (np.outer(np.arange(M // 4), odd) % M)))
        sin = np.sin(2 * np.pi / M * (np.outer(np.arange(M // 4) + 1, odd) % M))
        sin[-1] *= 0.5
        put((M, "sin"), sin)
    angle = 2 * np.pi / BASE * (np.outer(np.arange(BASE), np.arange(BASE)) % BASE)
    put((BASE, "cos"), np.cos(angle))
    put((BASE, "sin"), -np.sin(angle))
    angle = 2 * np.pi / P * (np.outer(np.arange(P), np.arange(P)) % P)
    channel = np.concatenate([np.cos(angle), np.sin(angle)], axis=1) / np.sqrt(P)
    return table.astype(np.float32), channel.astype(np.float32)


def edge_counts():
    out = []
    for k in WINDOWS:
        out += [1.0 / (t + k // 2) for t in range(k // 2)]
        out += [1.0 / (k - t) for t in range(k // 2)]
    out += [1.0 / k for k in WINDOWS]
    return np.tile(np.array(out, np.float32), (P, 1))


def low_over_raw(nc, ctx, name, shape):
    at = -(-nc.sbuf_base // 32) * 32
    lo = ctx.enter_context(nc.sbuf_tensor(f"{name}_lo", shape, F32R))
    return lo, nc.alloc_sbuf_tensor_at(f"{name}_raw", shape, F32, offset=at)


class Ahead:

    def __init__(self, nc, ctx):
        self.nc = nc
        self.bottom = -(-nc.sbuf_base // 32) * 32
        TW = table_places()[1]
        above = self.bottom + 4 * TW

        def sb(name, shape, dt, offset):
            return nc.alloc_sbuf_tensor_at(name, shape, dt, offset=offset)

        def sem(name):
            return ctx.enter_context(nc.semaphore(name))

        self.tables_bytes = 4 * TW
        self.tab_lo = sb("tab_lo", [P, TW], F32R, self.bottom)
        self.tab_raw = sb("tab_raw", [P, TW], F32, self.bottom)
        self.y_raw = sb("y_raw", [P, KT, HALF], F32, self.bottom)
        self.zy = sb("zy", [P, HEADS * SEQS[0]], F32, above)
        self.w_out_lo = sb("wout_lo", [P, KT, D], F32R, above)
        self.w_out_raw = sb("wout_raw", [P, KT, D], F32, above)
        self.tab_loaded = sem("tab_loaded")
        self.z_loaded = sem("zh_loaded0")
        self.w_out_loaded = [sem(f"wout_loaded{i}") for i in range(KT)]
        self.y_loaded = sem("y_loaded")
        at = nc.sbuf_usable_end // 32 * 32
        sizes = {"h": 4 * KT * HALF, "w": 4 * D, "gain": 4 * KT}
        self.top_bytes = sizes["h"] + 3 * sizes["w"] + sizes["gain"]
        self.top = at - self.top_bytes
        at -= sizes["h"]
        self.h2_lo = sb("h2_lo_ahead", [P, KT, HALF], F32R, at)
        self.h2_raw = sb("h2_raw_ahead", [P, KT, HALF], F32, at)
        self.w_raw = []
        for i in range(3):
            at -= sizes["w"]
            self.w_raw.append(sb(f"w_raw{i}", [P, D], F32, at))
        self.gain2 = sb("gain2", [P, KT], F32, self.top)
        self.h2_loaded = sem("h2_loaded0")
        self.w_loaded = [sem(f"raw_loaded{i}") for i in range(3)]
        self.gain2_loaded = sem("gain2_loaded")

    def reserve_top(self, ctx, stage):
        guard = self.nc.sbuf_tensor(f"ahead_top_{stage}", [P, self.top_bytes // 4], F32, side="right")
        ctx.enter_context(guard)
        assert self.nc.sbuf_top <= self.top

    def reserve(self, ctx, stage, above_tables):
        at = -(-self.nc.sbuf_base // 32) * 32
        assert at == self.bottom
        ctx.enter_context(self.nc.sbuf_tensor(f"ahead_{stage}", [P, (self.tables_bytes + above_tables) // 4], F32))


def three_products(pe, out, w_hi, w_lo, m_hi, m_lo, first, last):
    pe.matmul(out, w_hi, m_hi, start=first, stop=False)
    pe.matmul(out, w_hi, m_lo, start=False, stop=False)
    return pe.matmul(out, w_lo, m_hi, start=False, stop=last)


def refined_rstd(dve, chain, done, std, var, tmp, rstd):
    dve.reciprocal(tmp, std).then_inc(chain, 1)
    dve.wait_ge(chain, done + 1)
    dve.scalar_tensor_tensor(out=rstd, in0=tmp, scalar=-0.5, in1=tmp, op0=ALU.mult, op1=ALU.mult).then_inc(chain, 1)
    dve.wait_ge(chain, done + 2)
    dve.tensor_tensor(rstd, rstd, var, ALU.mult).then_inc(chain, 1)
    dve.wait_ge(chain, done + 3)
    dve.scalar_tensor_tensor(out=rstd, in0=rstd, scalar=1.5, in1=tmp, op0=ALU.add, op1=ALU.mult).then_inc(chain, 1)
    dve.wait_ge(chain, done + 4)


def project_in(nc, ahead, x, w_in, g1, ident, z_scr, table):
    NJ = TOKENS // HALF
    with ExitStack() as ctx:
        ahead.reserve(ctx, "project_in", 4 * SEQS[0])
        def sb(name, shape, dt=F32):
            return ctx.enter_context(nc.sbuf_tensor(name, shape, dt))

        def sem(name):
            return ctx.enter_context(nc.semaphore(name))

        w_hi = sb("win_hi", [P, KT, D], F32R)
        w_lo, w_raw = low_over_raw(nc, ctx, "win", [P, KT, D])
        xin = sb("xin", [P, 2, 4, D])
        h_hi = sb("h_hi", [P, 2, KT, HALF], F32R)
        h_lo = sb("h_lo", [P, 2, KT, HALF], F32R)
        z_out = sb("z_out", [P, 4, HALF])
        junk = sb("junk1", [P, D])
        eye = sb("eye1", [P, P])
        gain = sb("gain1", [P, KT])
        sumsq = sb("sumsq1", [P, 2, 4])
        var = sb("var1", [P, 2, 4])
        std = sb("std1", [P, 2, 4])
        tmp = sb("tmp1", [P, 2, 4])
        rstd = sb("rstd1", [P, 2, 4])
        z_ps = [ctx.enter_context(nc.psum_tensor(f"z_ps{i}", [P, HALF], F32)) for i in range(4)]
        t_ps = [ctx.enter_context(nc.psum_tensor(f"t_ps{i}", [P, HALF], F32)) for i in range(4)]

        const_loaded = sem("const_loaded1")
        w_loaded = [sem(f"win_loaded{i}") for i in range(KT)]
        x_first = [sem(f"x_first{i}") for i in range(4)]
        x_loaded = [sem(f"x_loaded{i}") for i in range(2)]
        w_hi_done = sem("win_hi_done")
        w_ready = sem("win_ready")
        squares_done = sem("squares_done1")
        var_ready = sem("var_ready1")
        std_ready = sem("std_ready1")
        rstd_chain = sem("rstd_chain1")
        xn_ready = sem("xn_ready1")
        transposed = sem("transposed1")
        h_hi_done = sem("h_hi_done1")
        h_ready = sem("h_ready1")
        z_ready = sem("z_ready")
        z_staged = sem("z_staged")
        z_stored = [sem(f"z_stored{i}") for i in range(4)]

        block = ctx.enter_context(nc.Block())

        @block.sync
        def _(sp):
            def load_x(j, slot):
                sp.dma_start(xin[:, slot, :, :],
                             x[bass.ds(j * HALF, HALF), :].rearrange("(t p) d -> p t d", p=P)).then_inc(x_loaded[slot], DMA)

            for t in range(4):
                sp.dma_start(xin[:, 0, t, :], x[t * P:(t + 1) * P, :]).then_inc(x_first[t], DMA)
            sp.dma_start(eye[:, :], ident).then_inc(const_loaded, DMA)
            sp.dma_start(gain[:, :], g1).then_inc(const_loaded, DMA)
            for d in range(KT):
                sp.dma_start(w_raw[:, d, :], w_in[d * P:(d + 1) * P, :]).then_inc(w_loaded[d], DMA)
            load_x(1, 1)
            with sp.Fori(0, (NJ - 2) // 2) as it:
                for slot in range(2):
                    j = it * 2 + 2 + slot
                    sp.wait_ge(transposed, (j - 1) * KT)
                    load_x(j, slot)
            sp.dma_start(ahead.tab_raw[:, :], table).then_inc(ahead.tab_loaded, DMA)
            for s in range(4):
                sp.wait_ge(z_stored[s], 2 * (SEQS[0] // HALF) * DMA)
            sp.dma_start(ahead.zy[:, 0:SEQS[0]], z_scr[0, :, 0:SEQS[0]]).then_inc(ahead.z_loaded, DMA)

        @block.scalar
        def _(act):
            def squares(j, n, slot):
                first = isinstance(j, int) and j == 0
                if not first:
                    act.wait_ge(x_loaded[slot], n * DMA)
                for t in range(4):
                    if first:
                        act.wait_ge(x_first[t], DMA)
                    if t:
                        act.wait_ge(squares_done, j * 4 + t)
                    act.activation(junk[:, :], xin[:, slot, t, :], ACT.Square,
                                   accum_out=sumsq[:, slot, t:t + 1]).then_inc(squares_done, 1)
                act.wait_ge(var_ready, j + 1)
                act.activation(std[:, slot, :], var[:, slot, :], ACT.Sqrt).then_inc(std_ready, 1)

            def round_h(j, slot, d):
                act.wait_ge(transposed, j * KT + d + 1)
                act.activation(h_hi[:, slot, d, :], t_ps[d % 4][:, :], ACT.Identity,
                               scale=gain[:, d:d + 1]).then_inc(h_hi_done, 1)

            def stage_z(j, c, first=False):
                act.wait_ge(z_ready, j * KT + c + 1)
                if not (first and c < 4):
                    act.wait_ge(z_stored[c % 4], (j * 2 + c // 4) * DMA)
                act.activation(z_out[:, c % 4, :], z_ps[c % 4][:, :], ACT.Copy).then_inc(z_staged, 1)

            def step(j, n_next, slot, first=False):
                squares(j + 1, n_next, 1 - slot)
                before = 5 if first else 3
                for c in range(before):
                    stage_z(j, c, first)
                for k in range(max(KT - before, 4)):
                    for d in range(2 * k, min(2 * k + 2, KT)):
                        round_h(j + 1, 1 - slot, d)
                    if before + k < KT:
                        stage_z(j, before + k, first)

            squares(0, 0, 0)
            for d in range(KT):
                act.wait_ge(w_loaded[d], DMA)
                act.activation(w_hi[:, d, :], w_raw[:, d, :], ACT.Copy).then_inc(w_hi_done, 1)
                if d == 0:
                    act.wait_ge(const_loaded, 2 * DMA)
                round_h(0, 0, d)
            step(0, 1, 0, first=True)
            with act.Fori(0, (NJ - 2) // 2) as it:
                step(it * 2 + 1, it + 1, 1)
                step(it * 2 + 2, it + 2, 0)
            for c in range(KT):
                stage_z(NJ - 1, c)

        @block.vector
        def _(dve):
            def norm(j, slot):
                dve.wait_ge(squares_done, j * 4 + 4)
                dve.tensor_scalar(var[:, slot, :], sumsq[:, slot, :], 1.0 / D, EPS, ALU.mult, ALU.add).then_inc(var_ready, 1)
                dve.wait_ge(std_ready, j + 1)
                refined_rstd(dve, rstd_chain, j * 4, std[:, slot, :], var[:, slot, :], tmp[:, slot, :], rstd[:, slot, :])
                for t in range(4):
                    dve.tensor_scalar(xin[:, slot, t, :], xin[:, slot, t, :], rstd[:, slot, t:t + 1], None,
                                      ALU.mult).then_inc(xn_ready, 1)

            def rest_of_h(j, slot, d):
                dve.wait_ge(h_hi_done, j * KT + d + 1)
                dve.scalar_tensor_tensor(out=h_lo[:, slot, d, :], in0=t_ps[d % 4][:, :], scalar=gain[:, d:d + 1],
                                         in1=h_hi[:, slot, d, :].bitcast(F32), op0=ALU.mult,
                                         op1=ALU.subtract).then_inc(h_ready, 1)

            def step(j, slot):
                norm(j + 1, 1 - slot)
                for d in range(KT):
                    rest_of_h(j + 1, 1 - slot, d)

            norm(0, 0)
            dve.wait_ge(const_loaded, 2 * DMA)
            for d in range(KT):
                dve.wait_ge(w_hi_done, d + 1)
                dve.tensor_tensor(w_lo[:, d, :], w_raw[:, d, :], w_hi[:, d, :].bitcast(F32),
                                  ALU.subtract).then_inc(w_ready, 1)
                rest_of_h(0, 0, d)
            step(0, 0)
            with dve.Fori(0, (NJ - 2) // 2) as it:
                step(it * 2 + 1, 1)
                step(it * 2 + 2, 0)

        @block.tensor
        def _(pe):
            def transposes(j, slot, d, first=False):
                if d == 0:
                    pe.wait_ge(xn_ready, j * 4 + 4)
                if not (first and d < 4):
                    pe.wait_ge(h_ready, j * KT + d - 3)
                for t in range(4):
                    mm = pe.transpose(t_ps[d % 4][:, t * P:(t + 1) * P], xin[:, slot, t, d * P:(d + 1) * P], eye[:, :])
                mm.then_inc(transposed, 1)

            def product(slot, c, d):
                return three_products(pe, z_ps[c % 4][:, :], w_hi[:, d, c * P:(c + 1) * P], w_lo[:, d, c * P:(c + 1) * P],
                                      h_hi[:, slot, d, :], h_lo[:, slot, d, :], d == 0, d == KT - 1)

            def products(j, slot, c):
                pe.wait_ge(z_staged, j * KT + c - 3)
                for d in range(KT):
                    if c == 0:
                        pe.wait_ge(h_ready, j * KT + d + 1)
                    mm = product(slot, c, d)
                mm.then_inc(z_ready, 1)

            def step(j, slot, begin=0):
                before = 4 if begin else 2
                for c in range(begin, max(KT, before + 4)):
                    if c < KT:
                        products(j, slot, c)
                    if 0 <= c - before < 4:
                        transposes(j + 1, 1 - slot, 2 * (c - before))
                        transposes(j + 1, 1 - slot, 2 * (c - before) + 1)

            pe.wait_ge(const_loaded, 2 * DMA)
            for d in range(2):
                transposes(0, 0, d, first=True)
            for d in range(KT):
                if d + 2 < KT:
                    transposes(0, 0, d + 2, first=True)
                pe.wait_ge(h_ready, d + 1)
                pe.wait_ge(w_ready, d + 1)
                for c in range(4):
                    mm = product(0, c, d)
                    if d == KT - 1:
                        mm.then_inc(z_ready, 1)
            step(0, 0, begin=4)
            with pe.Fori(0, (NJ - 2) // 2) as it:
                step(it * 2 + 1, 1)
                step(it * 2 + 2, 0)
            for c in range(KT):
                products(NJ - 1, (NJ - 1) % 2, c)

        @block.gpsimd
        def _(pool):
            with pool.Fori(0, NJ) as j:
                for c in range(KT):
                    pool.wait_ge(z_staged, j * KT + c + 1)
                    pool.dma_start(z_scr[c, :, bass.ds(j * HALF, HALF)], z_out[:, c % 4, :]).then_inc(z_stored[c % 4], DMA)
            for s in range(4):
                pool.wait_ge(z_stored[s], 2 * NJ * DMA)


def mix(nc, ahead, w_out, z_scr, y_scr, channel, w_fourier, w_pool, pool_gain, edge):
    places, TW = table_places()
    top = levels(max(SEQS))
    SMAX = max(SEQS)
    NCOL = 4

    def plan(S):
        lv = levels(S)
        fold_at, at = {}, 0
        for M in lv:
            for part in ("cos", "sin"):
                fold_at[M, part] = at
                at += M // 4 // P
        fold_at[BASE] = at
        n_fold = at + BASE // P
        tiles, need = [], []
        for i, M in enumerate(lv):
            for k, part in enumerate(("cos", "sin")):
                for t in range(M // 4 // P):
                    tiles.append((fold_at[M, part] + t, part))
                    need.append(2 * i + k + 1)
        for part in ("cos", "sin"):
            for t in range(BASE // P):
                tiles.append((fold_at[BASE] + t, part))
                need.append(2 * len(lv) + 1)
        tile_at = {}
        for i, (f, part) in enumerate(tiles):
            M = next((M for M in lv if fold_at[M, part] <= f < fold_at[M, part] + M // 4 // P), BASE)
            tile_at.setdefault((M, part), i)
        groups = [list(range(a, min(a + NCOL, len(tiles)))) for a in range(0, len(tiles), NCOL)]
        return {
            "levels": lv, "fold_at": fold_at, "n_fold": n_fold, "tiles": tiles, "groups": groups, "tile_at": tile_at,
            "need": [max(need[t] for t in g) for g in groups],
            "early": 2 * (S // 4 // P) // NCOL,
            "stages": len(lv) + 1,
            "folds": 2 * len(lv) + 1,
            "chain": 2 * len(lv) - 1,
        }

    plans = [plan(S) for S in SEQS]
    UV = max(len(p["tiles"]) for p in plans)
    NF = max(p["n_fold"] for p in plans)
    CREDIT = 4
    ch0 = [0, HEADS * len(plans[0]["groups"])]
    fold0 = [0, HEADS * plans[0]["folds"]]
    chain0 = [0, HEADS * plans[0]["chain"]]
    stage0 = [CREDIT, CREDIT + HEADS * plans[0]["stages"]]
    tok0 = [0, SEQS[0]]
    chunk0 = [0, HEADS * SEQS[0] // HALF]
    edge_at = [sum(WINDOWS[:g]) for g in range(4)]
    inverse_at = sum(WINDOWS)
    ORDER = (3, 2, 1, 0)
    DVE_GROUP = 1
    pool_groups = [g for g in ORDER if g != DVE_GROUP]
    RAW = TW // 4

    with ExitStack() as ctx:
        def sb(name, shape, dt=F32):
            return ctx.enter_context(nc.sbuf_tensor(name, shape, dt))

        def sem(name):
            return ctx.enter_context(nc.semaphore(name))

        ahead.reserve(ctx, "mix", 4 * HEADS * SMAX)
        tab_lo, tab_raw, tab_loaded = ahead.tab_lo, ahead.tab_raw, ahead.tab_loaded
        tab_hi = sb("tab_hi", [P, TW], F32R)
        zys = [ahead.zy, sb("zy1", [P, HEADS * SEQS[1]])]
        folds = sb("folds", [P, NF, P])
        scratch = sb("scratch", [P, SMAX - BASE + SMAX // 2 + 1])
        sums, diff = scratch[:, :SMAX - BASE], scratch[:, SMAX - BASE:]
        uv_hi = sb("uv_hi", [P, UV, P], F32R)
        uv_lo = sb("uv_lo", [P, UV, P], F32R)
        sine_part = sb("sine_part", [P, 2, SMAX // 4])
        chan = sb("chan", [P, 2, P])
        wf = sb("wf", [P, HEADS, P])
        chan_w = sb("chan_w", [P, 2, HEADS, P])
        wp = sb("wp", [P, 4, P])
        pg = sb("pg", [P, 4])
        edges = sb("edges", [P, sum(WINDOWS) + 4])
        edge_sums = sb("edge_sums", [P, WINDOWS[DVE_GROUP]])
        zb = sb("zb", [P, 4, PAD + SMAX + PAD])
        win = [sb(f"win{i}", [P, PAD + SMAX + PAD]) for i in range(2)]
        yb = sb("yb", [P, 4, HALF])
        ch_ps = [ctx.enter_context(nc.psum_tensor(f"ch_ps{i}", [P, NCOL, P], F32)) for i in range(2)]
        cos_ps = [ctx.enter_context(nc.psum_tensor(f"cos_ps{i}", [P, SMAX // 4], F32)) for i in range(2)]
        sin_ps = [ctx.enter_context(nc.psum_tensor(f"sin_ps{i}", [P, SMAX // 4], F32)) for i in range(2)]
        base_ps = ctx.enter_context(nc.psum_tensor("base_ps", [P, BASE], F32))

        chan_loaded = sem("chan_loaded")
        pool_w_loaded = sem("pool_w_loaded")
        tab_hi_done = sem("tab_hi_done")
        tab_ready = sem("tab_ready")
        chan_w_ps_ready = sem("chan_w_ps_ready")
        chan_w_ready = sem("chan_w_ready")
        z_loaded = [ahead.z_loaded] + [sem(f"zh_loaded{i}") for i in range(1, 2 * HEADS)]
        zb_loaded = [sem(f"zb_loaded{i}") for i in range(4)]
        zeroed = sem("zeroed")
        fold_chain = sem("fold_chain")
        fold_done = sem("fold_done")
        ch_ready = sem("ch_ready")
        uv_hi_done = sem("uv_hi_done")
        uv_ready = sem("uv_ready")
        cos_sin_ready = sem("cos_sin_ready")
        sine_copied = sem("sine_copied")
        stage_done = sem("stage_done")
        y_stored = [sem(f"y_stored{i}") for i in range(2)]
        pool_chain = sem("pool_chain")
        pooled = sem("pooled")
        d_by_pool = sem("d_by_pool")
        yb_ready = sem("yb_ready")
        yb_staged = sem("yb_staged")
        yb_stored = [sem(f"yb_stored{i}") for i in range(4)]

        block = ctx.enter_context(nc.Block())

        @block.sync
        def _(sp):
            sp.dma_start(chan[:, :, :], channel.rearrange("p (a c) -> p a c", a=2)).then_inc(chan_loaded, DMA)
            sp.dma_start(wf[:, :, :], w_fourier.rearrange("h c d -> c h d")).then_inc(chan_loaded, DMA)

            def load_head(q, h):
                S = SEQS[q]
                sp.dma_start(zys[q][:, h * S:(h + 1) * S], z_scr[h, :, tok0[q]:tok0[q] + S]).then_inc(z_loaded[q * HEADS + h], DMA)

            def load_group(q, g):
                S = SEQS[q]
                sp.dma_start(zb[:, g, PAD:PAD + S], z_scr[HEADS + g, :, tok0[q]:tok0[q] + S]).then_inc(zb_loaded[g], DMA)

            load_head(0, 1)
            load_group(0, 3)
            sp.dma_start(wp[:, :, :], w_pool.rearrange("g c d -> c g d")).then_inc(pool_w_loaded, DMA)
            sp.dma_start(pg[:, :], pool_gain).then_inc(pool_w_loaded, DMA)
            sp.dma_start(edges[:, :], edge).then_inc(pool_w_loaded, DMA)
            load_head(0, 2)
            load_head(0, 3)
            for g in (2, 0, 1):
                load_group(0, g)
            for h in range(HEADS):
                load_head(1, h)
            for q, S in enumerate(SEQS):
                with sp.Fori(0, HEADS) as h:
                    sp.wait_ge(stage_done, h * plans[q]["stages"] + (stage0[q] + plans[q]["stages"]))
                    sp.dma_start(y_scr[bass.ds(h, 1), :, tok0[q]:tok0[q] + S].rearrange("a p s -> p (a s)"),
                                 zys[q][:, bass.ds(h * S, S)]).then_inc(y_stored[q], DMA)
                for i in range(HEADS * S // HALF):
                    g, c = ORDER[i // (S // HALF)], i % (S // HALF)
                    at = tok0[q] + c * HALF
                    sp.wait_ge(yb_staged, chunk0[q] + i + 1)
                    sp.dma_start(y_scr[HEADS + g, :, at:at + HALF], yb[:, i % 4, :]).then_inc(yb_stored[i % 4], DMA)
                    if q == 0 and c == S // HALF - 1:
                        load_group(1, g)
                if q == 0:
                    sp.wait_ge(y_stored[0], HEADS * DMA)
                    for d in range(KT):
                        sp.dma_start(ahead.w_out_raw[:, d, :], w_out[d * P:(d + 1) * P, :]).then_inc(ahead.w_out_loaded[d], DMA)
                    for n in range(4):
                        sp.wait_ge(yb_stored[n], chunk0[1] // 4 * DMA)
                    sp.dma_start(ahead.y_raw[:, :, :], y_scr[:, :, 0:HALF].rearrange("c p s -> p c s")).then_inc(ahead.y_loaded, DMA)
            sp.wait_ge(y_stored[1], HEADS * DMA)
            for s in range(4):
                sp.wait_ge(yb_stored[s], HEADS * TOKENS // HALF // 4 * DMA)

        @block.gpsimd
        def _(pool):
            chained = 0

            def chain(ins):
                nonlocal chained
                chained += 1
                ins.then_inc(pool_chain, 1)
                pool.wait_ge(pool_chain, chained)

            def group(q, g):
                S, k, e = SEQS[q], WINDOWS[g], edge_at[g]
                pool.wait_ge(zb_loaded[g], (q + 1) * DMA)
                if q or g != pool_groups[0]:
                    pool.wait_ge(d_by_pool, 3 * q + pool_groups.index(g))
                src, lo, hi = zb[:, g, :], PAD - k // 2 + 1, PAD + S + k // 2 - 1
                chain(pool.tensor_tensor(win[0][:, lo:hi], src[:, lo - 1:hi - 1], src[:, lo:hi], ALU.add))
                n, a = 2, 0
                while n < k:
                    lo, hi = lo + n // 2, hi - n // 2
                    chain(pool.tensor_tensor(win[1 - a][:, lo:hi], win[a][:, lo - n // 2:hi - n // 2],
                                             win[a][:, lo + n // 2:hi + n // 2], ALU.add))
                    n, a = 2 * n, 1 - a
                s = win[a][:, PAD:PAD + S]
                z = src[:, PAD:PAD + S]
                inverse = edges[:, inverse_at + g:inverse_at + g + 1].to_broadcast([P, S - k])
                pool.tensor_tensor(s[:, k // 2:S - k // 2], s[:, k // 2:S - k // 2], inverse, ALU.mult)
                pool.tensor_tensor(s[:, :k // 2], s[:, :k // 2], edges[:, e:e + k // 2], ALU.mult)
                chain(pool.tensor_tensor(s[:, S - k // 2:], s[:, S - k // 2:], edges[:, e + k // 2:e + k], ALU.mult))
                pool.tensor_tensor(z, s, z, ALU.subtract).then_inc(d_by_pool, 1)

            pool.memset(diff[:, SMAX // 2:], 0.0).then_inc(zeroed, 1)
            for g in range(4):
                pool.memset(zb[:, g, 0:PAD], 0.0).then_inc(zeroed, 1)
                pool.memset(zb[:, g, PAD + SEQS[0]:PAD + SEQS[0] + PAD], 0.0).then_inc(zeroed, 1)
            pool.wait_ge(zeroed, 9)
            pool.wait_ge(pool_w_loaded, 3 * DMA)
            for g in pool_groups:
                group(0, g)
            for i, g in enumerate(ORDER):
                pool.wait_ge(yb_ready, (i + 1) * (SEQS[0] // HALF))
                pool.memset(zb[:, g, PAD + SEQS[1]:PAD + SEQS[1] + PAD], 0.0).then_inc(zeroed, 1)
                if g != DVE_GROUP:
                    pool.wait_ge(zeroed, 9 + i + 1)
                    group(1, g)

        @block.scalar
        def _(act):
            act.wait_ge(tab_loaded, DMA)
            for n in range(4):
                act.activation(tab_hi[:, n * RAW:(n + 1) * RAW], tab_raw[:, n * RAW:(n + 1) * RAW], ACT.Copy).then_inc(tab_hi_done, 1)
                if n == 0:
                    act.wait_ge(chan_w_ps_ready, 1)
                    for part in range(2):
                        act.activation(chan_w[:, part, :, :], ch_ps[part][:, :, :], ACT.Copy).then_inc(chan_w_ready, 1)
            act.wait_ge(pool_w_loaded, 3 * DMA)
            for q, S in enumerate(SEQS):
                p = plans[q]
                G, L = len(p["groups"]), len(p["levels"])

                def round_uv(r, h, g):
                    act.wait_ge(ch_ready, h * len(plans[r]["groups"]) + (ch0[r] + g + 1))
                    ts = plans[r]["groups"][g]
                    act.activation(uv_hi[:, ts[0]:ts[-1] + 1, :], ch_ps[g % 2][:, 0:len(ts), :], ACT.Copy).then_inc(uv_hi_done, 1)

                def copy_sine(h, level):
                    n = p["levels"][level] // 4
                    act.wait_ge(cos_sin_ready, h * p["stages"] + (stage0[q] - CREDIT + level + 1))
                    act.wait_ge(stage_done, h * p["stages"] + (stage0[q] + level - 1))
                    act.activation(sine_part[:, level % 2, 0:n], sin_ps[level % 2][:, 0:n], ACT.Copy,
                                   scale=float(S) ** -0.5).then_inc(sine_copied, 1)

                def body(h, following):
                    r, nxt = following or (q, h)
                    early = plans[r]["early"]
                    copy_sine(h, 0)
                    if following:
                        for g in range(early):
                            round_uv(r, nxt, g)
                    for level in range(1, L):
                        copy_sine(h, level)
                    if following:
                        for g in range(early, len(plans[r]["groups"])):
                            round_uv(r, nxt, g)

                if q == 0:
                    for g in range(G):
                        round_uv(0, 0, g)
                with act.Fori(0, HEADS - 1) as h:
                    body(h, (q, h + 1))
                body(HEADS - 1, None if q else (1, 0))

                def stage_yb(n, s, g, first=False):
                    act.wait_ge(yb_ready, n + 1)
                    if not first:
                        act.wait_ge(yb_stored[s], n // 4 * DMA)
                    act.activation(yb[:, s, :], ch_ps[s % 2][:, :, :].rearrange("p a b -> p (a b)"), ACT.Identity,
                                   scale=pg[:, g:g + 1]).then_inc(yb_staged, 1)

                for i in range(HEADS * S // HALF):
                    stage_yb(chunk0[q] + i, i % 4, ORDER[i // (S // HALF)], first=chunk0[q] + i < 4)

        @block.vector
        def _(dve):
            dve.sem_inc(stage_done, CREDIT)

            def fold(q, h):
                S, p = SEQS[q], plans[q]
                G, L, fold_at = len(p["groups"]), len(p["levels"]), p["fold_at"]
                static = isinstance(h, int) and h == 0
                first = static and q == 0
                gidx = {}
                for g, ts in enumerate(p["groups"]):
                    for t in ts:
                        gidx[p["tiles"][t][0]] = g

                def tiles_read(last_tile):
                    if static:
                        dve.wait_ge(ch_ready, ch0[q])
                    else:
                        dve.wait_ge(ch_ready, (h - 1) * G + (ch0[q] + gidx[last_tile] + 1))

                src = zys[q][:, bass.ds(h * S, S)]
                chain = h * p["chain"] + chain0[q]
                steps = 0
                out = 0
                for level, M in enumerate(p["levels"]):
                    n, m = M // 2, M // 4
                    last = level == L - 1
                    d = diff[:, SMAX // 2 - n:SMAX // 2 + 1]
                    if level or not first:
                        dve.wait_ge(fold_done, h * p["folds"] + (fold0[q] + 2 * level))
                    dve.tensor_tensor(d[:, 0:n], src[:, 0:n], src[:, n:M], ALU.subtract).then_inc(fold_chain, 1)
                    if last:
                        dst = folds[:, fold_at[BASE]:fold_at[BASE] + BASE // P, :].rearrange("p a b -> p (a b)")
                    else:
                        dst = sums[:, out:out + n]
                        dve.tensor_tensor(dst, src[:, 0:n], src[:, n:M], ALU.add).then_inc(fold_chain, 1)
                    dve.wait_ge(fold_chain, chain + steps + 1)
                    for k, part in enumerate(("cos", "sin")):
                        f = fold_at[M, part]
                        if not first:
                            tiles_read(f + m // P - 1)
                        o = folds[:, f:f + m // P, :].rearrange("p a b -> p (a b)")
                        if k == 0:
                            dve.tensor_tensor(o, d[:, 0:m], d[:, n:n - m:-1], ALU.subtract).then_inc(fold_done, 1)
                        else:
                            dve.tensor_tensor(o, d[:, 1:m + 1], d[:, n - 1:n - m - 1:-1], ALU.add).then_inc(fold_done, 1)
                    if last:
                        if not first:
                            tiles_read(max(gidx))
                        dve.tensor_tensor(dst, src[:, 0:n], src[:, n:M], ALU.add).then_inc(fold_done, 1)
                    else:
                        dve.wait_ge(fold_chain, chain + steps + 2)
                        src, out, steps = dst, out + n, steps + 2

            def rest_of_uv(q, h, g):
                p = plans[q]
                dve.wait_ge(uv_hi_done, h * len(p["groups"]) + (ch0[q] + g + 1))
                ts = p["groups"][g]
                dve.tensor_tensor(uv_lo[:, ts[0]:ts[-1] + 1, :], ch_ps[g % 2][:, 0:len(ts), :],
                                  uv_hi[:, ts[0]:ts[-1] + 1, :].bitcast(F32), ALU.subtract).then_inc(uv_ready, 1)

            def outputs(q, h, level):
                S, L, M = SEQS[q], len(plans[q]["levels"]), plans[q]["levels"][level]
                m, step = M // 4, S // M
                y = zys[q][:, bass.ds(h * S, S)]
                dve.wait_ge(sine_copied, h * L + (q * HEADS * len(plans[0]["levels"]) + level + 1))
                dve.scalar_tensor_tensor(out=y[:, step:step + 2 * step * m:2 * step], in0=cos_ps[level % 2][:, 0:m],
                                         scalar=float(S) ** -0.5, in1=sine_part[:, level % 2, 0:m],
                                         op0=ALU.mult, op1=ALU.subtract)
                dve.scalar_tensor_tensor(out=y[:, S // 2 + step:S:2 * step], in0=cos_ps[level % 2][:, m - 1::-1],
                                         scalar=float(S) ** -0.5, in1=sine_part[:, level % 2, m - 1::-1],
                                         op0=ALU.mult, op1=ALU.add).then_inc(stage_done, 1)

            def base_outputs(q, h):
                S, p = SEQS[q], plans[q]
                dve.wait_ge(cos_sin_ready, h * p["stages"] + (stage0[q] - CREDIT + p["stages"]))
                y = zys[q][:, bass.ds(h * S, S)]
                dve.tensor_scalar(y[:, 0:S:S // BASE], base_ps[:, :], float(S) ** -0.5, None,
                                  ALU.mult).then_inc(stage_done, 1)

            def body(q, h, following=None, fold_next=None):
                outputs(q, h, 0)
                if following:
                    r, nxt = following
                    for g in range(plans[r]["early"]):
                        rest_of_uv(r, nxt, g)
                for level in range(1, len(plans[q]["levels"])):
                    outputs(q, h, level)
                if following:
                    for g in range(plans[r]["early"], len(plans[r]["groups"])):
                        rest_of_uv(r, nxt, g)
                base_outputs(q, h)
                if fold_next:
                    fold(*fold_next)

            def group(q, folded):
                S, g, k = SEQS[q], DVE_GROUP, WINDOWS[DVE_GROUP]
                e, r = edge_at[g], k // 2
                steps = 5 * q
                dve.wait_ge(zb_loaded[g], (q + 1) * DMA)
                dve.wait_ge(zeroed, 9 + q * (ORDER.index(g) + 1))
                dve.wait_ge(pool_w_loaded, 3 * DMA)
                dve.wait_ge(fold_done, folded)
                lo, hi = PAD - 1, PAD + S + 1
                z = zb[:, g, PAD:PAD + S]
                pairs = scratch[:, 0:hi - lo]
                dve.tensor_tensor(pairs, zb[:, g, lo - 1:hi - 1], zb[:, g, lo:hi], ALU.add).then_inc(pooled, 1)
                dve.wait_ge(pooled, steps + 1)
                dve.tensor_tensor(edge_sums[:, 0:r], pairs[:, 0:r], pairs[:, 2:2 + r], ALU.add)
                dve.tensor_tensor(edge_sums[:, r:k], pairs[:, S - r:S], pairs[:, S + 2 - r:S + 2], ALU.add).then_inc(pooled, 1)
                dve.scalar_tensor_tensor(out=z[:, r:S - r], in0=pairs[:, r:S - r], scalar=1.0 / k, in1=z[:, r:S - r],
                                         op0=ALU.mult, op1=ALU.subtract).then_inc(pooled, 1)
                dve.wait_ge(pooled, steps + 2)
                dve.tensor_tensor(edge_sums[:, :], edge_sums[:, :], edges[:, e:e + k], ALU.mult).then_inc(pooled, 1)
                dve.wait_ge(pooled, steps + 4)
                dve.tensor_tensor(z[:, :r], edge_sums[:, 0:r], z[:, :r], ALU.subtract)
                dve.tensor_tensor(z[:, S - r:], edge_sums[:, r:k], z[:, S - r:], ALU.subtract)
                dve.scalar_tensor_tensor(out=z[:, r:S - r], in0=pairs[:, r + 2:S - r + 2], scalar=1.0 / k, in1=z[:, r:S - r],
                                         op0=ALU.mult, op1=ALU.add).then_inc(pooled, 1)
                dve.wait_ge(pooled, steps + 5)

            dve.wait_ge(zeroed, 1)
            dve.wait_ge(z_loaded[0], DMA)
            fold(0, 0)
            for g in range(len(plans[0]["groups"])):
                if g < 4:
                    dve.wait_ge(tab_hi_done, g + 1)
                    dve.tensor_tensor(tab_lo[:, g * RAW:(g + 1) * RAW], tab_raw[:, g * RAW:(g + 1) * RAW],
                                      tab_hi[:, g * RAW:(g + 1) * RAW].bitcast(F32), ALU.subtract).then_inc(tab_ready, 1)
                rest_of_uv(0, 0, g)
            dve.wait_ge(z_loaded[1], DMA)
            fold(0, 1)
            for h in (2, 3):
                dve.wait_ge(z_loaded[h], DMA)
            with dve.Fori(0, HEADS - 2) as h:
                body(0, h, (0, h + 1), (0, h + 2))
            for h in range(HEADS):
                dve.wait_ge(z_loaded[HEADS + h], DMA)
            body(0, HEADS - 2, (0, HEADS - 1), (1, 0))
            group(0, fold0[1] + plans[1]["folds"])
            body(0, HEADS - 1, (1, 0), (1, 1))
            with dve.Fori(0, HEADS - 2) as h:
                body(1, h, (1, h + 1), (1, h + 2))
            body(1, HEADS - 2, (1, HEADS - 1))
            group(1, fold0[1] + HEADS * plans[1]["folds"])
            body(1, HEADS - 1)

        @block.tensor
        def _(pe):
            pe.wait_ge(chan_loaded, 2 * DMA)
            for part in range(2):
                for h in range(HEADS):
                    mm = pe.matmul(ch_ps[part][:, h, :], chan[:, part, :], wf[:, h, :], start=True, stop=True)
            mm.then_inc(chan_w_ps_ready, 1)
            pe.wait_ge(chan_w_ready, 2)

            def chan_w_of(h, part):
                return chan_w[:, ("cos", "sin").index(part), bass.ds(h, 1), :].rearrange("p a b -> p (a b)")

            def channel_products(q, h, g, first=False):
                p = plans[q]
                G = len(p["groups"])
                pe.wait_ge(fold_done, h * p["folds"] + (fold0[q] + p["need"][g]))
                if g >= 2:
                    pe.wait_ge(uv_ready, h * G + (ch0[q] + g - 1))
                elif not first:
                    pe.wait_ge(uv_ready, h * G + ch0[q])
                    if q and not (isinstance(h, int) and h == 0):
                        pe.wait_ge(yb_staged, chunk0[1])
                for i, t in enumerate(p["groups"][g]):
                    f, part = p["tiles"][t]
                    mm = pe.matmul(ch_ps[g % 2][:, i, :], folds[:, f, :], chan_w_of(h, part), start=True, stop=True)
                mm.then_inc(ch_ready, 1)

            def transform(p, out, M, part, width, rows, first, last):
                for r in range(rows):
                    t = p["tile_at"][M, part] + r
                    a = places[M, part] + r * width
                    mm = three_products(pe, out, uv_hi[:, t, :], uv_lo[:, t, :], tab_hi[:, a:a + width], tab_lo[:, a:a + width],
                                        first and r == 0, last and r == rows - 1)
                return mm

            def level_products(q, h, level):
                p = plans[q]
                M = p["levels"][level]
                m = M // 4
                pe.wait_ge(stage_done, h * p["stages"] + (stage0[q] + level - 1))
                transform(p, cos_ps[level % 2][:, 0:m], M, "cos", m, m // P, True, True)
                transform(p, sin_ps[level % 2][:, 0:m], M, "sin", m, m // P, True, True).then_inc(cos_sin_ready, 1)

            def base_products(q, h):
                p = plans[q]
                pe.wait_ge(stage_done, h * p["stages"] + stage0[q])
                transform(p, base_ps[:, :], BASE, "cos", BASE, BASE // P, True, False)
                transform(p, base_ps[:, :], BASE, "sin", BASE, BASE // P, False, True).then_inc(cos_sin_ready, 1)

            def body(q, h, following):
                p = plans[q]
                G = len(p["groups"])
                pe.wait_ge(uv_ready, h * G + (ch0[q] + p["early"]))
                level_products(q, h, 0)
                if following:
                    r, nxt = following
                    for g in range(plans[r]["early"]):
                        channel_products(r, nxt, g)
                pe.wait_ge(uv_ready, h * G + (ch0[q] + G))
                for level in range(1, len(p["levels"])):
                    level_products(q, h, level)
                base_products(q, h)
                if following:
                    for g in range(plans[r]["early"], len(plans[r]["groups"])):
                        channel_products(r, nxt, g)

            def group_products(q, begun):
                S = SEQS[q]
                pe.wait_ge(uv_ready, begun)
                pe.wait_ge(pool_w_loaded, 3 * DMA)
                for i in range(HEADS * S // HALF):
                    n, g, c = chunk0[q] + i, ORDER[i // (S // HALF)], i % (S // HALF)
                    if c == 0:
                        if g == DVE_GROUP:
                            pe.wait_ge(pooled, 5 * q + 5)
                        else:
                            pe.wait_ge(d_by_pool, 3 * q + pool_groups.index(g) + 1)
                    if n >= 2:
                        pe.wait_ge(yb_staged, n - 1)
                    pe.matmul(ch_ps[i % 2][:, :, :].rearrange("p a b -> p (a b)"), wp[:, g, :],
                              zb[:, g, PAD + c * HALF:PAD + (c + 1) * HALF], start=True, stop=True).then_inc(yb_ready, 1)

            for g in range(len(plans[0]["groups"])):
                channel_products(0, 0, g, first=True)
            pe.wait_ge(tab_ready, 4)
            with pe.Fori(0, HEADS - 1) as h:
                body(0, h, (0, h + 1))
            body(0, HEADS - 1, (1, 0))
            group_products(0, ch0[1] + len(plans[1]["groups"]))
            with pe.Fori(0, HEADS - 1) as h:
                body(1, h, (1, h + 1))
            body(1, HEADS - 1, None)
            group_products(1, ch0[1] + HEADS * len(plans[1]["groups"]))


def project_out(nc, ahead, y_scr, x, ident, w_gate, w_up, g2, x1_scr, h2_scr):
    NT = TOKENS // P
    with ExitStack() as ctx:
        def sb(name, shape, dt=F32):
            return ctx.enter_context(nc.sbuf_tensor(name, shape, dt))

        def sem(name):
            return ctx.enter_context(nc.semaphore(name))

        ahead.reserve(ctx, "project_out", 4 * KT * D)
        ahead.reserve_top(ctx, "project_out")
        w_hi = sb("wout_hi", [P, KT, D], F32R)
        w_lo, w_raw, y_raw = ahead.w_out_lo, ahead.w_out_raw, ahead.y_raw
        y_hi = sb("y_hi", [P, 4, KT, P], F32R)
        y_lo = sb("y_lo", [P, 4, KT, P], F32R)
        x1 = sb("x1", [P, 4, D])
        xn = sb("xn", [P, 2, D])
        junk = sb("junk3", [P, D])
        h_out = sb("h_out", [P, 4, KT, P])
        eye = sb("eye3", [P, P])
        sumsq = sb("sumsq3", [P, 4])
        var = sb("var3", [P, 4])
        std = sb("std3", [P, 4])
        tmp = sb("tmp3", [P, 4])
        rstd = sb("rstd3", [P, 4])
        o_ps = [ctx.enter_context(nc.psum_tensor(f"o_ps{i}", [P, HALF], F32)) for i in range(4)]
        t_ps = [ctx.enter_context(nc.psum_tensor(f"t3_ps{i}", [P, 4, P], F32)) for i in range(4)]

        const_loaded = sem("const_loaded3")
        w_loaded, y_loaded = ahead.w_out_loaded, ahead.y_loaded
        w_hi_done = sem("wout_hi_done")
        w_ready = sem("wout_ready")
        x_loaded = [sem(f"x3_loaded{i}") for i in range(4)]
        y_hi_done = sem("y_hi_done")
        y_ready = sem("y_ready")
        o_ready_half = sem("o_ready_half")
        x1_ready = sem("x1_ready")
        squares_done = sem("squares_done3")
        var_ready = sem("var_ready3")
        std_ready = sem("std_ready3")
        rstd_chain = sem("rstd_chain3")
        xn_ready = sem("xn_ready3")
        transposed = sem("transposed3")
        h_staged = sem("h_staged3")
        x1_stored = [sem(f"x1_stored{i}") for i in range(4)]
        h_stored = [sem(f"h_stored{i}") for i in range(4)]

        block = ctx.enter_context(nc.Block())

        @block.sync
        def _(sp):
            def load_y(j):
                sp.dma_start(y_raw[:, :, :], y_scr[:, :, bass.ds(j * HALF, HALF)].rearrange("c p s -> p c s")).then_inc(y_loaded, DMA)

            def load_x(j, t):
                sp.dma_start(x1[:, t, :], x[bass.ds(j * HALF + t * P, P), :]).then_inc(x_loaded[t], DMA)

            sp.dma_start(eye[:, :], ident).then_inc(const_loaded, DMA)
            for t in range(4):
                load_x(0, t)
            with sp.Fori(1, NT // 4) as j:
                sp.wait_ge(y_ready, j * 4)
                load_y(j)
                for t in range(4):
                    sp.wait_ge(x1_stored[t], j * DMA)
                    load_x(j, t)
            sp.dma_start(ahead.gain2[:, :], g2).then_inc(ahead.gain2_loaded, DMA)
            for i, w in enumerate((w_gate, w_up, w_gate)):
                sp.dma_start(ahead.w_raw[i][:, :], w[i // 2]).then_inc(ahead.w_loaded[i], DMA)
            for t in range(4):
                sp.wait_ge(h_stored[t], DMA)
            sp.dma_start(ahead.h2_raw[:, :, :], h2_scr[:, :, 0:HALF].rearrange("d p s -> p d s")).then_inc(ahead.h2_loaded, DMA)

        @block.scalar
        def _(act):
            def round_y(j, t, first=False):
                act.wait_ge(y_loaded, (j + 1) * DMA)
                if not first:
                    act.wait_ge(o_ready_half, j * 8 + 2 * (t - 3))
                act.activation(y_hi[:, t, :, :], y_raw[:, :, t * P:(t + 1) * P], ACT.Copy).then_inc(y_hi_done, 1)

            def norm(n, t):
                act.wait_ge(x1_ready, n * 2 + 2)
                act.activation(junk[:, :], x1[:, t, :], ACT.Square, accum_out=sumsq[:, t:t + 1]).then_inc(squares_done, 1)
                act.wait_ge(var_ready, n + 1)
                act.activation(std[:, t:t + 1], var[:, t:t + 1], ACT.Sqrt).then_inc(std_ready, 1)

            def stage_h(m, slot, stored=None):
                for k in range(2):
                    act.wait_ge(transposed, m * 2 + (k + 1))
                    if k == 0 and stored is not None:
                        act.wait_ge(h_stored[slot], stored)
                    act.activation(h_out[:, slot, 4 * k:4 * k + 4, :], t_ps[(slot % 2) * 2 + k][:, :, :], ACT.Copy).then_inc(h_staged, 1)

            def step(j, t, lead=True, first=False):
                n = j * 4 + t
                if lead:
                    round_y(j + (t + 2) // 4, (t + 2) % 4, first=first and t < 2)
                if not (first and t == 0):
                    norm(n - 1, (t + 3) % 4)
                    uses = j if t else j - 1
                    stage_h(n - 1, (t + 3) % 4, None if isinstance(uses, int) and uses < 1 else uses * DMA)

            for d in range(KT):
                if d == 0:
                    round_y(0, 0, first=True)
                act.wait_ge(w_loaded[d], DMA)
                act.activation(w_hi[:, d, :], w_raw[:, d, :], ACT.Copy).then_inc(w_hi_done, 1)
            round_y(0, 1, first=True)
            for t in range(4):
                step(0, t, first=True)
            for t in range(4):
                step(1, t)
            with act.Fori(2, NT // 4 - 1) as j:
                for t in range(4):
                    step(j, t)
            for t in range(4):
                step(NT // 4 - 1, t, lead=t < 2)
            norm(NT - 1, 3)
            stage_h(NT - 1, 3, (NT // 4 - 1) * DMA)

        @block.vector
        def _(dve):
            def rest_of_y(j, t):
                dve.wait_ge(y_hi_done, j * 4 + (t + 1))
                dve.tensor_tensor(y_lo[:, t, :, :], y_raw[:, :, t * P:(t + 1) * P], y_hi[:, t, :, :].bitcast(F32),
                                  ALU.subtract).then_inc(y_ready, 1)

            def residual(m, slot, loads):
                dve.wait_ge(x_loaded[slot], loads)
                for c in range(2):
                    dve.wait_ge(o_ready_half, m * 2 + (c + 1))
                    dve.tensor_tensor(x1[:, slot, c * HALF:(c + 1) * HALF], o_ps[(slot % 2) * 2 + c][:, :],
                                      x1[:, slot, c * HALF:(c + 1) * HALF], ALU.add).then_inc(x1_ready, 1)
                dve.wait_ge(squares_done, m + 1)
                one = slice(slot, slot + 1)
                dve.tensor_scalar(var[:, one], sumsq[:, one], 1.0 / D, EPS, ALU.mult, ALU.add).then_inc(var_ready, 1)
                dve.wait_ge(std_ready, m + 1)
                refined_rstd(dve, rstd_chain, m * 4, std[:, one], var[:, one], tmp[:, one], rstd[:, one])
                dve.tensor_scalar(xn[:, slot % 2, :], x1[:, slot, :], rstd[:, one], None, ALU.mult).then_inc(xn_ready, 1)

            def step(j, t, lead=True, first=False):
                if lead:
                    rest_of_y(j + (t + 2) // 4, (t + 2) % 4)
                if not (first and t == 0):
                    residual(j * 4 + (t - 1), (t + 3) % 4, (j + 1) * DMA if t else j * DMA)

            rest_of_y(0, 0)
            for d in range(KT):
                dve.wait_ge(w_hi_done, d + 1)
                dve.tensor_tensor(w_lo[:, d, :], w_raw[:, d, :], w_hi[:, d, :].bitcast(F32),
                                  ALU.subtract).then_inc(w_ready, 1)
            rest_of_y(0, 1)
            for t in range(4):
                step(0, t, first=True)
            with dve.Fori(1, NT // 4 - 1) as j:
                for t in range(4):
                    step(j, t)
            for t in range(4):
                step(NT // 4 - 1, t, lead=t < 2)
            residual(NT - 1, 3, NT // 4 * DMA)

        @block.tensor
        def _(pe):
            def products(n, t, first=False):
                pe.wait_ge(y_ready, n + 1)
                for c in range(2):
                    if not (first and t < 2):
                        pe.wait_ge(x1_ready, n * 2 + (c - 3))
                    for d in range(KT):
                        if first and t == 0 and c == 0:
                            pe.wait_ge(w_ready, d + 1)
                        mm = three_products(pe, o_ps[(t % 2) * 2 + c][:, :], y_hi[:, t, d, :], y_lo[:, t, d, :],
                                            w_hi[:, d, c * HALF:(c + 1) * HALF], w_lo[:, d, c * HALF:(c + 1) * HALF],
                                            d == 0, d == KT - 1)
                    mm.then_inc(o_ready_half, 1)

            def transposes(m, slot, first=False):
                pe.wait_ge(xn_ready, m + 1)
                for k in range(2):
                    if not first:
                        pe.wait_ge(h_staged, m * 2 + (k - 3))
                    for i in range(4):
                        d = 4 * k + i
                        mm = pe.transpose(t_ps[(slot % 2) * 2 + k][:, i, :], xn[:, slot % 2, d * P:(d + 1) * P], eye[:, :])
                    mm.then_inc(transposed, 1)

            def step(j, t, first=False):
                products(j * 4 + t, t, first)
                if not (first and t == 0):
                    transposes(j * 4 + (t - 1), (t + 3) % 4, first=first and t < 3)

            pe.wait_ge(const_loaded, DMA)
            for t in range(4):
                step(0, t, first=True)
            with pe.Fori(1, NT // 4) as j:
                for t in range(4):
                    step(j, t)
            transposes(NT - 1, 3)

        @block.gpsimd
        def _(pool):
            def store_x1(j, t):
                pool.wait_ge(xn_ready, j * 4 + (t + 1))
                pool.dma_start(x1_scr[bass.ds(j * HALF + t * P, P), :], x1[:, t, :]).then_inc(x1_stored[t], DMA)

            def store_h(m, slot):
                pool.wait_ge(h_staged, m * 2 + 2)
                pool.dma_start(h2_scr[:, :, bass.ds(m * P, P)].rearrange("d p s -> p d s"), h_out[:, slot, :, :]).then_inc(h_stored[slot], DMA)

            for t in range(4):
                store_x1(0, t)
                if t:
                    store_h(t - 1, t - 1)
            with pool.Fori(1, NT // 4) as j:
                for t in range(4):
                    store_x1(j, t)
                    store_h(j * 4 + (t - 1), (t + 3) % 4)
            store_h(NT - 1, 3)
            for t in range(4):
                pool.wait_ge(x1_stored[t], NT // 4 * DMA)
                pool.wait_ge(h_stored[t], NT // 4 * DMA)


def ffn(nc, ahead, x1_scr, h2_scr, w_gate, w_up, w_down, gf, out):
    TB = 2 * HALF
    NB = TOKENS // TB
    NP = FT // 2
    ST = HALF // P
    with ExitStack() as ctx:
        def sb(name, shape, dt=F32):
            return ctx.enter_context(nc.sbuf_tensor(name, shape, dt))

        def sem(name):
            return ctx.enter_context(nc.semaphore(name))

        ahead.reserve_top(ctx, "ffn")
        h_hi = sb("h2_hi", [P, 2, KT, HALF], F32R)
        h_lo, h_raw = (list(pair) for pair in zip((ahead.h2_lo, ahead.h2_raw), low_over_raw(nc, ctx, "h2", [P, KT, HALF])))
        acc = sb("acc", [P, 2 * ST, D])
        raw = ahead.w_raw
        w_hi = sb("w_hi4", [P, 6, D], F32R)
        w_lo = sb("w_lo4", [P, 6, D], F32R)
        silu = sb("silu", [P, 2, HALF])
        prod = sb("prod", [P, 2, HALF])
        a_hi = sb("a_hi", [P, 4, HALF], F32R)
        a_lo = sb("a_lo", [P, 4, HALF], F32R)
        junk = sb("junk4", [P, D])
        gain2 = ahead.gain2
        gain_f = sb("gain_f", [P, D])
        sumsq = sb("sumsq4", [P, 2 * ST])
        var = sb("var4", [P, 2 * ST])
        std = sb("std4", [P, 2 * ST])
        tmp = sb("tmp4", [P, 2 * ST])
        rstd = sb("rstd4", [P, 2 * ST])
        gate_ps = [ctx.enter_context(nc.psum_tensor(f"gate_ps{i}", [P, HALF], F32)) for i in range(2)]
        up_ps = [ctx.enter_context(nc.psum_tensor(f"up_ps{i}", [P, HALF], F32)) for i in range(2)]
        down_ps = [ctx.enter_context(nc.psum_tensor(f"down_ps{i}", [P, HALF], F32)) for i in range(4)]

        gain_f_loaded = sem("gain_f_loaded")
        raw_loaded = ahead.w_loaded
        w_hi_done = sem("w_hi_done4")
        w_ready = sem("w_ready4")
        h_loaded = [ahead.h2_loaded, sem("h2_loaded1")]
        h_hi_done = sem("h_hi_done4")
        h_ready = sem("h_ready4")
        x1_loaded = [sem(f"x1_loaded{i}") for i in range(2)]
        gate_ready = sem("gate_ready")
        up_ready = sem("up_ready")
        silu_done = sem("silu_done")
        prod_done = sem("prod_done")
        a_hi_done = sem("a_hi_done")
        a_ready = sem("a_ready")
        down_ready = sem("down_ready")
        down_added = sem("down_added")
        squares_done = sem("squares_done4")
        var_ready = sem("var_ready4")
        std_ready = sem("std_ready4")
        rstd_chain = sem("rstd_chain4")
        out_ready = sem("out_ready")
        out_stored = [sem(f"out_stored{i}") for i in range(2)]

        block = ctx.enter_context(nc.Block())

        def run(eng, body, tail):
            body(0, 0, 0, "first")
            with eng.Fori(0, NB - 1) as b:
                with eng.Fori(1, NP - 1) as i:
                    body(b * NP + i, b, i, "inner")
                body(b * NP + (NP - 1), b, NP - 1, "last")
                body(b * NP + NP, b + 1, 0, "first")
            with eng.Fori(1, NP - 1) as i:
                body(i + (NB - 1) * NP, NB - 1, i, "inner")
            body(NB * NP - 1, NB - 1, NP - 1, "last")
            tail()

        def fixed(q, value):
            return isinstance(q, int) and q == value

        @block.sync
        def _(sp):
            def load_weights(q, i, ks):
                for k in ks:
                    sp.wait_ge(w_ready, q * 6 + (k - 2))
                    if k >= 6:
                        f = 0 if fixed(i, NP - 1) else i * 2 + 2
                    else:
                        f = i * 2 + (0, 0, 1, 1, 0, 1)[k]
                    if k % 6 < 4:
                        src = (w_gate, w_up)[k % 2][bass.ds(f, 1), :, :].rearrange("a p n -> p (a n)")
                    else:
                        src = w_down[bass.ds(f * P, P), :]
                    sp.dma_start(raw[k % 3][:, :], src).then_inc(raw_loaded[k % 3], DMA)

            def load_h(b, half):
                if not fixed(b, 0):
                    sp.wait_ge(up_ready, b * (4 * NP) + (2 * half - 2))
                sp.dma_start(h_raw[half][:, :, :],
                             h2_scr[:, :, bass.ds(b * TB + half * HALF, HALF)].rearrange("d p s -> p d s")).then_inc(h_loaded[half], DMA)

            def load_x1(b, half):
                if not fixed(b, 0):
                    sp.wait_ge(out_stored[half], b * (ST * DMA))
                sp.dma_start(acc[:, half * ST:(half + 1) * ST, :],
                             x1_scr[bass.ds(b * TB + half * HALF, HALF), :].rearrange("(t p) n -> p t n", p=P)).then_inc(x1_loaded[half], DMA)

            def body(q, b, i, place):
                final = place == "last" and isinstance(b, int)
                if place == "inner":
                    load_weights(q, i, (2, 3, 4, 5, 6, 7))
                elif place == "first":
                    load_weights(q, i, (3, 4) if fixed(q, 0) else (2, 3, 4))
                    load_h(b, 1)
                    load_x1(b, 0)
                    load_weights(q, i, (5, 6, 7))
                    load_x1(b, 1)
                else:
                    load_weights(q, i, (2, 3, 4, 5))
                    if not final:
                        load_h(b + 1, 0)
                        load_weights(q, i, (6, 7))

            sp.dma_start(gain_f[:, :], gf.partition_broadcast(P)).then_inc(gain_f_loaded, DMA)
            run(sp, body, lambda: None)

        @block.scalar
        def _(act):
            def round_w(q, ks):
                for k in ks:
                    if k in (2, 3) and not fixed(q, 0):
                        act.wait_ge(up_ready, q * 4)
                    if k in (4, 5) and not fixed(q, 0):
                        act.wait_ge(down_ready, q * 16)
                    if k in (6, 7):
                        act.wait_ge(up_ready, q * 4 + 3)
                    act.wait_ge(raw_loaded[k % 3], (q * 2 + (k // 3 + 1)) * DMA)
                    act.activation(w_hi[:, k % 6, :], raw[k % 3][:, :], ACT.Copy).then_inc(w_hi_done, 1)

            def round_h(b, half):
                if not fixed(b, 0):
                    act.wait_ge(up_ready, b * (4 * NP) + (2 * half - 2))
                act.wait_ge(h_loaded[half], (b + 1) * DMA)
                for d in range(KT):
                    act.activation(h_hi[:, half, d, :], h_raw[half][:, d, :], ACT.Identity,
                                   scale=gain2[:, d:d + 1]).then_inc(h_hi_done, 1)

            def gate(q, m):
                act.wait_ge(gate_ready, q * 4 + (m + 1))
                if not (fixed(q, 0) and m < 2):
                    act.wait_ge(prod_done, q * 4 + (m - 1))
                act.activation(silu[:, m % 2, :], gate_ps[m % 2][:, :], ACT.Silu).then_inc(silu_done, 1)

            def round_a(q, m):
                act.wait_ge(prod_done, q * 4 + (m + 1))
                act.activation(a_hi[:, m, :], prod[:, m % 2, :], ACT.Copy).then_inc(a_hi_done, 1)

            def last_norm(b, half):
                nth = b * 2 + half
                act.wait_ge(down_added, down_done(b, half))
                for t in range(ST):
                    one = half * ST + t
                    if t:
                        act.wait_ge(squares_done, nth * ST + t)
                    act.activation(junk[:, :], acc[:, one, :], ACT.Square,
                                   accum_out=sumsq[:, one:one + 1]).then_inc(squares_done, 1)
                act.wait_ge(var_ready, nth + 1)
                act.activation(std[:, half * ST:(half + 1) * ST], var[:, half * ST:(half + 1) * ST], ACT.Sqrt).then_inc(std_ready, 1)

            def down_done(b, half):
                return b * (16 * NP) + (16 * NP - 8 + 8 * half)

            def body(q, b, i, place):
                first, last = place == "first", place == "last"
                final = last and isinstance(b, int)
                if fixed(q, 0):
                    round_w(q, (0,))
                    act.wait_ge(ahead.gain2_loaded, DMA)
                    round_h(b, 0)
                    round_w(q, (1,))
                round_w(q, (2, 3))
                gate(q, 0)
                round_a(q, 0)
                if first:
                    round_h(b, 1)
                round_w(q, (4, 5))
                if first and not fixed(q, 0):
                    last_norm(b - 1, 1)
                gate(q, 1)
                round_a(q, 1)
                gate(q, 2)
                round_a(q, 2)
                if not final:
                    round_w(q, (6, 7))
                    if last:
                        round_h(b + 1, 0)
                gate(q, 3)
                round_a(q, 3)
                if last:
                    last_norm(b, 0)

            run(act, body, lambda: last_norm(NB - 1, 1))

        @block.vector
        def _(dve):
            def rest_of_w(q, ks):
                for k in ks:
                    dve.wait_ge(w_hi_done, q * 6 + (k + 1))
                    dve.tensor_tensor(w_lo[:, k % 6, :], raw[k % 3][:, :], w_hi[:, k % 6, :].bitcast(F32),
                                      ALU.subtract).then_inc(w_ready, 1)

            def rest_of_h(b, half):
                for d in range(KT):
                    dve.wait_ge(h_hi_done, b * (2 * KT) + (half * KT + d + 1))
                    dve.scalar_tensor_tensor(out=h_lo[half][:, d, :], in0=h_raw[half][:, d, :], scalar=gain2[:, d:d + 1],
                                             in1=h_hi[:, half, d, :].bitcast(F32), op0=ALU.mult,
                                             op1=ALU.subtract).then_inc(h_ready, 1)

            def product(q, m):
                dve.wait_ge(silu_done, q * 4 + (m + 1))
                dve.wait_ge(up_ready, q * 4 + (m + 1))
                dve.tensor_tensor(prod[:, m % 2, :], up_ps[m % 2][:, :], silu[:, m % 2, :], ALU.mult).then_inc(prod_done, 1)
                dve.wait_ge(a_hi_done, q * 4 + (m + 1))
                dve.tensor_tensor(a_lo[:, m, :], prod[:, m % 2, :], a_hi[:, m, :].bitcast(F32),
                                  ALU.subtract).then_inc(a_ready, 1)

            def add(q, half, loaded=None):
                if loaded is not None:
                    dve.wait_ge(x1_loaded[half], loaded)
                for t in range(ST):
                    for c in range(2):
                        g = 2 * t + c
                        dve.wait_ge(down_ready, q * 16 + (half * 8 + g + 1))
                        dst = acc[:, half * ST + t, c * HALF:(c + 1) * HALF]
                        dve.tensor_tensor(dst, down_ps[g % 4][:, :], dst, ALU.add).then_inc(down_added, 1)

            def last_norm_var(b, half):
                these = slice(half * ST, (half + 1) * ST)
                nth = b * 2 + half
                dve.wait_ge(squares_done, nth * ST + ST)
                dve.tensor_scalar(var[:, these], sumsq[:, these], 1.0 / D, EPS, ALU.mult, ALU.add).then_inc(var_ready, 1)
                dve.wait_ge(std_ready, nth + 1)
                refined_rstd(dve, rstd_chain, nth * 4, std[:, these], var[:, these], tmp[:, these], rstd[:, these])
                for t in range(ST):
                    one = half * ST + t
                    dve.scalar_tensor_tensor(out=acc[:, one, :], in0=acc[:, one, :], scalar=rstd[:, one:one + 1],
                                             in1=gain_f[:, :], op0=ALU.mult, op1=ALU.mult).then_inc(out_ready, 1)

            def body(q, b, i, place):
                first, last = place == "first", place == "last"
                final = last and isinstance(b, int)
                loaded = (b + 1) * DMA if first else None
                if fixed(q, 0):
                    rest_of_w(q, (0,))
                    dve.wait_ge(ahead.gain2_loaded, DMA)
                    rest_of_h(b, 0)
                    rest_of_w(q, (1,))
                    dve.wait_ge(gain_f_loaded, DMA)
                rest_of_w(q, (2, 3))
                product(q, 0)
                if not fixed(q, 0):
                    add(q - 1, 1)
                if first:
                    rest_of_h(b, 1)
                rest_of_w(q, (4, 5))
                if first and not fixed(q, 0):
                    last_norm_var(b - 1, 1)
                product(q, 1)
                product(q, 2)
                if not final:
                    rest_of_w(q, (6, 7))
                add(q, 0, loaded)
                if last and not final:
                    rest_of_h(b + 1, 0)
                product(q, 3)
                if first:
                    dve.wait_ge(x1_loaded[1], loaded)
                if last:
                    last_norm_var(b, 0)

            def tail():
                add(NB * NP - 1, 1)
                last_norm_var(NB - 1, 1)

            run(dve, body, tail)

        @block.tensor
        def _(pe):
            def up(q, m, b, first):
                tile, half = m % 2, m // 2
                if not (fixed(q, 0) and m < 2):
                    pe.wait_ge(prod_done, q * 4 + (m - 1))
                for part, ps in ((0, gate_ps), (1, up_ps)):
                    k = 2 * tile + part
                    if half == 0:
                        pe.wait_ge(w_ready, q * 6 + (k + 1))
                    for d in range(KT):
                        if first and tile == 0 and part == 0:
                            pe.wait_ge(h_ready, b * (2 * KT) + (half * KT + d + 1))
                        mm = three_products(pe, ps[m % 2][:, :], w_hi[:, k, d * P:(d + 1) * P], w_lo[:, k, d * P:(d + 1) * P],
                                            h_hi[:, half, d, :], h_lo[half][:, d, :], d == 0, d == KT - 1)
                    mm.then_inc((gate_ready, up_ready)[part], 1)

            def down(q, half):
                pe.wait_ge(a_ready, q * 4 + (2 * half + 2))
                if half == 0:
                    pe.wait_ge(w_ready, q * 6 + 6)
                for t in range(ST):
                    for c in range(2):
                        g = 2 * t + c
                        if not (fixed(q, 0) and half == 0 and g < 4):
                            pe.wait_ge(down_added, q * 16 + (half * 8 + g - 3))
                        for f in range(2):
                            m = 2 * half + f
                            mm = three_products(pe, down_ps[g % 4][:, :], a_hi[:, m, t * P:(t + 1) * P], a_lo[:, m, t * P:(t + 1) * P],
                                                w_hi[:, 4 + f, c * HALF:(c + 1) * HALF], w_lo[:, 4 + f, c * HALF:(c + 1) * HALF],
                                                f == 0, f == 1)
                        mm.then_inc(down_ready, 1)

            def body(q, b, i, place):
                first = place == "first"
                up(q, 0, b, first)
                if not fixed(q, 0):
                    down(q - 1, 1)
                up(q, 1, b, first)
                up(q, 2, b, first)
                down(q, 0)
                up(q, 3, b, first)

            run(pe, body, lambda: down(NB * NP - 1, 1))

        @block.gpsimd
        def _(pool):
            def store(b, half):
                for t in range(ST):
                    pool.wait_ge(out_ready, b * (2 * ST) + (half * ST + t + 1))
                    pool.dma_start(out[bass.ds(b * TB + (half * ST + t) * P, P), :],
                                   acc[:, half * ST + t, :]).then_inc(out_stored[half], DMA)

            with pool.Fori(0, NB) as b:
                for half in range(2):
                    store(b, half)
            for half in range(2):
                pool.wait_ge(out_stored[half], NB * ST * DMA)


def encoder(nc, x, w_in, w_fourier, w_pool, w_out, w_gate, w_up, w_down, g1, g2, gf, pool_gain,
            table, channel, edge, ident, out):
    def scratch(name, shape):
        return nc.dram_tensor(name, shape, F32, kind="Internal").ap()

    z_scr = scratch("z_scr", (KT, P, TOKENS))
    y_scr = scratch("y_scr", (KT, P, TOKENS))
    x1_scr = scratch("x1_scr", (TOKENS, D))
    h2_scr = scratch("h2_scr", (KT, P, TOKENS))
    with ExitStack() as ctx:
        ahead = Ahead(nc, ctx)
        project_in(nc, ahead, x, w_in, g1, ident, z_scr, table)
        mix(nc, ahead, w_out, z_scr, y_scr, channel, w_fourier, w_pool, pool_gain, edge)
        project_out(nc, ahead, y_scr, x, ident, w_gate, w_up, g2, x1_scr, h2_scr)
        ffn(nc, ahead, x1_scr, h2_scr, w_gate, w_up, w_down, gf, out)


def kernel(x_prompt, x_sample, norm1_g, w_in, w_fourier, w_pool, pool_scale, w_out, norm2_g, w_gate, w_up, w_down, normf_g):
    import concourse.bacc as bacc
    from concourse.bass_utils import run_bass_kernel_spmd

    def a(v):
        return np.ascontiguousarray(np.asarray(v))

    def by_partition(g):
        return a(a(g).reshape(-1, P).T)

    def hidden_tiles(w):
        return a(a(w).reshape(KT, P, FT, P).transpose(2, 1, 0, 3).reshape(FT, P, KT * P))

    table, channel = fourier_tables()
    arrays = {
        "x": a(np.concatenate([a(x_prompt)[0], a(x_sample)[0]], axis=0)),
        "w_in": a(w_in)[0],
        "w_fourier": a(w_fourier)[0],
        "w_pool": a(w_pool)[0],
        "w_out": a(w_out)[0],
        "w_gate": hidden_tiles(a(w_gate)[0]),
        "w_up": hidden_tiles(a(w_up)[0]),
        "w_down": a(w_down)[0],
        "g1": by_partition(a(norm1_g)[0]),
        "g2": by_partition(a(norm2_g)[0]),
        "gf": a(normf_g),
        "pool_gain": by_partition(a(pool_scale)[0]),
        "table": table,
        "channel": channel,
        "edge": edge_counts(),
        "ident": np.eye(P, dtype=np.float32),
    }
    arrays = {f"in_{k}": a(v) for k, v in arrays.items()}
    nc = bacc.Bacc("TRN2", target_bir_lowering=False, num_devices=1)
    args = [nc.dram_tensor(k, v.shape, mybir.dt.from_np(v.dtype), kind="ExternalInput").ap() for k, v in arrays.items()]
    out = nc.dram_tensor("out", (TOKENS, D), F32, kind="ExternalOutput").ap()
    encoder(nc, *args, out)
    r = run_bass_kernel_spmd(nc, [arrays], core_ids=[0])
    y = r.results[0]["out"]
    return y[:SEQS[0]][None], y[SEQS[0]:][None]
```

```python
from contextlib import ExitStack

import numpy as np

import concourse.bass as bass
from concourse import mybir

F32 = mybir.dt.float32
F32R = mybir.dt.float32r
ALU = mybir.AluOpType
ACT = mybir.ActivationFunctionType

P = 128
D = 1024
KT = D // P
SEQS = (2048, 1024)
TOKENS = sum(SEQS)
HALF = 512
EPS = 1e-6
HEADS = 4
WINDOWS = (2, 4, 8, 16)
PAD = max(WINDOWS) // 2
BASE = 256
D_FF = 2816
FT = D_FF // P
DMA = 16


def levels(S):
    out = []
    while S > BASE:
        out.append(S)
        S //= 2
    return out


def table_places():
    at, places = 0, {}
    for M in levels(max(SEQS)):
        for part in ("cos", "sin"):
            places[M, part] = at
            at += (M // 4 // P) * (M // 4)
    for part in ("cos", "sin"):
        places[BASE, part] = at
        at += (BASE // P) * BASE
    return places, at


def fourier_tables():
    places, width = table_places()
    table = np.zeros((P, width))

    def put(key, rows_by_cols):
        rows, cols = rows_by_cols.shape
        for t in range(rows // P):
            table[:, places[key] + t * cols:places[key] + (t + 1) * cols] = rows_by_cols[t * P:(t + 1) * P]

    for M in levels(max(SEQS)):
        odd = 2 * np.arange(M // 4) + 1
        put((M, "cos"), np.cos(2 * np.pi / M * (np.outer(np.arange(M // 4), odd) % M)))
        sin = np.sin(2 * np.pi / M * (np.outer(np.arange(M // 4) + 1, odd) % M))
        sin[-1] *= 0.5
        put((M, "sin"), sin)
    angle = 2 * np.pi / BASE * (np.outer(np.arange(BASE), np.arange(BASE)) % BASE)
    put((BASE, "cos"), np.cos(angle))
    put((BASE, "sin"), -np.sin(angle))
    angle = 2 * np.pi / P * (np.outer(np.arange(P), np.arange(P)) % P)
    channel = np.concatenate([np.cos(angle), np.sin(angle)], axis=1) / np.sqrt(P)
    return table.astype(np.float32), channel.astype(np.float32)


def edge_counts():
    out = []
    for k in WINDOWS:
        out += [1.0 / (t + k // 2) for t in range(k // 2)]
        out += [1.0 / (k - t) for t in range(k // 2)]
    out += [1.0 / k for k in WINDOWS]
    return np.tile(np.array(out, np.float32), (P, 1))


def low_over_raw(nc, ctx, name, shape):
    at = -(-nc.sbuf_base // 32) * 32
    lo = ctx.enter_context(nc.sbuf_tensor(f"{name}_lo", shape, F32R))
    return lo, nc.alloc_sbuf_tensor_at(f"{name}_raw", shape, F32, offset=at)


class Ahead:

    def __init__(self, nc, ctx):
        self.nc = nc
        self.bottom = -(-nc.sbuf_base // 32) * 32
        TW = table_places()[1]
        tables = self.bottom + 4 * (2 + HEADS) * P
        above = tables + 4 * TW
        self.tables_bytes = above - self.bottom

        def sb(name, shape, dt, offset):
            return nc.alloc_sbuf_tensor_at(name, shape, dt, offset=offset)

        def sem(name):
            return ctx.enter_context(nc.semaphore(name))

        self.chan = sb("chan", [P, 2, P], F32, self.bottom)
        self.wf = sb("wf", [P, HEADS, P], F32, self.bottom + 4 * 2 * P)
        self.chan_loaded = sem("chan_loaded")
        self.tab_lo = sb("tab_lo", [P, TW], F32R, tables)
        self.tab_raw = sb("tab_raw", [P, TW], F32, tables)
        self.y_raw = sb("y_raw", [P, KT, HALF], F32, tables)
        self.zy = sb("zy", [P, HEADS * SEQS[0]], F32, above)
        self.w_out_lo = sb("wout_lo", [P, KT, D], F32R, above)
        self.w_out_raw = sb("wout_raw", [P, KT, D], F32, above)
        self.tab_loaded = sem("tab_loaded")
        self.z_loaded = sem("zh_loaded0")
        self.w_out_loaded = [sem(f"wout_loaded{i}") for i in range(KT)]
        self.y_loaded = sem("y_loaded")
        at = nc.sbuf_usable_end // 32 * 32
        self.end = at
        at -= 4 * 4 * D
        self.z_out = sb("z_out", [P, 4, HALF], F32, self.end - 4 * 4 * HALF)
        self.zy1 = sb("zy1", [P, HEADS * SEQS[1]], F32, at)
        self.x1 = sb("x1", [P, 4, D], F32, at)
        at -= 4 * 4 * HALF
        self.yb = sb("yb", [P, 4, HALF], F32, at)
        self.yb_bytes = self.end - at
        at = self.end - 2 * 4 * 4 * D
        self.h_out = sb("h_out", [P, 4, KT, P], F32, at)
        self.acc = sb("acc", [P, 8, D], F32, at)
        self.z_stored = [sem(f"z_stored{i}") for i in range(4)]
        self.y_stored = [sem(f"y_stored{i}") for i in range(2)]
        self.yb_stored = [sem(f"yb_stored{i}") for i in range(4)]
        self.x1_stored = [sem(f"x1_stored{i}") for i in range(4)]
        self.h_stored = [sem(f"h_stored{i}") for i in range(4)]
        sizes = {"h": 4 * KT * HALF, "w": 4 * D, "gain": 4 * KT}
        self.top = at - (sizes["h"] + 3 * sizes["w"] + sizes["gain"])
        self.top_bytes = self.end - self.top
        at -= sizes["h"]
        self.h2_lo = sb("h2_lo_ahead", [P, KT, HALF], F32R, at)
        self.h2_raw = sb("h2_raw_ahead", [P, KT, HALF], F32, at)
        self.w_raw = []
        for i in range(3):
            at -= sizes["w"]
            self.w_raw.append(sb(f"w_raw{i}", [P, D], F32, at))
        self.gain2 = sb("gain2", [P, KT], F32, self.top)
        self.h2_loaded = sem("h2_loaded0")
        self.w_loaded = [sem(f"raw_loaded{i}") for i in range(3)]
        self.gain2_loaded = sem("gain2_loaded")

    def reserve_top(self, ctx, stage, size):
        ctx.enter_context(self.nc.sbuf_tensor(f"ahead_top_{stage}", [P, size // 4], F32, side="right"))
        assert self.nc.sbuf_top <= self.end - size

    def reserve(self, ctx, stage, above_tables):
        at = -(-self.nc.sbuf_base // 32) * 32
        assert at == self.bottom
        ctx.enter_context(self.nc.sbuf_tensor(f"ahead_{stage}", [P, (self.tables_bytes + above_tables) // 4], F32))


def three_products(pe, out, w_hi, w_lo, m_hi, m_lo, first, last):
    pe.matmul(out, w_hi, m_hi, start=first, stop=False)
    pe.matmul(out, w_hi, m_lo, start=False, stop=False)
    return pe.matmul(out, w_lo, m_hi, start=False, stop=last)


def refined_rstd(dve, chain, done, std, var, tmp, rstd):
    dve.reciprocal(tmp, std).then_inc(chain, 1)
    dve.wait_ge(chain, done + 1)
    dve.scalar_tensor_tensor(out=rstd, in0=tmp, scalar=-0.5, in1=tmp, op0=ALU.mult, op1=ALU.mult).then_inc(chain, 1)
    dve.wait_ge(chain, done + 2)
    dve.tensor_tensor(rstd, rstd, var, ALU.mult).then_inc(chain, 1)
    dve.wait_ge(chain, done + 3)
    dve.scalar_tensor_tensor(out=rstd, in0=rstd, scalar=1.5, in1=tmp, op0=ALU.add, op1=ALU.mult).then_inc(chain, 1)
    dve.wait_ge(chain, done + 4)


def project_in(nc, ahead, x, w_in, g1, ident, z_scr, table, channel, w_fourier):
    NJ = TOKENS // HALF
    with ExitStack() as ctx:
        ahead.reserve(ctx, "project_in", 4 * SEQS[0])
        ahead.reserve_top(ctx, "project_in", 4 * 4 * HALF)
        def sb(name, shape, dt=F32):
            return ctx.enter_context(nc.sbuf_tensor(name, shape, dt))

        def sem(name):
            return ctx.enter_context(nc.semaphore(name))

        w_hi = sb("win_hi", [P, KT, D], F32R)
        w_lo, w_raw = low_over_raw(nc, ctx, "win", [P, KT, D])
        xin = sb("xin", [P, 2, 4, D])
        h_hi = sb("h_hi", [P, 2, KT, HALF], F32R)
        h_lo = sb("h_lo", [P, 2, KT, HALF], F32R)
        z_out = ahead.z_out
        junk = sb("junk1", [P, D], mybir.dt.bfloat16)
        eye = sb("eye1", [P, P])
        gain = sb("gain1", [P, KT])
        warm = sb("warm", [P, 2])
        sumsq = sb("sumsq1", [P, 2, 4])
        var = sb("var1", [P, 2, 4])
        std = sb("std1", [P, 2, 4])
        tmp = sb("tmp1", [P, 2, 4])
        rstd = sb("rstd1", [P, 2, 4])
        z_ps = [ctx.enter_context(nc.psum_tensor(f"z_ps{i}", [P, HALF], F32)) for i in range(4)]
        t_ps = [ctx.enter_context(nc.psum_tensor(f"t_ps{i}", [P, HALF], F32)) for i in range(4)]

        const_loaded = sem("const_loaded1")
        w_loaded = [sem(f"win_loaded{i}") for i in range(KT)]
        x_first = [sem(f"x_first{i}") for i in range(4)]
        x_loaded = [sem(f"x_loaded{i}") for i in range(2)]
        w_hi_done = sem("win_hi_done")
        w_ready = sem("win_ready")
        warm_ready = sem("warm_ready")
        squares_done = sem("squares_done1")
        var_ready = sem("var_ready1")
        std_ready = sem("std_ready1")
        rstd_chain = sem("rstd_chain1")
        xn_ready = sem("xn_ready1")
        transposed = sem("transposed1")
        h_hi_done = sem("h_hi_done1")
        h_ready = sem("h_ready1")
        z_ready = sem("z_ready")
        z_staged = sem("z_staged")
        z_stored = ahead.z_stored

        block = ctx.enter_context(nc.Block())

        @block.sync
        def _(sp):
            def load_x(j, slot):
                sp.dma_start(xin[:, slot, :, :],
                             x[bass.ds(j * HALF, HALF), :].rearrange("(t p) d -> p t d", p=P)).then_inc(x_loaded[slot], DMA)

            def store_z(j, c):
                sp.wait_ge(z_staged, j * KT + c + 1)
                sp.dma_start(z_scr[c, :, bass.ds(j * HALF, HALF)], z_out[:, c % 4, :]).then_inc(z_stored[c % 4], DMA)

            for t in range(4):
                sp.dma_start(xin[:, 0, t, :], x[t * P:(t + 1) * P, :]).then_inc(x_first[t], DMA)
            sp.dma_start(eye[:, :], ident).then_inc(const_loaded, DMA)
            sp.dma_start(gain[:, :], g1).then_inc(const_loaded, DMA)
            for d in range(KT):
                sp.dma_start(w_raw[:, d, :], w_in[d * P:(d + 1) * P, :]).then_inc(w_loaded[d], DMA)
            load_x(1, 1)
            with sp.Fori(0, NJ // 2 - 1) as it:
                for slot in range(2):
                    sp.wait_ge(transposed, (it * 2 + slot + 1) * KT)
                    load_x(it * 2 + slot + 2, slot)
                    for c in range(KT):
                        store_z(it * 2 + slot, c)
            sp.dma_start(ahead.chan[:, :, :], channel.rearrange("p (a c) -> p a c", a=2)).then_inc(ahead.chan_loaded, DMA)
            sp.dma_start(ahead.wf[:, :, :], w_fourier.rearrange("h c d -> c h d")).then_inc(ahead.chan_loaded, DMA)
            sp.dma_start(ahead.tab_raw[:, :], table).then_inc(ahead.tab_loaded, DMA)
            for s in range(4):
                sp.wait_ge(z_stored[s], 2 * (SEQS[0] // HALF) * DMA)
            sp.dma_start(ahead.zy[:, 0:SEQS[0]], z_scr[0, :, 0:SEQS[0]]).then_inc(ahead.z_loaded, DMA)
            for j in range(NJ - 2, NJ):
                for c in range(KT):
                    store_z(j, c)

        @block.scalar
        def _(act):
            def squares(j, n, slot):
                first = isinstance(j, int) and j == 0
                if not first:
                    act.wait_ge(x_loaded[slot], n * DMA)
                for t in range(4):
                    if first:
                        act.wait_ge(x_first[t], DMA)
                    if t:
                        act.wait_ge(squares_done, j * 4 + t)
                    act.activation(junk[:, :], xin[:, slot, t, :], ACT.Square,
                                   accum_out=sumsq[:, slot, t:t + 1]).then_inc(squares_done, 1)
                    if first:
                        act.wait_ge(var_ready, t + 1)
                        act.activation(std[:, 0, t:t + 1], var[:, 0, t:t + 1], ACT.Sqrt).then_inc(std_ready, 1)
                if not first:
                    act.wait_ge(var_ready, j + 4)
                    act.activation(std[:, slot, :], var[:, slot, :], ACT.Sqrt).then_inc(std_ready, 1)

            def round_h(j, slot, d):
                act.wait_ge(transposed, j * KT + d + 1)
                act.activation(h_hi[:, slot, d, :], t_ps[d % 4][:, :], ACT.Identity,
                               scale=gain[:, d:d + 1]).then_inc(h_hi_done, 1)

            def stage_z(j, c, first=False):
                act.wait_ge(z_ready, j * KT + c + 1)
                if not (first and c < 4):
                    act.wait_ge(z_stored[c % 4], (j * 2 + c // 4) * DMA)
                act.activation(z_out[:, c % 4, :], z_ps[c % 4][:, :], ACT.Copy).then_inc(z_staged, 1)

            def step(j, n_next, slot, first=False):
                squares(j + 1, n_next, 1 - slot)
                before = 5 if first else 3
                for c in range(before):
                    stage_z(j, c, first)
                for k in range(max(KT - before, 4)):
                    for d in range(2 * k, min(2 * k + 2, KT)):
                        round_h(j + 1, 1 - slot, d)
                    if before + k < KT:
                        stage_z(j, before + k, first)

            act.wait_ge(warm_ready, 1)
            act.activation(warm[:, 1:2], warm[:, 0:1], ACT.Sqrt)
            squares(0, 0, 0)
            for d in range(KT):
                act.wait_ge(w_loaded[d], DMA)
                act.activation(w_hi[:, d, :], w_raw[:, d, :], ACT.Copy).then_inc(w_hi_done, 1)
                if d == 0:
                    act.wait_ge(const_loaded, 2 * DMA)
                round_h(0, 0, d)
            step(0, 1, 0, first=True)
            with act.Fori(0, (NJ - 2) // 2) as it:
                step(it * 2 + 1, it + 1, 1)
                step(it * 2 + 2, it + 2, 0)
            for c in range(KT):
                stage_z(NJ - 1, c)

        @block.vector
        def _(dve):
            def rows_norm(slot, tiles, count, squares):
                dve.wait_ge(squares_done, squares)
                dve.tensor_scalar(var[:, slot, tiles], sumsq[:, slot, tiles], 1.0 / D, EPS, ALU.mult, ALU.add).then_inc(var_ready, 1)
                dve.wait_ge(std_ready, count + 1)
                refined_rstd(dve, rstd_chain, count * 4, std[:, slot, tiles], var[:, slot, tiles], tmp[:, slot, tiles],
                             rstd[:, slot, tiles])
                for t in range(tiles.start, tiles.stop):
                    dve.tensor_scalar(xin[:, slot, t, :], xin[:, slot, t, :], rstd[:, slot, t:t + 1], None,
                                      ALU.mult).then_inc(xn_ready, 1)

            def norm(j, slot):
                rows_norm(slot, slice(0, 4), j + 3, j * 4 + 4)

            def rest_of_h(j, slot, d):
                dve.wait_ge(h_hi_done, j * KT + d + 1)
                dve.scalar_tensor_tensor(out=h_lo[:, slot, d, :], in0=t_ps[d % 4][:, :], scalar=gain[:, d:d + 1],
                                         in1=h_hi[:, slot, d, :].bitcast(F32), op0=ALU.mult,
                                         op1=ALU.subtract).then_inc(h_ready, 1)

            def step(j, slot):
                norm(j + 1, 1 - slot)
                for d in range(KT):
                    rest_of_h(j + 1, 1 - slot, d)

            dve.memset(warm[:, 0:1], 1.0).then_inc(warm_ready, 1)
            for t in range(4):
                rows_norm(0, slice(t, t + 1), t, t + 1)
            dve.wait_ge(const_loaded, 2 * DMA)
            for d in range(KT):
                dve.wait_ge(w_hi_done, d + 1)
                dve.tensor_tensor(w_lo[:, d, :], w_raw[:, d, :], w_hi[:, d, :].bitcast(F32),
                                  ALU.subtract).then_inc(w_ready, 1)
                rest_of_h(0, 0, d)
            step(0, 0)
            with dve.Fori(0, (NJ - 2) // 2) as it:
                step(it * 2 + 1, 1)
                step(it * 2 + 2, 0)

        @block.tensor
        def _(pe):
            def transposes(j, slot, d, first=False):
                if d == 0:
                    pe.wait_ge(xn_ready, j * 4 + 4)
                if not (first and d < 4):
                    pe.wait_ge(h_ready, j * KT + d - 3)
                for t in range(4):
                    mm = pe.transpose(t_ps[d % 4][:, t * P:(t + 1) * P], xin[:, slot, t, d * P:(d + 1) * P], eye[:, :])
                mm.then_inc(transposed, 1)

            def product(slot, c, d):
                return three_products(pe, z_ps[c % 4][:, :], w_hi[:, d, c * P:(c + 1) * P], w_lo[:, d, c * P:(c + 1) * P],
                                      h_hi[:, slot, d, :], h_lo[:, slot, d, :], d == 0, d == KT - 1)

            def products(j, slot, c):
                pe.wait_ge(z_staged, j * KT + c - 3)
                for d in range(KT):
                    if c == 0:
                        pe.wait_ge(h_ready, j * KT + d + 1)
                    mm = product(slot, c, d)
                mm.then_inc(z_ready, 1)

            def step(j, slot, begin=0):
                before = 4 if begin else 2
                for c in range(begin, max(KT, before + 4)):
                    if c < KT:
                        products(j, slot, c)
                    if 0 <= c - before < 4:
                        transposes(j + 1, 1 - slot, 2 * (c - before))
                        transposes(j + 1, 1 - slot, 2 * (c - before) + 1)

            pe.wait_ge(const_loaded, 2 * DMA)
            for d in range(2):
                transposes(0, 0, d, first=True)
            for d in range(KT):
                if d + 2 < KT:
                    transposes(0, 0, d + 2, first=True)
                pe.wait_ge(h_ready, d + 1)
                pe.wait_ge(w_ready, d + 1)
                for c in range(4):
                    mm = product(0, c, d)
                    if d == KT - 1:
                        mm.then_inc(z_ready, 1)
            step(0, 0, begin=4)
            with pe.Fori(0, (NJ - 2) // 2) as it:
                step(it * 2 + 1, 1)
                step(it * 2 + 2, 0)
            for c in range(KT):
                products(NJ - 1, (NJ - 1) % 2, c)


def mix(nc, ahead, w_out, z_scr, y_scr, w_pool, pool_gain, edge):
    places, TW = table_places()
    top = levels(max(SEQS))
    SMAX = max(SEQS)
    NCOL = 4

    def plan(S):
        lv = levels(S)
        fold_at, at = {}, 0
        for M in lv:
            for part in ("cos", "sin"):
                fold_at[M, part] = at
                at += M // 4 // P
        fold_at[BASE] = at
        n_fold = at + BASE // P
        tiles, need = [], []
        for i, M in enumerate(lv):
            for k, part in enumerate(("cos", "sin")):
                for t in range(M // 4 // P):
                    tiles.append((fold_at[M, part] + t, part))
                    need.append(2 * i + k + 1)
        for part in ("cos", "sin"):
            for t in range(BASE // P):
                tiles.append((fold_at[BASE] + t, part))
                need.append(2 * len(lv) + 1)
        tile_at = {}
        for i, (f, part) in enumerate(tiles):
            M = next((M for M in lv if fold_at[M, part] <= f < fold_at[M, part] + M // 4 // P), BASE)
            tile_at.setdefault((M, part), i)
        groups = [list(range(a, min(a + NCOL, len(tiles)))) for a in range(0, len(tiles), NCOL)]
        return {
            "levels": lv, "fold_at": fold_at, "n_fold": n_fold, "tiles": tiles, "groups": groups, "tile_at": tile_at,
            "need": [max(need[t] for t in g) for g in groups],
            "early": 2 * (S // 4 // P) // NCOL,
            "stages": len(lv) + 1,
            "folds": 2 * len(lv) + 1,
            "chain": 2 * len(lv) - 1,
        }

    plans = [plan(S) for S in SEQS]
    UV = max(len(p["tiles"]) for p in plans)
    NF = max(p["n_fold"] for p in plans)
    CREDIT = 4
    ch0 = [0, HEADS * len(plans[0]["groups"])]
    fold0 = [0, HEADS * plans[0]["folds"]]
    chain0 = [0, HEADS * plans[0]["chain"]]
    stage0 = [CREDIT, CREDIT + HEADS * plans[0]["stages"]]
    tok0 = [0, SEQS[0]]
    chunk0 = [0, HEADS * SEQS[0] // HALF]
    edge_at = [sum(WINDOWS[:g]) for g in range(4)]
    inverse_at = sum(WINDOWS)
    ORDER = (3, 2, 1, 0)
    POOLED = len(ORDER) - 1
    chunks = [(q, g, c) for q, S in enumerate(SEQS) for g in ORDER for c in range(S // HALF)]
    BEGIN = 2
    PER_HEAD = len(chunks) // (2 * HEADS - BEGIN)

    def chunks_of(q, h):
        n = (q * HEADS + h - BEGIN) * PER_HEAD
        return range(n, n + PER_HEAD) if n >= 0 else range(0)
    bounds = [places[top[0], "cos"], places[top[0], "sin"], places[top[1], "cos"], places[top[2], "cos"], TW]
    parts = [slice(a, b) for a, b in zip(bounds, bounds[1:])]

    with ExitStack() as ctx:
        def sb(name, shape, dt=F32):
            return ctx.enter_context(nc.sbuf_tensor(name, shape, dt))

        def sem(name):
            return ctx.enter_context(nc.semaphore(name))

        ahead.reserve(ctx, "mix", 4 * HEADS * SMAX)
        ahead.reserve_top(ctx, "mix", ahead.yb_bytes)
        tab_lo, tab_raw, tab_loaded = ahead.tab_lo, ahead.tab_raw, ahead.tab_loaded
        tab_hi = sb("tab_hi", [P, TW], F32R)
        zys = [ahead.zy, ahead.zy1]
        folds = sb("folds", [P, NF, P])
        scratch = sb("scratch", [P, SMAX - BASE + SMAX // 2 + 1])
        sums, diff = scratch[:, :SMAX - BASE], scratch[:, SMAX - BASE:]
        uv_hi = sb("uv_hi", [P, UV, P], F32R)
        uv_lo = sb("uv_lo", [P, UV, P], F32R)
        sine_part = sb("sine_part", [P, 2, SMAX // 4])
        chan, wf, chan_loaded = ahead.chan, ahead.wf, ahead.chan_loaded
        chan_w = sb("chan_w", [P, 2, HEADS, P])
        wp = sb("wp", [P, 4, P])
        pg = sb("pg", [P, 4])
        edges = sb("edges", [P, sum(WINDOWS) + 4])
        zb = sb("zb", [P, 4, PAD + SMAX + PAD])
        win = [sb(f"win{i}", [P, PAD + SMAX + PAD]) for i in range(2)]
        yb = ahead.yb
        ch_ps = [ctx.enter_context(nc.psum_tensor(f"ch_ps{i}", [P, NCOL, P], F32)) for i in range(2)]
        cos_ps = [ctx.enter_context(nc.psum_tensor(f"cos_ps{i}", [P, SMAX // 4], F32)) for i in range(2)]
        sin_ps = [ctx.enter_context(nc.psum_tensor(f"sin_ps{i}", [P, SMAX // 4], F32)) for i in range(2)]
        base_ps = [sin_ps[len(p["levels"]) % 2][:, 0:BASE] for p in plans]
        yb_ps = [ctx.enter_context(nc.psum_tensor(f"yb_ps{i}", [P, HALF], F32)) for i in range(2)]

        pool_w_loaded = sem("pool_w_loaded")
        tab_hi_done = sem("tab_hi_done")
        tab_ready = sem("tab_ready")
        tab_by_pool = sem("tab_by_pool")
        chan_w_ps_ready = sem("chan_w_ps_ready")
        chan_w_ready = sem("chan_w_ready")
        z_loaded = [ahead.z_loaded] + [sem(f"zh_loaded{i}") for i in range(1, 2 * HEADS)]
        zb_loaded = [sem(f"zb_loaded{i}") for i in range(4)]
        zeroed = sem("zeroed")
        fold_chain = sem("fold_chain")
        fold_done = sem("fold_done")
        ch_ready = sem("ch_ready")
        uv_hi_done = sem("uv_hi_done")
        uv_ready = sem("uv_ready")
        cos_sin_ready = sem("cos_sin_ready")
        sine_copied = sem("sine_copied")
        stage_done = sem("stage_done")
        y_stored = ahead.y_stored
        pool_chain = sem("pool_chain")
        d_by_pool = sem("d_by_pool")
        pooled = sem("pooled")
        yb_ready = sem("yb_ready")
        yb_staged = sem("yb_staged")
        yb_stored = ahead.yb_stored

        block = ctx.enter_context(nc.Block())

        @block.sync
        def _(sp):
            def load_head(q, h):
                S = SEQS[q]
                sp.dma_start(zys[q][:, h * S:(h + 1) * S], z_scr[h, :, tok0[q]:tok0[q] + S]).then_inc(z_loaded[q * HEADS + h], DMA)

            def load_group(q, g):
                S = SEQS[q]
                sp.dma_start(zb[:, g, PAD:PAD + S], z_scr[HEADS + g, :, tok0[q]:tok0[q] + S]).then_inc(zb_loaded[g], DMA)

            load_group(0, 3)
            load_head(0, 1)
            sp.dma_start(wp[:, :, :], w_pool.rearrange("g c d -> c g d")).then_inc(pool_w_loaded, DMA)
            sp.dma_start(pg[:, :], pool_gain).then_inc(pool_w_loaded, DMA)
            sp.dma_start(edges[:, :], edge).then_inc(pool_w_loaded, DMA)
            load_head(0, 2)
            load_head(0, 3)
            for g in (2, 0, 1):
                load_group(0, g)
            for s in range(4):
                sp.wait_ge(ahead.z_stored[s], 2 * TOKENS // HALF * DMA)
            for h in range(HEADS):
                load_head(1, h)
            for q, S in enumerate(SEQS):
                for h in range(HEADS):
                    done = q * HEADS + h
                    if 0 < done <= HEADS:
                        sp.wait_ge(y_stored[0], done * DMA)
                        for d in range((done - 1) * KT // HEADS, done * KT // HEADS):
                            sp.dma_start(ahead.w_out_raw[:, d, :], w_out[d * P:(d + 1) * P, :]).then_inc(ahead.w_out_loaded[d], DMA)
                    for n in chunks_of(q, h):
                        of, g, c = chunks[n]
                        at = tok0[of] + c * HALF
                        sp.wait_ge(yb_staged, n + 1)
                        sp.dma_start(y_scr[HEADS + g, :, at:at + HALF], yb[:, n % 4, :]).then_inc(yb_stored[n % 4], DMA)
                        if 0 <= n - chunk0[1] < 4:
                            t = slice((n - chunk0[1]) * P, (n - chunk0[1] + 1) * P)
                            sp.dma_start(ahead.y_raw[:, :, t], y_scr[:, :, t].rearrange("c p s -> p c s")).then_inc(ahead.y_loaded, DMA)
                        if of == 0 and c == SEQS[0] // HALF - 1:
                            load_group(1, g)
                        if n == chunk0[1] - 1:
                            for i in range(4):
                                sp.wait_ge(yb_stored[i], chunk0[1] // 4 * DMA)
                    sp.wait_ge(stage_done, (h + 1) * plans[q]["stages"] + stage0[q])
                    sp.dma_start(y_scr[h, :, tok0[q]:tok0[q] + S], zys[q][:, h * S:(h + 1) * S]).then_inc(y_stored[q], DMA)

        @block.gpsimd
        def _(pool):
            chained = 0

            def chain(ins):
                nonlocal chained
                chained += 1
                ins.then_inc(pool_chain, 1)
                pool.wait_ge(pool_chain, chained)

            def group(q, g):
                S, k, e = SEQS[q], WINDOWS[g], edge_at[g]
                pool.wait_ge(zb_loaded[g], (q + 1) * DMA)
                if q or g != ORDER[0]:
                    pool.wait_ge(d_by_pool, POOLED * q + ORDER.index(g))
                src, lo, hi = zb[:, g, :], PAD - k // 2 + 1, PAD + S + k // 2 - 1
                chain(pool.tensor_tensor(win[0][:, lo:hi], src[:, lo - 1:hi - 1], src[:, lo:hi], ALU.add))
                n, a = 2, 0
                while n < k:
                    lo, hi = lo + n // 2, hi - n // 2
                    chain(pool.tensor_tensor(win[1 - a][:, lo:hi], win[a][:, lo - n // 2:hi - n // 2],
                                             win[a][:, lo + n // 2:hi + n // 2], ALU.add))
                    n, a = 2 * n, 1 - a
                s = win[a][:, PAD:PAD + S]
                z = src[:, PAD:PAD + S]
                inverse = edges[:, inverse_at + g:inverse_at + g + 1].to_broadcast([P, S - k])
                pool.tensor_tensor(s[:, k // 2:S - k // 2], s[:, k // 2:S - k // 2], inverse, ALU.mult)
                pool.tensor_tensor(s[:, :k // 2], s[:, :k // 2], edges[:, e:e + k // 2], ALU.mult)
                chain(pool.tensor_tensor(s[:, S - k // 2:], s[:, S - k // 2:], edges[:, e + k // 2:e + k], ALU.mult))
                pool.tensor_tensor(z, s, z, ALU.subtract).then_inc(d_by_pool, 1)

            pool.memset(diff[:, SMAX // 2:], 0.0).then_inc(zeroed, 1)
            for g in range(4):
                pool.memset(zb[:, g, 0:PAD], 0.0).then_inc(zeroed, 1)
                pool.memset(zb[:, g, PAD + SEQS[0]:PAD + SEQS[0] + PAD], 0.0).then_inc(zeroed, 1)
            for part, rounded in ((1, 1), (3, 4)):
                pool.wait_ge(tab_hi_done, rounded)
                pool.tensor_tensor(tab_lo[:, parts[part]], tab_raw[:, parts[part]], tab_hi[:, parts[part]].bitcast(F32),
                                   ALU.subtract).then_inc(tab_by_pool, 1)
            pool.wait_ge(zeroed, 9)
            pool.wait_ge(pool_w_loaded, 3 * DMA)
            for g in ORDER[:POOLED]:
                group(0, g)
            for i, g in enumerate(ORDER):
                pool.wait_ge(yb_ready, (i + 1) * (SEQS[0] // HALF))
                pool.memset(zb[:, g, PAD + SEQS[1]:PAD + SEQS[1] + PAD], 0.0).then_inc(zeroed, 1)
                if i < POOLED:
                    pool.wait_ge(zeroed, 9 + i + 1)
                    group(1, g)

        @block.scalar
        def _(act):
            def round_table(part):
                act.activation(tab_hi[:, parts[part]], tab_raw[:, parts[part]], ACT.Copy).then_inc(tab_hi_done, 1)

            act.wait_ge(tab_loaded, DMA)
            round_table(1)
            act.wait_ge(chan_w_ps_ready, 1)
            for part in range(2):
                act.activation(chan_w[:, part, :, :], ch_ps[part][:, :, :], ACT.Copy).then_inc(chan_w_ready, 1)
            round_table(0)
            for q, S in enumerate(SEQS):
                p = plans[q]
                G, L = len(p["groups"]), len(p["levels"])

                def round_uv(r, h, g):
                    act.wait_ge(ch_ready, h * len(plans[r]["groups"]) + (ch0[r] + g + 1))
                    ts = plans[r]["groups"][g]
                    act.activation(uv_hi[:, ts[0]:ts[-1] + 1, :], ch_ps[g % 2][:, 0:len(ts), :], ACT.Copy).then_inc(uv_hi_done, 1)

                def copy_sine(h, level):
                    n = p["levels"][level] // 4
                    act.wait_ge(cos_sin_ready, h * p["stages"] + (stage0[q] - CREDIT + level + 1))
                    act.wait_ge(stage_done, h * p["stages"] + (stage0[q] + level - 1))
                    act.activation(sine_part[:, level % 2, 0:n], sin_ps[level % 2][:, 0:n], ACT.Copy,
                                   scale=float(S) ** -0.5).then_inc(sine_copied, 1)

                def body(h, following):
                    r, nxt = following or (q, h)
                    early = plans[r]["early"]
                    staged = iter(chunks_of(q, h) if isinstance(h, int) else ())

                    def stage_yb():
                        n = next(staged, None)
                        if n is None:
                            return
                        act.wait_ge(yb_ready, n + 1)
                        if n >= 4:
                            act.wait_ge(yb_stored[n % 4], n // 4 * DMA)
                        g = chunks[n][1]
                        act.activation(yb[:, n % 4, :], yb_ps[n % 2][:, :], ACT.Identity, scale=pg[:, g:g + 1]).then_inc(yb_staged, 1)

                    copy_sine(h, 0)
                    if following:
                        for g in range(early):
                            round_uv(r, nxt, g)
                    stage_yb()
                    for level in range(1, L):
                        copy_sine(h, level)
                    if following:
                        for g in range(early, len(plans[r]["groups"])):
                            round_uv(r, nxt, g)
                    for _ in range(PER_HEAD - 1):
                        stage_yb()

                if q == 0:
                    for g in range(G):
                        round_uv(0, 0, g)
                        if g in (1, 2):
                            round_table(g + 1)
                    act.wait_ge(pool_w_loaded, 3 * DMA)
                    with act.Fori(0, BEGIN) as h:
                        body(h, (q, h + 1))
                for h in range(0 if q else BEGIN, HEADS - 1):
                    body(h, (q, h + 1))
                body(HEADS - 1, None if q else (1, 0))

        @block.vector
        def _(dve):
            dve.sem_inc(stage_done, CREDIT)

            def fold(q, h):
                S, p = SEQS[q], plans[q]
                G, L, fold_at = len(p["groups"]), len(p["levels"]), p["fold_at"]
                static = isinstance(h, int) and h == 0
                first = static and q == 0
                gidx = {}
                for g, ts in enumerate(p["groups"]):
                    for t in ts:
                        gidx[p["tiles"][t][0]] = g

                def tiles_read(last_tile):
                    if static:
                        dve.wait_ge(ch_ready, ch0[q])
                    else:
                        dve.wait_ge(ch_ready, (h - 1) * G + (ch0[q] + gidx[last_tile] + 1))

                src = zys[q][:, bass.ds(h * S, S)]
                chain = h * p["chain"] + chain0[q]
                steps = 0
                out = 0
                for level, M in enumerate(p["levels"]):
                    n, m = M // 2, M // 4
                    last = level == L - 1
                    d = diff[:, SMAX // 2 - n:SMAX // 2 + 1]
                    if level or not first:
                        dve.wait_ge(fold_done, h * p["folds"] + (fold0[q] + 2 * level))
                    dve.tensor_tensor(d[:, 0:n], src[:, 0:n], src[:, n:M], ALU.subtract).then_inc(fold_chain, 1)
                    if last:
                        dst = folds[:, fold_at[BASE]:fold_at[BASE] + BASE // P, :].rearrange("p a b -> p (a b)")
                    else:
                        dst = sums[:, out:out + n]
                        dve.tensor_tensor(dst, src[:, 0:n], src[:, n:M], ALU.add).then_inc(fold_chain, 1)
                    dve.wait_ge(fold_chain, chain + steps + 1)
                    for k, part in enumerate(("cos", "sin")):
                        f = fold_at[M, part]
                        if not first:
                            tiles_read(f + m // P - 1)
                        o = folds[:, f:f + m // P, :].rearrange("p a b -> p (a b)")
                        if k == 0:
                            dve.tensor_tensor(o, d[:, 0:m], d[:, n:n - m:-1], ALU.subtract).then_inc(fold_done, 1)
                        else:
                            dve.tensor_tensor(o, d[:, 1:m + 1], d[:, n - 1:n - m - 1:-1], ALU.add).then_inc(fold_done, 1)
                    if last:
                        if not first:
                            tiles_read(max(gidx))
                        dve.tensor_tensor(dst, src[:, 0:n], src[:, n:M], ALU.add).then_inc(fold_done, 1)
                    else:
                        dve.wait_ge(fold_chain, chain + steps + 2)
                        src, out, steps = dst, out + n, steps + 2

            def rest_of_uv(q, h, g):
                p = plans[q]
                dve.wait_ge(uv_hi_done, h * len(p["groups"]) + (ch0[q] + g + 1))
                ts = p["groups"][g]
                dve.tensor_tensor(uv_lo[:, ts[0]:ts[-1] + 1, :], ch_ps[g % 2][:, 0:len(ts), :],
                                  uv_hi[:, ts[0]:ts[-1] + 1, :].bitcast(F32), ALU.subtract).then_inc(uv_ready, 1)

            def outputs(q, h, level):
                S, L, M = SEQS[q], len(plans[q]["levels"]), plans[q]["levels"][level]
                m, step = M // 4, S // M
                y = zys[q][:, bass.ds(h * S, S)]
                dve.wait_ge(sine_copied, h * L + (q * HEADS * len(plans[0]["levels"]) + level + 1))
                dve.scalar_tensor_tensor(out=y[:, step:step + 2 * step * m:2 * step], in0=cos_ps[level % 2][:, 0:m],
                                         scalar=float(S) ** -0.5, in1=sine_part[:, level % 2, 0:m],
                                         op0=ALU.mult, op1=ALU.subtract)
                dve.scalar_tensor_tensor(out=y[:, S // 2 + step:S:2 * step], in0=cos_ps[level % 2][:, m - 1::-1],
                                         scalar=float(S) ** -0.5, in1=sine_part[:, level % 2, m - 1::-1],
                                         op0=ALU.mult, op1=ALU.add).then_inc(stage_done, 1)

            def base_outputs(q, h):
                S, p = SEQS[q], plans[q]
                dve.wait_ge(cos_sin_ready, h * p["stages"] + (stage0[q] - CREDIT + p["stages"]))
                y = zys[q][:, bass.ds(h * S, S)]
                dve.tensor_scalar(y[:, 0:S:S // BASE], base_ps[q], float(S) ** -0.5, None,
                                  ALU.mult).then_inc(stage_done, 1)

            def body(q, h, following=None, fold_next=None):
                outputs(q, h, 0)
                if following:
                    r, nxt = following
                    for g in range(plans[r]["early"]):
                        rest_of_uv(r, nxt, g)
                for level in range(1, len(plans[q]["levels"])):
                    outputs(q, h, level)
                if following:
                    for g in range(plans[r]["early"], len(plans[r]["groups"])):
                        rest_of_uv(r, nxt, g)
                base_outputs(q, h)
                if fold_next:
                    fold(*fold_next)

            def group_piece(q, k, folded):
                S, g = SEQS[q], ORDER[-1]
                a, b = k * S // 2, (k + 1) * S // 2
                steps = 6 * q + 3 * (1 - k)
                if k:
                    dve.wait_ge(zb_loaded[g], (q + 1) * DMA)
                    dve.wait_ge(zeroed, 9)
                    dve.wait_ge(pool_w_loaded, 3 * DMA)
                dve.wait_ge(fold_done, folded)
                z = zb[:, g, PAD:PAD + S]
                pairs = scratch[:, 0:b - a]
                dve.tensor_tensor(pairs, zb[:, g, PAD + a - 1:PAD + b - 1], z[:, a:b], ALU.add).then_inc(pooled, 1)
                dve.wait_ge(pooled, steps + 1)
                t = k * (S - 1)
                end = pairs[:, t - a:t - a + 1]
                e = edge_at[g] + k
                dve.tensor_tensor(end, end, edges[:, e:e + 1], ALU.mult).then_inc(pooled, 1)
                inner = slice(a + 1 - k, b - k)
                dve.scalar_tensor_tensor(out=z[:, inner], in0=pairs[:, 1 - k:b - a - k], scalar=0.5, in1=z[:, inner],
                                         op0=ALU.mult, op1=ALU.subtract)
                dve.wait_ge(pooled, steps + 2)
                dve.tensor_tensor(z[:, t:t + 1], end, z[:, t:t + 1], ALU.subtract).then_inc(pooled, 1)
                dve.wait_ge(pooled, steps + 3)

            dve.wait_ge(zeroed, 1)
            dve.wait_ge(z_loaded[0], DMA)
            fold(0, 0)
            for g in range(len(plans[0]["groups"])):
                rest_of_uv(0, 0, g)
                if g in (1, 2):
                    dve.wait_ge(tab_hi_done, g + 1)
                    part = parts[0 if g == 1 else 2]
                    dve.tensor_tensor(tab_lo[:, part], tab_raw[:, part], tab_hi[:, part].bitcast(F32),
                                      ALU.subtract).then_inc(tab_ready, 1)
            dve.wait_ge(z_loaded[1], DMA)
            fold(0, 1)
            for h in (2, 3):
                dve.wait_ge(z_loaded[h], DMA)
            with dve.Fori(0, HEADS - 2) as h:
                body(0, h, (0, h + 1), (0, h + 2))
            for h in range(HEADS):
                dve.wait_ge(z_loaded[HEADS + h], DMA)
            body(0, HEADS - 2, (0, HEADS - 1), (1, 0))
            body(0, HEADS - 1, (1, 0), (1, 1))
            group_piece(0, 1, fold0[1] + 2 * plans[1]["folds"])
            body(1, 0, (1, 1), (1, 2))
            group_piece(0, 0, fold0[1] + 3 * plans[1]["folds"])
            body(1, 1, (1, 2), (1, 3))
            body(1, 2, (1, 3))
            for k in (1, 0):
                group_piece(1, k, fold0[1] + HEADS * plans[1]["folds"])
            body(1, HEADS - 1)

        @block.tensor
        def _(pe):
            pe.wait_ge(chan_loaded, 2 * DMA)
            for part in range(2):
                for h in range(HEADS):
                    mm = pe.matmul(ch_ps[part][:, h, :], chan[:, part, :], wf[:, h, :], start=True, stop=True)
            mm.then_inc(chan_w_ps_ready, 1)
            pe.wait_ge(chan_w_ready, 2)

            def chan_w_of(h, part):
                return chan_w[:, ("cos", "sin").index(part), bass.ds(h, 1), :].rearrange("p a b -> p (a b)")

            def channel_products(q, h, g, first=False):
                p = plans[q]
                G = len(p["groups"])
                pe.wait_ge(fold_done, h * p["folds"] + (fold0[q] + p["need"][g]))
                if g >= 2:
                    pe.wait_ge(uv_ready, h * G + (ch0[q] + g - 1))
                elif not first:
                    pe.wait_ge(uv_ready, h * G + ch0[q])
                for i, t in enumerate(p["groups"][g]):
                    f, part = p["tiles"][t]
                    mm = pe.matmul(ch_ps[g % 2][:, i, :], folds[:, f, :], chan_w_of(h, part), start=True, stop=True)
                mm.then_inc(ch_ready, 1)

            def transform(p, out, M, part, width, rows, first, last):
                for r in range(rows):
                    t = p["tile_at"][M, part] + r
                    a = places[M, part] + r * width
                    mm = three_products(pe, out, uv_hi[:, t, :], uv_lo[:, t, :], tab_hi[:, a:a + width], tab_lo[:, a:a + width],
                                        first and r == 0, last and r == rows - 1)
                return mm

            def level_products(q, h, level):
                p = plans[q]
                M = p["levels"][level]
                m = M // 4
                if q == 0:
                    if level < 2:
                        pe.wait_ge(tab_ready, level + 1)
                    if level != 1:
                        pe.wait_ge(tab_by_pool, 1 + level // 2)
                pe.wait_ge(stage_done, h * p["stages"] + (stage0[q] + level - 1))
                transform(p, cos_ps[level % 2][:, 0:m], M, "cos", m, m // P, True, True)
                if level == 0:
                    pe.wait_ge(stage_done, h * p["stages"] + stage0[q])
                transform(p, sin_ps[level % 2][:, 0:m], M, "sin", m, m // P, True, True).then_inc(cos_sin_ready, 1)

            def base_products(q, h):
                p = plans[q]
                pe.wait_ge(stage_done, h * p["stages"] + (stage0[q] + len(p["levels"]) - 1))
                transform(p, base_ps[q], BASE, "cos", BASE, BASE // P, True, False)
                transform(p, base_ps[q], BASE, "sin", BASE, BASE // P, False, True).then_inc(cos_sin_ready, 1)

            def body(q, h, following):
                p = plans[q]
                G = len(p["groups"])
                spread = iter(chunks_of(q, h) if isinstance(h, int) else ())
                pe.wait_ge(uv_ready, h * G + (ch0[q] + p["early"]))
                level_products(q, h, 0)
                if following:
                    r, nxt = following
                    for g in range(plans[r]["early"]):
                        channel_products(r, nxt, g)
                group_product(next(spread, None))
                pe.wait_ge(uv_ready, h * G + (ch0[q] + G))
                for level in range(1, len(p["levels"])):
                    level_products(q, h, level)
                base_products(q, h)
                if following:
                    for g in range(plans[r]["early"], len(plans[r]["groups"])):
                        channel_products(r, nxt, g)
                for _ in range(PER_HEAD - 1):
                    group_product(next(spread, None))

            def group_product(n):
                if n is None:
                    return
                q, g, c = chunks[n]
                if n == 0:
                    pe.wait_ge(pool_w_loaded, 3 * DMA)
                elif n >= 2:
                    pe.wait_ge(yb_staged, n - 1)
                if c == 0:
                    if g == ORDER[-1]:
                        pe.wait_ge(pooled, 6 * q + 6)
                    else:
                        pe.wait_ge(d_by_pool, POOLED * q + ORDER.index(g) + 1)
                pe.matmul(yb_ps[n % 2][:, :], wp[:, g, :], zb[:, g, PAD + c * HALF:PAD + (c + 1) * HALF],
                          start=True, stop=True).then_inc(yb_ready, 1)

            for g in range(len(plans[0]["groups"])):
                channel_products(0, 0, g, first=True)
            with pe.Fori(0, BEGIN) as h:
                body(0, h, (0, h + 1))
            for h in range(BEGIN, HEADS - 1):
                body(0, h, (0, h + 1))
            body(0, HEADS - 1, (1, 0))
            for h in range(HEADS - 1):
                body(1, h, (1, h + 1))
            body(1, HEADS - 1, None)


def project_out(nc, ahead, y_scr, x, ident, w_gate, w_up, g2, x1_scr, h2_scr):
    NT = TOKENS // P
    EARLY = 2
    with ExitStack() as ctx:
        def sb(name, shape, dt=F32):
            return ctx.enter_context(nc.sbuf_tensor(name, shape, dt))

        def sem(name):
            return ctx.enter_context(nc.semaphore(name))

        ahead.reserve(ctx, "project_out", 4 * KT * D)
        ahead.reserve_top(ctx, "project_out", ahead.top_bytes)
        w_hi = sb("wout_hi", [P, KT, D], F32R)
        w_lo, w_raw, y_raw = ahead.w_out_lo, ahead.w_out_raw, ahead.y_raw
        y_hi = sb("y_hi", [P, 4, KT, P], F32R)
        y_lo = sb("y_lo", [P, 4, KT, P], F32R)
        x1, h_out = ahead.x1, ahead.h_out
        xn = sb("xn", [P, 2, D])
        junk = sb("junk3", [P, D])
        eye = sb("eye3", [P, P])
        sumsq = sb("sumsq3", [P, 4])
        var = sb("var3", [P, 4])
        std = sb("std3", [P, 4])
        tmp = sb("tmp3", [P, 4])
        rstd = sb("rstd3", [P, 4])
        o_ps = [ctx.enter_context(nc.psum_tensor(f"o_ps{i}", [P, HALF], F32)) for i in range(4)]
        t_ps = [ctx.enter_context(nc.psum_tensor(f"t3_ps{i}", [P, 4, P], F32)) for i in range(4)]

        const_loaded = sem("const_loaded3")
        w_loaded, y_loaded = ahead.w_out_loaded, ahead.y_loaded
        w_hi_done = sem("wout_hi_done")
        w_ready = sem("wout_ready")
        x_loaded = [sem(f"x3_loaded{i}") for i in range(4)]
        early_y_hi_done = sem("early_y_hi_done")
        early_y_ready = sem("early_y_ready")
        y_hi_done = sem("y_hi_done")
        y_ready = sem("y_ready")
        o_ready_half = sem("o_ready_half")
        x1_ready = sem("x1_ready")
        squares_done = sem("squares_done3")
        var_ready = sem("var_ready3")
        std_ready = sem("std_ready3")
        rstd_chain = sem("rstd_chain3")
        xn_ready = sem("xn_ready3")
        transposed = sem("transposed3")
        h_staged = sem("h_staged3")
        x1_stored, h_stored = ahead.x1_stored, ahead.h_stored

        block = ctx.enter_context(nc.Block())

        @block.sync
        def _(sp):
            def load_y(j):
                sp.dma_start(y_raw[:, :, :], y_scr[:, :, bass.ds(j * HALF, HALF)].rearrange("c p s -> p c s")).then_inc(y_loaded, DMA)

            def load_x(j, t):
                sp.dma_start(x1[:, t, :], x[bass.ds(j * HALF + t * P, P), :]).then_inc(x_loaded[t], DMA)

            def store_x1(j, t):
                sp.wait_ge(xn_ready, j * 4 + (t + 1))
                sp.dma_start(x1_scr[bass.ds(j * HALF + t * P, P), :], x1[:, t, :]).then_inc(x1_stored[t], DMA)

            def store_h(m, slot):
                sp.wait_ge(h_staged, m * 2 + 2)
                sp.dma_start(h2_scr[:, :, bass.ds(m * P, P)].rearrange("d p s -> p d s"), h_out[:, slot, :, :]).then_inc(h_stored[slot], DMA)

            sp.dma_start(eye[:, :], ident).then_inc(const_loaded, DMA)
            sp.wait_ge(ahead.y_stored[1], HEADS * DMA)
            for t in range(4):
                load_x(0, t)
            for s in range(4):
                sp.wait_ge(ahead.yb_stored[s], HEADS * TOKENS // HALF // 4 * DMA)
            def step(j, t, more):
                if more and t == 0:
                    sp.wait_ge(y_ready, (j + 1) * 4)
                    load_y(j + 1)
                store_x1(j, t)
                if t or not (isinstance(j, int) and j == 0):
                    store_h(j * 4 + (t - 1), (t + 3) % 4)
                if more and t:
                    sp.wait_ge(x1_stored[t - 1], (j + 1) * DMA)
                    load_x(j + 1, t - 1)
                if more and t == 3:
                    sp.wait_ge(x1_stored[3], (j + 1) * DMA)
                    load_x(j + 1, 3)

            for t in range(4):
                step(0, t, True)
            with sp.Fori(1, NT // 4 - 1) as j:
                for t in range(4):
                    step(j, t, True)
            sp.dma_start(ahead.gain2[:, :], g2).then_inc(ahead.gain2_loaded, DMA)
            for i, w in enumerate((w_gate, w_up, w_gate)):
                sp.dma_start(ahead.w_raw[i][:, :], w[i // 2]).then_inc(ahead.w_loaded[i], DMA)
            for t in range(4):
                sp.wait_ge(h_stored[t], DMA)
            sp.dma_start(ahead.h2_raw[:, :, :], h2_scr[:, :, 0:HALF].rearrange("d p s -> p d s")).then_inc(ahead.h2_loaded, DMA)
            for t in range(4):
                step(NT // 4 - 1, t, False)
            store_h(NT - 1, 3)

        @block.scalar
        def _(act):
            def round_y(j, t, first=False):
                act.wait_ge(y_loaded, (j + 4) * DMA)
                if not first:
                    act.wait_ge(o_ready_half, j * 8 + 2 * (t - 3))
                act.activation(y_hi[:, t, :, :], y_raw[:, :, t * P:(t + 1) * P], ACT.Copy).then_inc(y_hi_done, 1)

            def norm(n, t):
                act.wait_ge(x1_ready, n * 2 + 2)
                act.activation(junk[:, :], x1[:, t, :], ACT.Square, accum_out=sumsq[:, t:t + 1]).then_inc(squares_done, 1)
                act.wait_ge(var_ready, n + 1)
                act.activation(std[:, t:t + 1], var[:, t:t + 1], ACT.Sqrt).then_inc(std_ready, 1)

            def stage_h(m, slot, stored=None):
                for k in range(2):
                    act.wait_ge(transposed, m * 2 + (k + 1))
                    if k == 0 and stored is not None:
                        act.wait_ge(h_stored[slot], stored)
                    act.activation(h_out[:, slot, 4 * k:4 * k + 4, :], t_ps[(slot % 2) * 2 + k][:, :, :], ACT.Copy).then_inc(h_staged, 1)

            def step(j, t, lead=True, first=False):
                n = j * 4 + t
                if lead:
                    round_y(j + (t + 2) // 4, (t + 2) % 4, first=first and t < 2)
                if not (first and t == 0):
                    norm(n - 1, (t + 3) % 4)
                    uses = j if t else j - 1
                    stage_h(n - 1, (t + 3) % 4, None if isinstance(uses, int) and uses < 1 else uses * DMA)

            for d in range(KT):
                if d == 0:
                    act.wait_ge(y_loaded, 4 * DMA)
                    act.activation(y_hi[:, 0, :EARLY, :], y_raw[:, :EARLY, 0:P], ACT.Copy).then_inc(early_y_hi_done, 1)
                act.wait_ge(w_loaded[d], DMA)
                act.activation(w_hi[:, d, :], w_raw[:, d, :], ACT.Copy).then_inc(w_hi_done, 1)
                if d == 0:
                    act.activation(y_hi[:, 0, EARLY:, :], y_raw[:, EARLY:, 0:P], ACT.Copy).then_inc(y_hi_done, 1)
            round_y(0, 1, first=True)
            for s in range(4):
                act.wait_ge(ahead.yb_stored[s], HEADS * TOKENS // HALF // 4 * DMA)
            for t in range(4):
                step(0, t, first=True)
            for t in range(4):
                step(1, t)
            with act.Fori(2, NT // 4 - 1) as j:
                for t in range(4):
                    step(j, t)
            for t in range(4):
                step(NT // 4 - 1, t, lead=t < 2)
            norm(NT - 1, 3)
            stage_h(NT - 1, 3, (NT // 4 - 1) * DMA)

        @block.vector
        def _(dve):
            def rest_of_y(j, t):
                dve.wait_ge(y_hi_done, j * 4 + (t + 1))
                dve.tensor_tensor(y_lo[:, t, :, :], y_raw[:, :, t * P:(t + 1) * P], y_hi[:, t, :, :].bitcast(F32),
                                  ALU.subtract).then_inc(y_ready, 1)

            def residual(m, slot, loads):
                dve.wait_ge(x_loaded[slot], loads)
                for c in range(2):
                    dve.wait_ge(o_ready_half, m * 2 + (c + 1))
                    dve.tensor_tensor(x1[:, slot, c * HALF:(c + 1) * HALF], o_ps[(slot % 2) * 2 + c][:, :],
                                      x1[:, slot, c * HALF:(c + 1) * HALF], ALU.add).then_inc(x1_ready, 1)
                dve.wait_ge(squares_done, m + 1)
                one = slice(slot, slot + 1)
                dve.tensor_scalar(var[:, one], sumsq[:, one], 1.0 / D, EPS, ALU.mult, ALU.add).then_inc(var_ready, 1)
                dve.wait_ge(std_ready, m + 1)
                refined_rstd(dve, rstd_chain, m * 4, std[:, one], var[:, one], tmp[:, one], rstd[:, one])
                dve.tensor_scalar(xn[:, slot % 2, :], x1[:, slot, :], rstd[:, one], None, ALU.mult).then_inc(xn_ready, 1)

            def step(j, t, lead=True, first=False):
                if lead:
                    rest_of_y(j + (t + 2) // 4, (t + 2) % 4)
                if not (first and t == 0):
                    residual(j * 4 + (t - 1), (t + 3) % 4, (j + 1) * DMA if t else j * DMA)

            dve.wait_ge(early_y_hi_done, 1)
            dve.tensor_tensor(y_lo[:, 0, :EARLY, :], y_raw[:, :EARLY, 0:P], y_hi[:, 0, :EARLY, :].bitcast(F32),
                              ALU.subtract).then_inc(early_y_ready, 1)
            for d in range(KT):
                dve.wait_ge(w_hi_done, d + 1)
                dve.tensor_tensor(w_lo[:, d, :], w_raw[:, d, :], w_hi[:, d, :].bitcast(F32),
                                  ALU.subtract).then_inc(w_ready, 1)
                if d == 0:
                    dve.wait_ge(y_hi_done, 1)
                    dve.tensor_tensor(y_lo[:, 0, EARLY:, :], y_raw[:, EARLY:, 0:P], y_hi[:, 0, EARLY:, :].bitcast(F32),
                                      ALU.subtract).then_inc(y_ready, 1)
            rest_of_y(0, 1)
            for t in range(4):
                step(0, t, first=True)
            with dve.Fori(1, NT // 4 - 1) as j:
                for t in range(4):
                    step(j, t)
            for t in range(4):
                step(NT // 4 - 1, t, lead=t < 2)
            residual(NT - 1, 3, NT // 4 * DMA)

        @block.tensor
        def _(pe):
            def product(t, c, d):
                return three_products(pe, o_ps[(t % 2) * 2 + c][:, :], y_hi[:, t, d, :], y_lo[:, t, d, :],
                                      w_hi[:, d, c * HALF:(c + 1) * HALF], w_lo[:, d, c * HALF:(c + 1) * HALF],
                                      d == 0, d == KT - 1)

            def products(n, t, first=False):
                if first and t == 0:
                    pe.wait_ge(early_y_ready, 1)
                    for d in range(KT):
                        if d == EARLY:
                            pe.wait_ge(y_ready, 1)
                        pe.wait_ge(w_ready, d + 1)
                        for c in range(2):
                            mm = product(t, c, d)
                            if d == KT - 1:
                                mm.then_inc(o_ready_half, 1)
                    return
                pe.wait_ge(y_ready, n + 1)
                for c in range(2):
                    if not (first and t < 2):
                        pe.wait_ge(x1_ready, n * 2 + (c - 3))
                    for d in range(KT):
                        mm = product(t, c, d)
                    mm.then_inc(o_ready_half, 1)

            def transposes(m, slot, first=False):
                pe.wait_ge(xn_ready, m + 1)
                for k in range(2):
                    if not first:
                        pe.wait_ge(h_staged, m * 2 + (k - 3))
                    for i in range(4):
                        d = 4 * k + i
                        mm = pe.transpose(t_ps[(slot % 2) * 2 + k][:, i, :], xn[:, slot % 2, d * P:(d + 1) * P], eye[:, :])
                    mm.then_inc(transposed, 1)

            def step(j, t, first=False):
                products(j * 4 + t, t, first)
                if not (first and t == 0):
                    transposes(j * 4 + (t - 1), (t + 3) % 4, first=first and t < 3)

            pe.wait_ge(const_loaded, DMA)
            for t in range(4):
                step(0, t, first=True)
            with pe.Fori(1, NT // 4) as j:
                for t in range(4):
                    step(j, t)
            transposes(NT - 1, 3)


def ffn(nc, ahead, x1_scr, h2_scr, w_gate, w_up, w_down, gf, out):
    TB = 2 * HALF
    NB = TOKENS // TB
    NP = FT // 2
    ST = HALF // P
    with ExitStack() as ctx:
        def sb(name, shape, dt=F32):
            return ctx.enter_context(nc.sbuf_tensor(name, shape, dt))

        def sem(name):
            return ctx.enter_context(nc.semaphore(name))

        ahead.reserve_top(ctx, "ffn", ahead.top_bytes)
        h_hi = sb("h2_hi", [P, 2, KT, HALF], F32R)
        h_lo, h_raw = (list(pair) for pair in zip((ahead.h2_lo, ahead.h2_raw), low_over_raw(nc, ctx, "h2", [P, KT, HALF])))
        acc = ahead.acc
        raw = ahead.w_raw
        w_hi = sb("w_hi4", [P, 6, D], F32R)
        w_lo = sb("w_lo4", [P, 6, D], F32R)
        silu = sb("silu", [P, 2, HALF])
        prod = sb("prod", [P, 2, HALF])
        a_hi = sb("a_hi", [P, 4, HALF], F32R)
        a_lo = sb("a_lo", [P, 4, HALF], F32R)
        junk = sb("junk4", [P, D])
        gain2 = ahead.gain2
        gain_f = sb("gain_f", [P, D])
        sumsq = sb("sumsq4", [P, 2 * ST])
        var = sb("var4", [P, 2 * ST])
        std = sb("std4", [P, 2 * ST])
        tmp = sb("tmp4", [P, 2 * ST])
        rstd = sb("rstd4", [P, 2 * ST])
        gate_ps = [ctx.enter_context(nc.psum_tensor(f"gate_ps{i}", [P, HALF], F32)) for i in range(2)]
        up_ps = [ctx.enter_context(nc.psum_tensor(f"up_ps{i}", [P, HALF], F32)) for i in range(2)]
        down_ps = [ctx.enter_context(nc.psum_tensor(f"down_ps{i}", [P, HALF], F32)) for i in range(4)]

        gain_f_loaded = sem("gain_f_loaded")
        raw_loaded = ahead.w_loaded
        w_hi_done = sem("w_hi_done4")
        w_ready = sem("w_ready4")
        h_loaded = [ahead.h2_loaded, sem("h2_loaded1")]
        h_hi_done = sem("h_hi_done4")
        h_ready = sem("h_ready4")
        x1_loaded = [sem(f"x1_loaded{i}") for i in range(2)]
        gate_ready = sem("gate_ready")
        up_ready = sem("up_ready")
        silu_done = sem("silu_done")
        prod_done = sem("prod_done")
        a_hi_done = sem("a_hi_done")
        a_ready = sem("a_ready")
        down_ready = sem("down_ready")
        down_added = sem("down_added")
        squares_done = sem("squares_done4")
        var_ready = sem("var_ready4")
        std_ready = sem("std_ready4")
        rstd_chain = sem("rstd_chain4")
        out_ready = sem("out_ready")
        out_stored = [sem(f"out_stored{i}") for i in range(2)]
        last_stored = sem("last_stored")

        block = ctx.enter_context(nc.Block())

        def run(eng, body, tail):
            body(0, 0, 0, "first")
            with eng.Fori(0, NB - 1) as b:
                with eng.Fori(1, NP - 1) as i:
                    body(b * NP + i, b, i, "inner")
                body(b * NP + (NP - 1), b, NP - 1, "last")
                body(b * NP + NP, b + 1, 0, "first")
            with eng.Fori(1, NP - 1) as i:
                body(i + (NB - 1) * NP, NB - 1, i, "inner")
            body(NB * NP - 1, NB - 1, NP - 1, "last")
            tail()

        def fixed(q, value):
            return isinstance(q, int) and q == value

        @block.sync
        def _(sp):
            def load_weights(q, i, ks):
                for k in ks:
                    sp.wait_ge(w_ready, q * 6 + (k - 2))
                    if k >= 6:
                        f = 0 if fixed(i, NP - 1) else i * 2 + 2
                    else:
                        f = i * 2 + (0, 0, 1, 1, 0, 1)[k]
                    if k % 6 < 4:
                        src = (w_gate, w_up)[k % 2][bass.ds(f, 1), :, :].rearrange("a p n -> p (a n)")
                    else:
                        src = w_down[bass.ds(f * P, P), :]
                    sp.dma_start(raw[k % 3][:, :], src).then_inc(raw_loaded[k % 3], DMA)

            def load_h(b, half):
                if not fixed(b, 0):
                    sp.wait_ge(up_ready, b * (4 * NP) + (2 * half - 2))
                sp.dma_start(h_raw[half][:, :, :],
                             h2_scr[:, :, bass.ds(b * TB + half * HALF, HALF)].rearrange("d p s -> p d s")).then_inc(h_loaded[half], DMA)

            def load_x1(b, half):
                if not fixed(b, 0):
                    sp.wait_ge(out_stored[half], b * (ST * DMA))
                sp.dma_start(acc[:, half * ST:(half + 1) * ST, :],
                             x1_scr[bass.ds(b * TB + half * HALF, HALF), :].rearrange("(t p) n -> p t n", p=P)).then_inc(x1_loaded[half], DMA)

            def body(q, b, i, place):
                final = place == "last" and isinstance(b, int)
                if place == "inner":
                    load_weights(q, i, (2, 3, 4, 5, 6, 7))
                elif place == "first":
                    load_weights(q, i, (3, 4) if fixed(q, 0) else (2, 3, 4))
                    load_h(b, 1)
                    load_x1(b, 0)
                    load_weights(q, i, (5, 6, 7))
                    load_x1(b, 1)
                else:
                    load_weights(q, i, (2, 3, 4, 5))
                    if not final:
                        load_h(b + 1, 0)
                        load_weights(q, i, (6, 7))

            sp.dma_start(gain_f[:, :], gf.partition_broadcast(P)).then_inc(gain_f_loaded, DMA)
            for t in range(4):
                sp.wait_ge(ahead.x1_stored[t], TOKENS // P // 4 * DMA)
                sp.wait_ge(ahead.h_stored[t], TOKENS // P // 4 * DMA)
            def tail():
                for t in range(ST):
                    sp.wait_ge(out_ready, (2 * NB - 1) * ST + t + 1)
                    sp.dma_start(out[TOKENS - (ST - t) * P:TOKENS - (ST - 1 - t) * P, :], acc[:, ST + t, :]).then_inc(last_stored, DMA)
                sp.wait_ge(out_stored[0], NB * ST * DMA)
                sp.wait_ge(out_stored[1], (NB - 1) * ST * DMA)
                sp.wait_ge(last_stored, ST * DMA)

            run(sp, body, tail)

        @block.scalar
        def _(act):
            def round_w(q, ks):
                for k in ks:
                    if k in (2, 3) and not fixed(q, 0):
                        act.wait_ge(up_ready, q * 4)
                    if k in (4, 5) and not fixed(q, 0):
                        act.wait_ge(down_ready, q * 16)
                    if k in (6, 7):
                        act.wait_ge(up_ready, q * 4 + 3)
                    act.wait_ge(raw_loaded[k % 3], (q * 2 + (k // 3 + 1)) * DMA)
                    act.activation(w_hi[:, k % 6, :], raw[k % 3][:, :], ACT.Copy).then_inc(w_hi_done, 1)

            def round_h(b, half):
                if not fixed(b, 0):
                    act.wait_ge(up_ready, b * (4 * NP) + (2 * half - 2))
                act.wait_ge(h_loaded[half], (b + 1) * DMA)
                for d in range(KT):
                    act.activation(h_hi[:, half, d, :], h_raw[half][:, d, :], ACT.Identity,
                                   scale=gain2[:, d:d + 1]).then_inc(h_hi_done, 1)

            def gate(q, m):
                act.wait_ge(gate_ready, q * 4 + (m + 1))
                if not (fixed(q, 0) and m < 2):
                    act.wait_ge(prod_done, q * 4 + (m - 1))
                act.activation(silu[:, m % 2, :], gate_ps[m % 2][:, :], ACT.Silu).then_inc(silu_done, 1)

            def round_a(q, m):
                act.wait_ge(prod_done, q * 4 + (m + 1))
                act.activation(a_hi[:, m, :], prod[:, m % 2, :], ACT.Copy).then_inc(a_hi_done, 1)

            def last_norm(b, half):
                nth = b * 2 + half
                act.wait_ge(down_added, down_done(b, half))
                for t in range(ST):
                    one = half * ST + t
                    if t:
                        act.wait_ge(squares_done, nth * ST + t)
                    act.activation(junk[:, :], acc[:, one, :], ACT.Square,
                                   accum_out=sumsq[:, one:one + 1]).then_inc(squares_done, 1)
                act.wait_ge(var_ready, nth + 1)
                act.activation(std[:, half * ST:(half + 1) * ST], var[:, half * ST:(half + 1) * ST], ACT.Sqrt).then_inc(std_ready, 1)

            def down_done(b, half):
                return b * (16 * NP) + (16 * NP - 8 + 8 * half)

            def body(q, b, i, place):
                first, last = place == "first", place == "last"
                final = last and isinstance(b, int)
                if fixed(q, 0):
                    round_w(q, (0,))
                    act.wait_ge(ahead.gain2_loaded, DMA)
                    round_h(b, 0)
                    round_w(q, (1,))
                round_w(q, (2, 3))
                gate(q, 0)
                round_a(q, 0)
                if first:
                    round_h(b, 1)
                round_w(q, (4, 5))
                if first and not fixed(q, 0):
                    last_norm(b - 1, 1)
                gate(q, 1)
                round_a(q, 1)
                gate(q, 2)
                round_a(q, 2)
                if not final:
                    round_w(q, (6, 7))
                    if last:
                        round_h(b + 1, 0)
                if last:
                    last_norm(b, 0)
                gate(q, 3)
                round_a(q, 3)

            def tail():
                nth = 2 * NB - 1
                for t in range(ST):
                    one = ST + t
                    act.wait_ge(down_added, down_done(NB - 1, 1) - 2 * (ST - 1 - t))
                    act.activation(junk[:, :], acc[:, one, :], ACT.Square,
                                   accum_out=sumsq[:, one:one + 1]).then_inc(squares_done, 1)
                    act.wait_ge(var_ready, nth + t + 1)
                    act.activation(std[:, one:one + 1], var[:, one:one + 1], ACT.Sqrt).then_inc(std_ready, 1)

            run(act, body, tail)

        @block.vector
        def _(dve):
            def rest_of_w(q, ks):
                for k in ks:
                    dve.wait_ge(w_hi_done, q * 6 + (k + 1))
                    dve.tensor_tensor(w_lo[:, k % 6, :], raw[k % 3][:, :], w_hi[:, k % 6, :].bitcast(F32),
                                      ALU.subtract).then_inc(w_ready, 1)

            def rest_of_h(b, half):
                for d in range(KT):
                    dve.wait_ge(h_hi_done, b * (2 * KT) + (half * KT + d + 1))
                    dve.scalar_tensor_tensor(out=h_lo[half][:, d, :], in0=h_raw[half][:, d, :], scalar=gain2[:, d:d + 1],
                                             in1=h_hi[:, half, d, :].bitcast(F32), op0=ALU.mult,
                                             op1=ALU.subtract).then_inc(h_ready, 1)

            def product(q, m):
                dve.wait_ge(silu_done, q * 4 + (m + 1))
                dve.wait_ge(up_ready, q * 4 + (m + 1))
                dve.tensor_tensor(prod[:, m % 2, :], up_ps[m % 2][:, :], silu[:, m % 2, :], ALU.mult).then_inc(prod_done, 1)
                dve.wait_ge(a_hi_done, q * 4 + (m + 1))
                dve.tensor_tensor(a_lo[:, m, :], prod[:, m % 2, :], a_hi[:, m, :].bitcast(F32),
                                  ALU.subtract).then_inc(a_ready, 1)

            def add(q, half, loaded=None, tiles=range(ST)):
                if loaded is not None:
                    dve.wait_ge(x1_loaded[half], loaded)
                for t in tiles:
                    for c in range(2):
                        g = 2 * t + c
                        dve.wait_ge(down_ready, q * 16 + (half * 8 + g + 1))
                        dst = acc[:, half * ST + t, c * HALF:(c + 1) * HALF]
                        dve.tensor_tensor(dst, down_ps[g % 4][:, :], dst, ALU.add).then_inc(down_added, 1)

            def last_norm_var(b, half):
                these = slice(half * ST, (half + 1) * ST)
                nth = b * 2 + half
                dve.wait_ge(squares_done, nth * ST + ST)
                dve.tensor_scalar(var[:, these], sumsq[:, these], 1.0 / D, EPS, ALU.mult, ALU.add).then_inc(var_ready, 1)
                dve.wait_ge(std_ready, nth + 1)
                refined_rstd(dve, rstd_chain, nth * 4, std[:, these], var[:, these], tmp[:, these], rstd[:, these])
                scale(half, range(2))

            def scale(half, tiles):
                for t in tiles:
                    one = half * ST + t
                    dve.scalar_tensor_tensor(out=acc[:, one, :], in0=acc[:, one, :], scalar=rstd[:, one:one + 1],
                                             in1=gain_f[:, :], op0=ALU.mult, op1=ALU.mult).then_inc(out_ready, 1)

            def body(q, b, i, place):
                first, last = place == "first", place == "last"
                final = last and isinstance(b, int)
                loaded = (b + 1) * DMA if first else None
                if fixed(q, 0):
                    rest_of_w(q, (0,))
                    dve.wait_ge(ahead.gain2_loaded, DMA)
                    rest_of_h(b, 0)
                    rest_of_w(q, (1,))
                    dve.wait_ge(gain_f_loaded, DMA)
                rest_of_w(q, (2, 3))
                product(q, 0)
                if not fixed(q, 0):
                    add(q - 1, 1)
                if first:
                    rest_of_h(b, 1)
                rest_of_w(q, (4, 5))
                if first and not fixed(q, 0):
                    last_norm_var(b - 1, 1)
                product(q, 1)
                if first and not fixed(q, 0):
                    scale(1, range(2, ST))
                product(q, 2)
                if not final:
                    rest_of_w(q, (6, 7))
                add(q, 0, loaded)
                if last and not final:
                    rest_of_h(b + 1, 0)
                if last:
                    last_norm_var(b, 0)
                product(q, 3)
                if last:
                    scale(0, range(2, ST))
                if first:
                    dve.wait_ge(x1_loaded[1], loaded)

            def tail():
                for t in range(ST):
                    add(NB * NP - 1, 1, tiles=(t,))
                    if t:
                        last_tile_norm(t - 1)
                last_tile_norm(ST - 1)

            def last_tile_norm(t):
                one = slice(ST + t, ST + t + 1)
                nth = 2 * NB - 1
                dve.wait_ge(squares_done, nth * ST + t + 1)
                dve.tensor_scalar(var[:, one], sumsq[:, one], 1.0 / D, EPS, ALU.mult, ALU.add).then_inc(var_ready, 1)
                dve.wait_ge(std_ready, nth + t + 1)
                refined_rstd(dve, rstd_chain, (nth + t) * 4, std[:, one], var[:, one], tmp[:, one], rstd[:, one])
                dve.scalar_tensor_tensor(out=acc[:, ST + t, :], in0=acc[:, ST + t, :], scalar=rstd[:, one],
                                         in1=gain_f[:, :], op0=ALU.mult, op1=ALU.mult).then_inc(out_ready, 1)

            run(dve, body, tail)

        @block.tensor
        def _(pe):
            def up(q, m, b, first):
                tile, half = m % 2, m // 2
                if not (fixed(q, 0) and m < 2):
                    pe.wait_ge(prod_done, q * 4 + (m - 1))
                for part, ps in ((0, gate_ps), (1, up_ps)):
                    k = 2 * tile + part
                    if half == 0:
                        pe.wait_ge(w_ready, q * 6 + (k + 1))
                    for d in range(KT):
                        if first and tile == 0 and part == 0:
                            pe.wait_ge(h_ready, b * (2 * KT) + (half * KT + d + 1))
                        mm = three_products(pe, ps[m % 2][:, :], w_hi[:, k, d * P:(d + 1) * P], w_lo[:, k, d * P:(d + 1) * P],
                                            h_hi[:, half, d, :], h_lo[half][:, d, :], d == 0, d == KT - 1)
                    mm.then_inc((gate_ready, up_ready)[part], 1)

            def down(q, half):
                pe.wait_ge(a_ready, q * 4 + (2 * half + 2))
                if half == 0:
                    pe.wait_ge(w_ready, q * 6 + 6)
                for t in range(ST):
                    for c in range(2):
                        g = 2 * t + c
                        if not (fixed(q, 0) and half == 0 and g < 4):
                            pe.wait_ge(down_added, q * 16 + (half * 8 + g - 3))
                        for f in range(2):
                            m = 2 * half + f
                            mm = three_products(pe, down_ps[g % 4][:, :], a_hi[:, m, t * P:(t + 1) * P], a_lo[:, m, t * P:(t + 1) * P],
                                                w_hi[:, 4 + f, c * HALF:(c + 1) * HALF], w_lo[:, 4 + f, c * HALF:(c + 1) * HALF],
                                                f == 0, f == 1)
                        mm.then_inc(down_ready, 1)

            def body(q, b, i, place):
                first = place == "first"
                up(q, 0, b, first)
                if not fixed(q, 0):
                    down(q - 1, 1)
                up(q, 1, b, first)
                up(q, 2, b, first)
                down(q, 0)
                up(q, 3, b, first)

            run(pe, body, lambda: down(NB * NP - 1, 1))

        @block.gpsimd
        def _(pool):
            def store(b, half):
                for t in range(ST):
                    pool.wait_ge(out_ready, b * (2 * ST) + (half * ST + t + 1))
                    pool.dma_start(out[bass.ds(b * TB + (half * ST + t) * P, P), :],
                                   acc[:, half * ST + t, :]).then_inc(out_stored[half], DMA)

            with pool.Fori(0, NB - 1) as b:
                for half in range(2):
                    store(b, half)
            store(NB - 1, 0)


def encoder(nc, x, w_in, w_fourier, w_pool, w_out, w_gate, w_up, w_down, g1, g2, gf, pool_gain,
            table, channel, edge, ident, out):
    def scratch(name, shape):
        return nc.dram_tensor(name, shape, F32, kind="Internal").ap()

    z_scr = scratch("z_scr", (KT, P, TOKENS))
    y_scr = scratch("y_scr", (KT, P, TOKENS))
    x1_scr = scratch("x1_scr", (TOKENS, D))
    h2_scr = scratch("h2_scr", (KT, P, TOKENS))
    with ExitStack() as ctx:
        ahead = Ahead(nc, ctx)
        project_in(nc, ahead, x, w_in, g1, ident, z_scr, table, channel, w_fourier)
        mix(nc, ahead, w_out, z_scr, y_scr, w_pool, pool_gain, edge)
        project_out(nc, ahead, y_scr, x, ident, w_gate, w_up, g2, x1_scr, h2_scr)
        ffn(nc, ahead, x1_scr, h2_scr, w_gate, w_up, w_down, gf, out)


def kernel(x_prompt, x_sample, norm1_g, w_in, w_fourier, w_pool, pool_scale, w_out, norm2_g, w_gate, w_up, w_down, normf_g):
    import concourse.bacc as bacc
    from concourse.bass_utils import run_bass_kernel_spmd

    def a(v):
        return np.ascontiguousarray(np.asarray(v))

    def by_partition(g):
        return a(a(g).reshape(-1, P).T)

    def hidden_tiles(w):
        return a(a(w).reshape(KT, P, FT, P).transpose(2, 1, 0, 3).reshape(FT, P, KT * P))

    table, channel = fourier_tables()
    arrays = {
        "x": a(np.concatenate([a(x_prompt)[0], a(x_sample)[0]], axis=0)),
        "w_in": a(w_in)[0],
        "w_fourier": a(w_fourier)[0],
        "w_pool": a(w_pool)[0],
        "w_out": a(w_out)[0],
        "w_gate": hidden_tiles(a(w_gate)[0]),
        "w_up": hidden_tiles(a(w_up)[0]),
        "w_down": a(w_down)[0],
        "g1": by_partition(a(norm1_g)[0]),
        "g2": by_partition(a(norm2_g)[0]),
        "gf": a(normf_g),
        "pool_gain": by_partition(a(pool_scale)[0]),
        "table": table,
        "channel": channel,
        "edge": edge_counts(),
        "ident": np.eye(P, dtype=np.float32),
    }
    arrays = {f"in_{k}": a(v) for k, v in arrays.items()}
    nc = bacc.Bacc("TRN2", target_bir_lowering=False, num_devices=1)
    args = [nc.dram_tensor(k, v.shape, mybir.dt.from_np(v.dtype), kind="ExternalInput").ap() for k, v in arrays.items()]
    out = nc.dram_tensor("out", (TOKENS, D), F32, kind="ExternalOutput").ap()
    encoder(nc, *args, out)
    r = run_bass_kernel_spmd(nc, [arrays], core_ids=[0])
    y = r.results[0]["out"]
    return y[:SEQS[0]][None], y[SEQS[0]:][None]
```
